# Optimizing a Trainium2 kernel written in Bass

```python
import jax, jax.numpy as jnp
from jax import lax
import numpy as np

D_MODEL = 1024
BATCH = 1
SEQ = 512
DEPTH = 1

ATTN_HEADS = 8
ATTN_KV_HEADS = 2
ATTN_GROUP = ATTN_HEADS // ATTN_KV_HEADS
ATTN_HEAD_DIM = 64
ATTN_WIDTH = ATTN_HEADS * ATTN_HEAD_DIM
KV_WIDTH = ATTN_KV_HEADS * ATTN_HEAD_DIM
WINDOW = 128
ATTN_BLOCK = 128

HGRN_HEADS = 4
HGRN_DK = 128
HGRN_DV = 128
HGRN_WIDTH = HGRN_HEADS * HGRN_DK
HGRN_V_WIDTH = HGRN_HEADS * HGRN_DV
HGRN_CHUNK = 32

N_BRANCHES = 2
IN_WIDTH = ATTN_WIDTH + 2 * KV_WIDTH + 2 * HGRN_WIDTH + 2 * HGRN_V_WIDTH + N_BRANCHES * D_MODEL

PEER_HEADS = 8
PEER_N_KEYS = 128
PEER_N_EXPERTS = PEER_N_KEYS * PEER_N_KEYS
PEER_KEY_DIM = 128
PEER_TOPK = 16
PEER_TOKEN_BLOCK = 128

EPS = 1e-6
MASK_VALUE = -1e30


def rms_norm(x, g):
    xf = x.astype(jnp.float32)
    y = xf * lax.rsqrt(jnp.mean(xf * xf, axis=-1, keepdims=True) + EPS)
    return (y * g.astype(jnp.float32)).astype(x.dtype)

def alibi_slopes():
    return jnp.asarray(2.0 ** (-8.0 * np.arange(1, ATTN_HEADS + 1) / ATTN_HEADS), dtype=jnp.float32)

def split_combined(proj):
    sizes = (ATTN_WIDTH, KV_WIDTH, KV_WIDTH, HGRN_WIDTH, HGRN_WIDTH,
             HGRN_V_WIDTH, HGRN_V_WIDTH, D_MODEL, D_MODEL)
    offsets = np.cumsum(sizes)[:-1].tolist()
    return jnp.split(proj, offsets, axis=-1)

def sliding_window_attention(q, k, v, sinks):
    B, S = q.shape[0], q.shape[1]
    W = ATTN_BLOCK
    nb = S // W
    qb = q.reshape(B, nb, W, ATTN_KV_HEADS, ATTN_GROUP, ATTN_HEAD_DIM)

    def with_prev(t):
        tb = t.reshape(B, nb, W, ATTN_KV_HEADS, ATTN_HEAD_DIM)
        prev = jnp.concatenate([jnp.zeros_like(tb[:, :1]), tb[:, :-1]], axis=1)
        return jnp.concatenate([prev, tb], axis=2)

    kc, vc = with_prev(k), with_prev(v)
    scale = ATTN_HEAD_DIM ** -0.5
    s = jnp.einsum('bnqkgd,bnskd->bnkgqs', qb, kc,
                   preferred_element_type=jnp.float32) * scale
    qpos = jnp.arange(W)[:, None] + W
    kpos = jnp.arange(2 * W)[None, :]
    dist = qpos - kpos
    blk = jnp.arange(nb)[:, None, None]
    valid = (dist >= 0) & (dist < WINDOW) & (blk * W + kpos - W >= 0)
    slopes = alibi_slopes().reshape(ATTN_KV_HEADS, ATTN_GROUP)
    s = s - slopes[:, :, None, None] * dist.astype(jnp.float32)
    s = jnp.where(valid[None, :, None, None], s, MASK_VALUE)
    sink = jnp.broadcast_to(sinks.astype(jnp.float32).reshape(ATTN_KV_HEADS, ATTN_GROUP)[:, :, None, None],
                            s.shape[:-1] + (1,))
    p = jax.nn.softmax(jnp.concatenate([s, sink], axis=-1), axis=-1)[..., :-1]
    o = jnp.einsum('bnkgqs,bnskd->bnqkgd', p.astype(v.dtype), vc)
    return o.reshape(B, S, ATTN_WIDTH)

def hgrn2_recurrence(q, f_logit, i, lower_bound):
    B, S = q.shape[0], q.shape[1]
    C = HGRN_CHUNK
    nc = S // C
    f32 = jnp.float32
    f = lower_bound + (1.0 - lower_bound) * jax.nn.sigmoid(f_logit.astype(f32))
    k = 1.0 - f
    logf = jnp.log(f)

    def chunk(t):
        return t.reshape(B, nc, C, HGRN_HEADS, t.shape[-1])

    qc, kc, lc, vc = chunk(q.astype(f32)), chunk(k), chunk(logf), chunk(i.astype(f32))
    b = jnp.cumsum(lc, axis=2)
    q_dec = qc * jnp.exp(b)
    k_inv = kc * jnp.exp(-b)
    causal = jnp.tril(jnp.ones((C, C), dtype=bool))
    a = jnp.where(causal, jnp.einsum('bnthd,bnshd->bnhts', q_dec, k_inv), 0.0)
    o_intra = jnp.einsum('bnhts,bnshv->bnthv', a, vc)
    b_last = b[:, :, -1:]
    ds = jnp.einsum('bnshd,bnshv->bnhdv', kc * jnp.exp(b_last - b), vc)
    decay = jnp.exp(b_last[:, :, 0])

    def step(state, inp):
        dec, d = inp
        return dec[..., None] * state + d, state

    s0 = jnp.zeros((B, HGRN_HEADS, HGRN_DK, HGRN_DV), f32)
    _, s_prev = lax.scan(step, s0, (jnp.moveaxis(decay, 1, 0), jnp.moveaxis(ds, 1, 0)))
    s_prev = jnp.moveaxis(s_prev, 0, 1)
    o_inter = jnp.einsum('bnthd,bnhdv->bnthv', q_dec, s_prev)
    return (o_intra + o_inter).reshape(B, S, HGRN_HEADS, HGRN_DV)

def peer_layer(h, w_q, keys, u, v):
    B, S = h.shape[0], h.shape[1]
    q = (h @ w_q).reshape(B, S, PEER_HEADS, 2, PEER_KEY_DIM)
    sc = jnp.einsum('bshpd,phnd->bshpn', q, keys).astype(jnp.float32)
    v1, i1 = lax.top_k(sc[..., 0, :], PEER_TOPK)
    v2, i2 = lax.top_k(sc[..., 1, :], PEER_TOPK)
    cand = (v1[..., :, None] + v2[..., None, :]).reshape(B, S, PEER_HEADS, PEER_TOPK * PEER_TOPK)
    cidx = (i1[..., :, None] * PEER_N_KEYS + i2[..., None, :]).reshape(B, S, PEER_HEADS, PEER_TOPK * PEER_TOPK)
    best, pos = lax.top_k(cand, PEER_TOPK)
    idx = jnp.take_along_axis(cidx, pos, axis=-1)
    gates = jax.nn.softmax(best, axis=-1)
    T = B * S
    nblk = T // PEER_TOKEN_BLOCK
    hk = PEER_HEADS * PEER_TOPK
    hb = h.reshape(nblk, PEER_TOKEN_BLOCK, D_MODEL)
    ib = idx.reshape(nblk, PEER_TOKEN_BLOCK, hk)
    gb = gates.reshape(nblk, PEER_TOKEN_BLOCK, hk).astype(h.dtype)

    def expert_block(args):
        ht, it, gt = args
        ue = jnp.take(u, it, axis=0)
        act = jax.nn.gelu(jnp.einsum('tkd,td->tk', ue, ht), approximate=False)
        ve = jnp.take(v, it, axis=0)
        return jnp.einsum('tk,tkd->td', gt * act, ve)

    out = lax.map(expert_block, (hb, ib, gb))
    return out.reshape(B, S, D_MODEL)

def hybrid_layer(x, norm_mix_g, w_in, sinks, lower_bound, hgrn_norm_g, w_attn_proj,
                 w_hgrn_proj, w_out, norm_ffn_g, w_peer_q, peer_keys, peer_u, peer_v):
    B, S = x.shape[0], x.shape[1]
    h = rms_norm(x, norm_mix_g)
    aq, ak, av, hq, hf, hi, hg, ga, gh = split_combined(h @ w_in)
    y_attn = sliding_window_attention(aq.reshape(B, S, ATTN_HEADS, ATTN_HEAD_DIM),
                                      ak.reshape(B, S, ATTN_KV_HEADS, ATTN_HEAD_DIM),
                                      av.reshape(B, S, ATTN_KV_HEADS, ATTN_HEAD_DIM), sinks)
    o = hgrn2_recurrence(jax.nn.silu(hq).reshape(B, S, HGRN_HEADS, HGRN_DK),
                         hf.reshape(B, S, HGRN_HEADS, HGRN_DK),
                         hi.reshape(B, S, HGRN_HEADS, HGRN_DV), lower_bound)
    o = rms_norm(o, hgrn_norm_g).astype(x.dtype) * jax.nn.silu(hg.reshape(B, S, HGRN_HEADS, HGRN_DV))
    y_hgrn = o.reshape(B, S, HGRN_V_WIDTH)
    merged = jax.nn.sigmoid(ga) * (y_attn @ w_attn_proj) + jax.nn.sigmoid(gh) * (y_hgrn @ w_hgrn_proj)
    x = x + merged @ w_out
    x = x + peer_layer(rms_norm(x, norm_ffn_g), w_peer_q, peer_keys, peer_u, peer_v)
    return x

def first_inputs(seed: int = 0) -> dict:
    key = jax.random.key(seed)
    ks = jax.random.split(key, 16)
    f32 = jnp.float32
    n = jax.random.normal
    return {
        "x": n(ks[0], (BATCH, SEQ, D_MODEL), f32),
        "norm_mix_g": 1.0 + 0.02 * n(ks[1], (DEPTH, D_MODEL), f32),
        "w_in": n(ks[2], (DEPTH, D_MODEL, IN_WIDTH), f32) * D_MODEL ** -0.5,
        "attn_sinks": n(ks[3], (DEPTH, ATTN_HEADS), f32),
        "hgrn_lb_logits": 0.1 * n(ks[4], (DEPTH + 1, HGRN_WIDTH), f32),
        "hgrn_norm_g": 1.0 + 0.02 * n(ks[5], (DEPTH, HGRN_DV), f32),
        "w_attn_proj": n(ks[6], (DEPTH, ATTN_WIDTH, D_MODEL), f32) * ATTN_WIDTH ** -0.5,
        "w_hgrn_proj": n(ks[7], (DEPTH, HGRN_V_WIDTH, D_MODEL), f32) * HGRN_V_WIDTH ** -0.5,
        "w_out": n(ks[8], (DEPTH, D_MODEL, D_MODEL), f32) * D_MODEL ** -0.5,
        "norm_ffn_g": 1.0 + 0.02 * n(ks[9], (DEPTH, D_MODEL), f32),
        "w_peer_q": n(ks[10], (DEPTH, D_MODEL, PEER_HEADS * 2 * PEER_KEY_DIM), f32) * D_MODEL ** -0.5,
        "peer_keys": n(ks[11], (DEPTH, 2, PEER_HEADS, PEER_N_KEYS, PEER_KEY_DIM), f32) * PEER_KEY_DIM ** -0.5,
        "peer_u": n(ks[12], (DEPTH, PEER_N_EXPERTS, D_MODEL), f32) * D_MODEL ** -0.5,
        "peer_v": n(ks[13], (DEPTH, PEER_N_EXPERTS, D_MODEL), f32) * PEER_HEADS ** -0.5,
        "norm_final_g": 1.0 + 0.02 * n(ks[14], (D_MODEL,), f32),
    }

def first_block(x, norm_mix_g, w_in, attn_sinks, hgrn_lb_logits, hgrn_norm_g, w_attn_proj,
              w_hgrn_proj, w_out, norm_ffn_g, w_peer_q, peer_keys, peer_u, peer_v, norm_final_g):
    lower_bounds = jnp.cumsum(jax.nn.softmax(hgrn_lb_logits.astype(jnp.float32), axis=0), axis=0)
    for layer in range(DEPTH):
        x = hybrid_layer(x, norm_mix_g[layer], w_in[layer], attn_sinks[layer],
                         lower_bounds[layer].reshape(HGRN_HEADS, HGRN_DK), hgrn_norm_g[layer],
                         w_attn_proj[layer], w_hgrn_proj[layer], w_out[layer], norm_ffn_g[layer],
                         w_peer_q[layer], peer_keys[layer], peer_u[layer], peer_v[layer])
    return rms_norm(x, norm_final_g)


NSA_HEADS = 8
NSA_KV_GROUPS = 2
NSA_HPG = NSA_HEADS // NSA_KV_GROUPS
NSA_HEAD_DIM = 64
NSA_WIDTH = NSA_HEADS * NSA_HEAD_DIM
NSA_KV_WIDTH = NSA_KV_GROUPS * NSA_HEAD_DIM
CMP_BLOCK = 32
CMP_STRIDE = 16
CMP_HIDDEN = 128
SLC_BLOCK = 64
SLC_TOPK = 16
WINDOW_2 = 512
N_BRANCH = 3
FORCED_SCORE = 1.0e4
MLA_HEADS = 8
MLA_NOPE_DIM = 64
MLA_ROPE_DIM = 32
MLA_V_DIM = 64
MLA_WIDTH = MLA_HEADS * MLA_V_DIM
MLA_Q_RANK = 256
MLA_KV_RANK = 128
MIX_WIDTH = NSA_WIDTH + MLA_WIDTH
Q_BLOCK = 128
ROPE_THETA = 10000.0
NORM_EPS = 1e-6
NEG_INF = -1e30

IN_SIZES = (
    NSA_WIDTH,
    NSA_KV_WIDTH, NSA_KV_WIDTH,
    NSA_KV_WIDTH, NSA_KV_WIDTH,
    NSA_KV_WIDTH, NSA_KV_WIDTH,
    NSA_HEADS * N_BRANCH,
    NSA_WIDTH,
    MLA_Q_RANK,
    MLA_KV_RANK,
    MLA_ROPE_DIM,
    MLA_WIDTH,
)
IN_WIDTH_2 = sum(IN_SIZES)
IN_OFFSETS = tuple(int(o) for o in np.cumsum(IN_SIZES)[:-1])


def rms_norm_2(x, g):
    xf = x.astype(jnp.float32)
    y = xf * lax.rsqrt(jnp.mean(xf * xf, axis=-1, keepdims=True) + NORM_EPS)
    return (y * g.astype(jnp.float32)).astype(x.dtype)

def rope(x, pos):
    half = x.shape[-1] // 2
    inv = ROPE_THETA ** (-jnp.arange(half, dtype=jnp.float32) / half)
    ang = pos.astype(jnp.float32)[..., None] * inv
    cos = jnp.cos(ang)[:, :, None, :]
    sin = jnp.sin(ang)[:, :, None, :]
    xf = x.astype(jnp.float32)
    x1, x2 = xf[..., :half], xf[..., half:]
    out = jnp.concatenate([x1 * cos - x2 * sin, x2 * cos + x1 * sin], axis=-1)
    return out.astype(x.dtype)

def masked_softmax(s, mask):
    s = jnp.where(mask, s.astype(jnp.float32), NEG_INF)
    p = jax.nn.softmax(s, axis=-1)
    return jnp.where(mask, p, 0.0)

def compress(kv, cmp_pos, w1, w2):
    B, S, G, D = kv.shape
    r = CMP_BLOCK // CMP_STRIDE
    ns = S // CMP_STRIDE
    sub = kv.reshape(B, ns, CMP_STRIDE, G, D)
    nc = ns - r + 1
    blocks = jnp.concatenate([sub[:, j:j + nc] for j in range(r)], axis=2)
    blocks = blocks + cmp_pos[None, None, :, None, :]
    flat = blocks.transpose(0, 1, 3, 2, 4).reshape(B, nc, G, CMP_BLOCK * D)
    return jax.nn.silu(flat @ w1) @ w2

def cmp_to_slc_matrix(nc, nslc):
    start = np.arange(nc)[:, None] * CMP_STRIDE
    bstart = np.arange(nslc)[None, :] * SLC_BLOCK
    ov = np.minimum(start + CMP_BLOCK, bstart + SLC_BLOCK) - np.maximum(start, bstart)
    return (np.clip(ov, 0, None) / CMP_BLOCK).astype(np.float32)

def nsa_attention(q, k_cmp, v_cmp, k_slc, v_slc, k_win, v_win, gate_logits, positions,
                  cmp_pos, cmp_k_w1, cmp_k_w2, cmp_v_w1, cmp_v_w2):
    B, S = q.shape[:2]
    G, HPG, dk = NSA_KV_GROUPS, NSA_HPG, NSA_HEAD_DIM
    scale = dk ** -0.5
    nqb = S // Q_BLOCK
    t = np.arange(S)
    qg = rope(q.reshape(B, S, NSA_HEADS, dk), positions).reshape(B, S, G, HPG, dk)

    kc = compress(k_cmp.reshape(B, S, G, dk), cmp_pos, cmp_k_w1, cmp_k_w2)
    vc = compress(v_cmp.reshape(B, S, G, dk), cmp_pos, cmp_v_w1, cmp_v_w2)
    nc = kc.shape[1]
    cmp_end = np.arange(nc) * CMP_STRIDE + CMP_BLOCK - 1
    kc = rope(kc, positions[:, cmp_end])
    s_cmp = jnp.einsum('bsghd,bngd->bghsn', qg, kc).astype(jnp.float32) * scale
    p_cmp = masked_softmax(s_cmp, cmp_end[None, :] <= t[:, None])
    o_cmp = jnp.einsum('bghsn,bngd->bsghd', p_cmp.astype(vc.dtype), vc)

    nslc = S // SLC_BLOCK
    m = jnp.asarray(cmp_to_slc_matrix(nc, nslc))
    imp = jnp.einsum('bghsn,nj->bgsj', p_cmp, m)
    blk = np.arange(nslc)[None, :]
    cur = (t // SLC_BLOCK)[:, None]
    forced = (blk == 0) | (blk == cur) | (blk == cur - 1)
    imp = jnp.where(forced, FORCED_SCORE, jnp.where(blk > cur, -FORCED_SCORE, imp))
    n_sel = min(SLC_TOPK, nslc)
    _, sel_idx = lax.top_k(imp, n_sel)

    kb = rope(k_slc.reshape(B, S, G, dk), positions).reshape(B, nslc, SLC_BLOCK, G, dk).transpose(0, 3, 1, 2, 4)
    vb = v_slc.reshape(B, nslc, SLC_BLOCK, G, dk).transpose(0, 3, 1, 2, 4)
    q_chunks = qg.reshape(B, nqb, Q_BLOCK, G, HPG, dk).transpose(1, 0, 3, 2, 4, 5)
    idx_chunks = sel_idx.reshape(B, G, nqb, Q_BLOCK, n_sel).transpose(2, 0, 1, 3, 4)
    t_chunks = jnp.arange(S, dtype=jnp.int32).reshape(nqb, Q_BLOCK)
    gather = jax.vmap(jax.vmap(lambda blocks, ix: blocks[ix]))
    sb_offsets = jnp.arange(SLC_BLOCK, dtype=jnp.int32)

    def slc_block(args):
        qc, ic, tc = args
        kg = gather(kb, ic)
        vg = gather(vb, ic)
        s = jnp.einsum('bgqhd,bgqnkd->bgqhnk', qc, kg).astype(jnp.float32) * scale
        key_pos = ic[..., None] * SLC_BLOCK + sb_offsets
        mask = (key_pos <= tc[None, None, :, None, None]).reshape(B, G, Q_BLOCK, 1, n_sel * SLC_BLOCK)
        p = masked_softmax(s.reshape(B, G, Q_BLOCK, HPG, n_sel * SLC_BLOCK), mask)
        p = p.reshape(B, G, Q_BLOCK, HPG, n_sel, SLC_BLOCK)
        return jnp.einsum('bgqhnk,bgqnkd->bqghd', p.astype(vg.dtype), vg)

    o_slc = lax.map(slc_block, (q_chunks, idx_chunks, t_chunks))
    o_slc = o_slc.transpose(1, 0, 2, 3, 4, 5).reshape(B, S, G, HPG, dk)

    n_back = WINDOW_2 // Q_BLOCK

    def band(a):
        ap = jnp.pad(a, ((0, 0), (WINDOW_2, 0), (0, 0), (0, 0)))
        ab = ap.reshape(B, nqb + n_back, Q_BLOCK, G, dk)
        return jnp.concatenate([ab[:, j:j + nqb] for j in range(n_back + 1)], axis=2)

    kband = band(rope(k_win.reshape(B, S, G, dk), positions))
    vband = band(v_win.reshape(B, S, G, dk))
    qw = qg.reshape(B, nqb, Q_BLOCK, G, HPG, dk)
    s_win = jnp.einsum('bnqghd,bnkgd->bnghqk', qw, kband).astype(jnp.float32) * scale
    q_idx = np.arange(nqb)[:, None] * Q_BLOCK + np.arange(Q_BLOCK)[None, :]
    k_idx = np.arange(nqb)[:, None] * Q_BLOCK - WINDOW_2 + np.arange((n_back + 1) * Q_BLOCK)[None, :]
    diff = q_idx[:, :, None] - k_idx[:, None, :]
    win_mask = (diff >= 0) & (diff < WINDOW_2) & (k_idx[:, None, :] >= 0)
    p_win = masked_softmax(s_win, win_mask[None, :, None, None])
    o_win = jnp.einsum('bnghqk,bnkgd->bnqghd', p_win.astype(vband.dtype), vband).reshape(B, S, G, HPG, dk)

    g = jax.nn.sigmoid(gate_logits.astype(jnp.float32)).reshape(B, S, G, HPG, N_BRANCH).astype(q.dtype)
    o = g[..., 0:1] * o_cmp + g[..., 1:2] * o_slc + g[..., 2:3] * o_win
    return o.reshape(B, S, NSA_WIDTH)

def mla_attention(c_q, c_kv, k_rope, positions, q_norm_g, w_q_up, kv_norm_g, w_kv_up):
    B, S = c_q.shape[:2]
    H = MLA_HEADS
    nqb = S // Q_BLOCK
    q = (rms_norm_2(c_q, q_norm_g) @ w_q_up).reshape(B, S, H, MLA_NOPE_DIM + MLA_ROPE_DIM)
    q_nope = q[..., :MLA_NOPE_DIM]
    q_rot = rope(q[..., MLA_NOPE_DIM:], positions)
    kv = (rms_norm_2(c_kv, kv_norm_g) @ w_kv_up).reshape(B, S, H, MLA_NOPE_DIM + MLA_V_DIM)
    k_nope, v = kv[..., :MLA_NOPE_DIM], kv[..., MLA_NOPE_DIM:]
    k_rot = rope(k_rope[:, :, None, :], positions)[:, :, 0]
    scale = (MLA_NOPE_DIM + MLA_ROPE_DIM) ** -0.5
    qn_c = q_nope.reshape(B, nqb, Q_BLOCK, H, MLA_NOPE_DIM).transpose(1, 0, 2, 3, 4)
    qr_c = q_rot.reshape(B, nqb, Q_BLOCK, H, MLA_ROPE_DIM).transpose(1, 0, 2, 3, 4)
    t_chunks = jnp.arange(S, dtype=jnp.int32).reshape(nqb, Q_BLOCK)
    key_idx = jnp.arange(S, dtype=jnp.int32)

    def mla_block(args):
        qn, qr, tc = args
        s = (jnp.einsum('bqhd,bkhd->bhqk', qn, k_nope)
             + jnp.einsum('bqhd,bkd->bhqk', qr, k_rot)).astype(jnp.float32) * scale
        p = masked_softmax(s, key_idx[None, :] <= tc[:, None])
        return jnp.einsum('bhqk,bkhd->bqhd', p.astype(v.dtype), v)

    o = lax.map(mla_block, (qn_c, qr_c, t_chunks))
    return o.transpose(1, 0, 2, 3, 4).reshape(B, S, MLA_WIDTH)

def second_inputs(seed: int = 0) -> dict:
    key = jax.random.key(seed)
    ks = jax.random.split(key, 20)
    f32 = jnp.float32
    L, D = DEPTH, D_MODEL

    def nrm(k, shape, fan_in, gain=1.0):
        return jax.random.normal(k, shape, f32) * (gain * fan_in ** -0.5)

    def gain(k, shape):
        return 1.0 + 0.02 * jax.random.normal(k, shape, f32)

    x = jax.random.normal(ks[0], (BATCH, SEQ, D), f32)
    c = jax.random.normal(ks[1], (BATCH, D), f32)
    offset = jax.random.randint(ks[2], (BATCH, 1), 0, 1024, dtype=jnp.int32)
    positions = offset + jnp.arange(SEQ, dtype=jnp.int32)[None, :]
    return {
        "x": x,
        "c": c,
        "positions": positions,
        "ada_w": nrm(ks[3], (L, D, 3 * D), D, 0.5),
        "ada_b": 0.01 * jax.random.normal(ks[4], (L, 3 * D), f32),
        "norm_g": gain(ks[5], (L, D)),
        "w_in": nrm(ks[6], (L, D, IN_WIDTH_2), D),
        "cmp_pos": 0.02 * jax.random.normal(ks[7], (L, CMP_BLOCK, NSA_HEAD_DIM), f32),
        "cmp_k_w1": nrm(ks[8], (L, CMP_BLOCK * NSA_HEAD_DIM, CMP_HIDDEN), CMP_BLOCK * NSA_HEAD_DIM),
        "cmp_k_w2": nrm(ks[9], (L, CMP_HIDDEN, NSA_HEAD_DIM), CMP_HIDDEN),
        "cmp_v_w1": nrm(ks[10], (L, CMP_BLOCK * NSA_HEAD_DIM, CMP_HIDDEN), CMP_BLOCK * NSA_HEAD_DIM),
        "cmp_v_w2": nrm(ks[11], (L, CMP_HIDDEN, NSA_HEAD_DIM), CMP_HIDDEN),
        "q_norm_g": gain(ks[12], (L, MLA_Q_RANK)),
        "w_q_up": nrm(ks[13], (L, MLA_Q_RANK, MLA_HEADS * (MLA_NOPE_DIM + MLA_ROPE_DIM)), MLA_Q_RANK),
        "kv_norm_g": gain(ks[14], (L, MLA_KV_RANK)),
        "w_kv_up": nrm(ks[15], (L, MLA_KV_RANK, MLA_HEADS * (MLA_NOPE_DIM + MLA_V_DIM)), MLA_KV_RANK),
        "w_out": nrm(ks[16], (L, MIX_WIDTH, D), MIX_WIDTH),
        "final_norm_g": gain(ks[17], (D,)),
    }

def second_block(x, c, positions, ada_w, ada_b, norm_g, w_in, cmp_pos, cmp_k_w1, cmp_k_w2,
              cmp_v_w1, cmp_v_w2, q_norm_g, w_q_up, kv_norm_g, w_kv_up, w_out, final_norm_g):
    for l in range(DEPTH):
        mod = jax.nn.silu(c) @ ada_w[l] + ada_b[l]
        shift, scl, gate = jnp.split(mod, 3, axis=-1)
        h = rms_norm_2(x, norm_g[l]) * (1.0 + scl[:, None, :]) + shift[:, None, :]

        proj = h @ w_in[l]
        (q_n, kc_n, vc_n, ks_n, vs_n, kw_n, vw_n, gl_n, z_nsa,
         cq_m, ckv_m, kr_m, z_mla) = jnp.split(proj, IN_OFFSETS, axis=-1)

        o_nsa = nsa_attention(q_n, kc_n, vc_n, ks_n, vs_n, kw_n, vw_n, gl_n, positions,
                              cmp_pos[l], cmp_k_w1[l], cmp_k_w2[l], cmp_v_w1[l], cmp_v_w2[l])
        o_mla = mla_attention(cq_m, ckv_m, kr_m, positions,
                              q_norm_g[l], w_q_up[l], kv_norm_g[l], w_kv_up[l])

        mixed = jnp.concatenate([o_nsa * jax.nn.silu(z_nsa), o_mla * jax.nn.silu(z_mla)], axis=-1)
        x = x + gate[:, None, :] * (mixed @ w_out[l])
    return rms_norm_2(x, final_norm_g)


def setup_inputs(seed=0):
    out = dict(first_inputs(seed))
    for name, value in second_inputs(seed + 1).items():
        if name != "x":
            out[name + "_2"] = value
    return out


def reference(
    x, norm_mix_g, w_in, attn_sinks, hgrn_lb_logits, hgrn_norm_g, w_attn_proj, w_hgrn_proj,
    w_out, norm_ffn_g, w_peer_q, peer_keys, peer_u, peer_v, norm_final_g, c_2, positions_2,
    ada_w_2, ada_b_2, norm_g_2, w_in_2, cmp_pos_2, cmp_k_w1_2, cmp_k_w2_2, cmp_v_w1_2,
    cmp_v_w2_2, q_norm_g_2, w_q_up_2, kv_norm_g_2, w_kv_up_2, w_out_2, final_norm_g_2,
):
    x = first_block(
        x, norm_mix_g, w_in, attn_sinks, hgrn_lb_logits, hgrn_norm_g, w_attn_proj, w_hgrn_proj,
        w_out, norm_ffn_g, w_peer_q, peer_keys, peer_u, peer_v, norm_final_g,
    )
    return second_block(
        x, c_2, positions_2, ada_w_2, ada_b_2, norm_g_2, w_in_2, cmp_pos_2, cmp_k_w1_2,
        cmp_k_w2_2, cmp_v_w1_2, cmp_v_w2_2, q_norm_g_2, w_q_up_2, kv_norm_g_2, w_kv_up_2,
        w_out_2, final_norm_g_2,
    )


_drawn_inputs = setup_inputs


def setup_inputs(seed=0):
    import zlib

    import numpy as np

    out = dict(_drawn_inputs(seed))
    spreads = {}
    factors = {'hgrn_lb_logits': 4.482,
     'hgrn_norm_g': 3.29,
     'norm_final_g': 2.875,
     'ada_b_2': 8.0,
     'norm_g_2': 8.0,
     'cmp_pos_2': 8.0,
     'cmp_k_w1_2': 6.258,
     'cmp_k_w2_2': 5.691,
     'q_norm_g_2': 8.0,
     'w_q_up_2': 2.933,
     'kv_norm_g_2': 8.0,
     'final_norm_g_2': 2.843}
    for name, (base, spread) in spreads.items():
        noise = np.random.default_rng([zlib.crc32(name.encode()), seed]).standard_normal(out[name].shape)
        drawn = base * np.exp(spread * noise) if base else spread * noise
        out[name] = __import__('jax').numpy.asarray(drawn.astype(out[name].dtype))
    for name, factor in factors.items():
        out[name] = (out[name] * factor).astype(out[name].dtype)
    return out
```

```python
from contextlib import ExitStack

import numpy as np
import concourse.bass as bass
from concourse import mybir

F32 = mybir.dt.float32
F32R = mybir.dt.float32r
BF16 = mybir.dt.bfloat16
I32 = mybir.dt.int32
U32 = mybir.dt.uint32
ALU = mybir.AluOpType
ACT = mybir.ActivationFunctionType
AX = mybir.AxisListType

P = 128
T = 512
NT = T // P
D = 1024
KD = D // P
HEADS = 8
NEG = -1e30
HG = 4
CHUNK = 32
EXP_N = 128
TOPK = 16
NCMP = 31
RING = 3
NBANK = 3
GRP = 4

VEC = {}
_at = 0
for _n, _w in (("norm_mix_g", 8), ("hgrn_norm_g", 1), ("norm_ffn_g", 8), ("norm_final_g", 8), ("lb0", 4), ("lb1", 4),
               ("ada_b", 24), ("norm_g_2", 8), ("q_norm_g", 2), ("kv_norm_g", 1), ("final_norm_g", 8), ("c", 8)):
    VEC[_n] = (_at, _w)
    _at += _w
NVEC = _at
CST = {}
_at = 0
for _n, _w in (("ident", 128), ("mean1024", 128), ("mean128", 128), ("mean256", 128), ("hgrn_mask", 128),
               ("rot64", 128), ("rot32", 32), ("inv64", 1), ("inv32", 1), ("eps", 1), ("iota", 128), ("iota16", 16),
               ("cmp_mask", 4 * 32)):
    CST[_n] = (_at, _w)
    _at += _w
NCST = _at
CSB = {"ident": (0, 128), "causal": (128, 128), "alibi": (256, 8 * 256), "cmp_bias": (256 + 2048, 4 * 256)}
NCSB = 256 + 2048 + 1024

PAN = {}
_at = 0
for _n, _w in (("q", 4), ("k", 1), ("v", 1), ("hq", 4), ("hf", 4), ("hi", 4), ("hg", 4),
               ("merge", 24), ("out", 8), ("peerq", 16), ("ada", 24),
               ("q2", 4), ("kc", 1), ("vc", 1), ("ks", 1), ("vs", 1), ("kw", 1), ("vw", 1), ("gl", 1), ("kr", 1),
               ("zn", 4), ("cq", 2), ("ckv", 1), ("zm", 4), ("out2", 8)):
    PAN[_n] = _at
    _at += _w
NPAN = _at


def program(nc, io):
    top = ExitStack()

    def sb(stack, name, shape, dt=F32):
        return stack.enter_context(nc.sbuf_tensor(name, shape, dt))

    used = set()

    def sems(stack, names):
        out = [stack.enter_context(nc.semaphore(n)) for n in names.split()]
        used.update(s.num for s in out)
        return out

    def recycle():
        nums = sorted(used)
        starts = [n for n in nums if n - 1 not in used]
        ends = [n for n in nums if n + 1 not in used]
        with nc.Block() as block:
            @block.sync
            def _(sp):
                for lo, hi in zip(starts, ends):
                    sp.sem_clear(range(lo, hi + 1))
        used.clear()

    ps = top.enter_context(nc.psum_tensor("ps", [P, 8, 512], F32))
    xT = sb(top, "xT", [P, KD, T])
    act_hi = sb(top, "act_hi", [P, KD, T], F32R)
    act_lo = sb(top, "act_lo", [P, KD, T], F32R)
    cf = sb(top, "cf", [P, NCST])
    cb = sb(top, "cb", [P, NCSB], BF16)
    vecs = sb(top, "vecs", [P, NVEC])

    def cst(name):
        a, w = CST[name]
        return cf[:, a:a + w]

    def vec(name, k=0):
        a = VEC[name][0] + k
        return vecs[:, a:a + 1]

    ident = cst("ident")
    identb = cb[:, 0:128]
    causal = cb[:, 128:256]

    class Chain:

        def __init__(self, eng, sem):
            self.eng, self.sem, self.n = eng, sem, 0

        def __call__(self, ins):
            self.n += 1
            ins.then_inc(self.sem, 1)
            self.eng.wait_ge(self.sem, self.n)

    with ExitStack() as st:
        (loaded,) = sems(st, "const_loaded")
        block = st.enter_context(nc.Block())

        @block.sync
        def _(sp):
            sp.dma_start(xT[:], io["x"]).then_inc(loaded, 16)
            sp.dma_start(vecs[:], io["vecs"]).then_inc(loaded, 16)
            sp.dma_start(cf[:], io["cf"]).then_inc(loaded, 16)
            sp.dma_start(cb[:].bitcast(mybir.dt.uint16), io["cb"]).then_inc(loaded, 16)
            sp.wait_ge(loaded, 64)

    def norm_stage(name, src, kt, mean, gain, shift=None, dst_hi=None, dst_lo=None, dst=None):
        with ExitStack() as st:
            sq = sb(st, name + "_sq", [P, 2, T])
            y = sb(st, name + "_y", [P, 2, T])
            rstd = sb(st, name + "_rstd", [P, T])
            sq_ready, sum_step, root_ready, y_ready, hi_ready, lo_done, dve, actc = sems(
                st, " ".join(name + s for s in ("_sq_ready", "_sum_step", "_root", "_y", "_hi", "_lo", "_dve", "_act")))
            block = st.enter_context(nc.Block())

            @block.scalar
            def _(act):
                for k in range(kt):
                    if k >= 2:
                        act.wait_ge(sum_step, k - 1)
                    nc.scalar.activation(sq[:, k % 2], src[:, k], ACT.Square).then_inc(sq_ready, 1)
                act.wait_ge(sum_step, kt)
                nc.scalar.activation(rstd[:], ps[:, 0], ACT.Sqrt, bias=cst("eps")).then_inc(root_ready, 1)
                if dst is None:
                    for k in range(kt):
                        act.wait_ge(y_ready, k + 1)
                        nc.scalar.activation(dst_hi[:, k], y[:, k % 2], ACT.Copy).then_inc(hi_ready, 1)

            @block.tensor
            def _(pe):
                for k in range(kt):
                    pe.wait_ge(sq_ready, k + 1)
                    nc.tensor.matmul(ps[:, 0], mean, sq[:, k % 2], start=k == 0, stop=k == kt - 1).then_inc(sum_step, 1)

            @block.vector
            def _(v):
                step = Chain(v, dve)
                v.wait_ge(root_ready, 1)
                step(nc.vector.reciprocal(rstd[:], rstd[:]))
                for k in range(kt):
                    if dst is None and k >= 2:
                        v.wait_ge(lo_done, k - 1)
                        v.wait_ge(hi_ready, k - 1)
                    out = y[:, k % 2] if dst is None else dst[:, k]
                    ins = nc.vector.scalar_tensor_tensor(out=out, in0=src[:, k], scalar=gain(k), in1=rstd[:],
                                                         op0=ALU.mult, op1=ALU.mult)
                    if shift is not None:
                        step(ins)
                        ins = nc.vector.tensor_scalar(out, out, shift(k), None, ALU.add)
                    ins.then_inc(y_ready, 1)

            if dst is None:
                @block.gpsimd
                def _(pool):
                    for k in range(kt):
                        pool.wait_ge(hi_ready, k + 1)
                        nc.gpsimd.tensor_tensor(dst_lo[:, k], y[:, k % 2], dst_hi[:, k].bitcast(F32),
                                                ALU.subtract).then_inc(lo_done, 1)

    def panel_stage(name, first, specs):
        panel_of, n = [], 0
        for s in specs:
            n += not s.get("same")
            panel_of.append(n - 1)
        last_use = {p: u for u, p in enumerate(panel_of)}
        with ExitStack() as st:
            raw = sb(st, name + "_raw", [P, RING, KD, P])
            whi = sb(st, name + "_whi", [P, 2, KD, P], F32R)
            wlo = sb(st, name + "_wlo", [P, 2, KD, P], F32R)
            hi_ready, lo_ready, bank_ready, evac_act, evac_dve, dve, actc = sems(
                st, " ".join(f"{name}_{x}" for x in "hi_ready lo_ready bank_ready evac_act evac_dve dve act".split()))
            loaded = sems(st, " ".join(f"{name}_loaded{i}" for i in range(RING)))
            block = st.enter_context(nc.Block())

            def wait_out(eng, u):
                on = specs[u]["on"]
                eng.wait_ge(evac_act if on == "act" else evac_dve, sum(s["on"] == on for s in specs[:u + 1]))

            def evac(eng, u, chain):
                s = specs[u]
                for w in s.get("pre", ()):
                    wait_out(eng, w)
                eng.wait_ge(bank_ready, u + 1)
                s["evac"](ps[:, u % NBANK], chain).then_inc(evac_act if s["on"] == "act" else evac_dve, 1)

            @block.sync
            def _(sp):
                for i in range(n):
                    if i >= RING:
                        sp.wait_ge(lo_ready, i - RING + 1)
                    sp.dma_start(raw[:, i % RING], io["panels"][first + i]).then_inc(loaded[i % RING], 16)

            @block.scalar
            def _(act):
                chain = Chain(act, actc)
                for i in range(n + 2):
                    if i < n:
                        act.wait_ge(loaded[i % RING], 16 * (i // RING + 1))
                        if i >= 2:
                            act.wait_ge(bank_ready, last_use[i - 2] + 1)
                            act.wait_ge(lo_ready, i - 1)
                        nc.scalar.activation(whi[:, i % 2], raw[:, i % RING], ACT.Copy).then_inc(hi_ready, 1)
                    for u, p in enumerate(panel_of):
                        if p == i - 2 and specs[u]["on"] == "act":
                            evac(act, u, chain)

            @block.gpsimd
            def _(pool):
                for i in range(n):
                    pool.wait_ge(hi_ready, i + 1)
                    nc.gpsimd.tensor_tensor(wlo[:, i % 2], raw[:, i % RING], whi[:, i % 2].bitcast(F32),
                                            ALU.subtract).then_inc(lo_ready, 1)

            @block.vector
            def _(v):
                chain = Chain(v, dve)
                for u, s in enumerate(specs):
                    if s["on"] == "dve":
                        evac(v, u, chain)

            @block.tensor
            def _(pe):
                for u, s in enumerate(specs):
                    i = panel_of[u]
                    if s.get("after") is not None:
                        wait_out(pe, s["after"])
                    pe.wait_ge(hi_ready, i + 1)
                    pe.wait_ge(lo_ready, i + 1)
                    if u >= NBANK:
                        wait_out(pe, u - NBANK)
                    bank = ps[:, u % NBANK]
                    ahi, alo, ks = s["src"]
                    passes = ((whi, ahi), (whi, alo), (wlo, ahi))
                    tiles = range(NT) if s["kind"] == "V" else (0,)
                    for t in tiles:
                        for x, (w, a) in enumerate(passes):
                            for k in ks:
                                weight = w[:, i % 2, k - ks[0] + s.get("w0", 0)]
                                if s["kind"] == "V":
                                    tok = slice(t * P, (t + 1) * P)
                                    out, lhsT, rhs = bank[:, tok], a[:, k, tok], weight
                                else:
                                    cols = 2 if s["kind"] == "C" else T
                                    out, lhsT, rhs = bank[:, 0:cols], weight, a[:, k, 0:cols]
                                mm = nc.tensor.matmul(out, lhsT, rhs, start=x == 0 and k == ks[0],
                                                      stop=x == 2 and k == ks[-1])
                    mm.then_inc(bank_ready, 1)

    ALLK = list(range(KD))
    act_src = (act_hi, act_lo, ALLK)

    def a_copy(dst):
        return lambda bank, chain: nc.scalar.activation(dst, bank, ACT.Copy)

    def a_func(dst, f):
        return lambda bank, chain: nc.scalar.activation(dst, bank, f)

    def v_copy(dst):
        return lambda bank, chain: nc.vector.tensor_copy(dst, bank)

    def attention_stage(name, jobs, units, sink=None):
        n = len(jobs)
        NS, NPB, NPT = 3, 3, 2
        with ExitStack() as st:
            prob = sb(st, name + "_prob", [P, NPB, T])
            ptT = sb(st, name + "_ptT", [P, 2, NT, T])
            mx = sb(st, name + "_mx", [P, 4, 4])
            rs = sb(st, name + "_rs", [P, 4, 4])
            names = ["scores", "negmax", "expd", "prob", "turned", "copied", "pv", "unit_out", "dve", "sinkexp"]
            scores_ready, negmax_ready, exp_ready, prob_ready, turned, copied, pv_done, unit_out, dve, sinkexp = sems(
                st, " ".join(f"{name}_{x}" for x in names))
            block = st.enter_context(nc.Block())
            groups = sorted({j["group"] for j in jobs})
            last_job = {g: max(i for i, j in enumerate(jobs) if j["group"] == g) for g in groups}
            unit_of = {g: u for u, un in enumerate(units) for g in un["groups"]}

            @block.tensor
            def _(pe):
                def pv(g):
                    u = unit_of[g]
                    un = units[u]
                    if u >= 2 and g == un["groups"][0]:
                        pe.wait_ge(unit_out, u - 1)
                    pe.wait_ge(copied, last_job[g] + 1)
                    bank = ps[:, 5 + u % 2]
                    mms = un["pv"](g, bank, ptT[:, g % 2])
                    for lhsT, rhs, out, start, stop in mms:
                        mm = nc.tensor.matmul(out, lhsT, rhs, start=start, stop=stop)
                    mm.then_inc(pv_done, 1)

                for i in range(n + 3):
                    if i < n:
                        job = jobs[i]
                        if i >= NS:
                            pe.wait_ge(exp_ready, i - NS + 1)
                        bank = ps[:, i % NS]
                        bias = job["bias"]
                        mms = [(l, r, a, b) for l, r, a, b in job["scores"]]
                        mms += [(identb, r, a, b) for r, a, b in bias]
                        for x, (l, r, a, b) in enumerate(mms):
                            mm = nc.tensor.matmul(bank[:, a:b], l, r, start=x == 0, stop=x == len(mms) - 1,
                                                  skip_group_check=True)
                        mm.then_inc(scores_ready, 1)
                    if i >= 2 and i - 2 < n:
                        j = i - 2
                        job = jobs[j]
                        pe.wait_ge(prob_ready, j + 1)
                        if j >= NPT:
                            pe.wait_ge(copied, j - NPT + 1)
                        bank = ps[:, 3 + j % NPT]
                        for c in range(job["n"] // P):
                            mm = nc.tensor.transpose(bank[:, c * P:(c + 1) * P], prob[:, j % NPB, c * P:(c + 1) * P], ident)
                        mm.then_inc(turned, 1)
                    if i >= 3:
                        for g in groups:
                            if last_job[g] == i - 3:
                                pv(g)

            @block.vector
            def _(v):
                chain = Chain(v, dve)

                def finish(j):
                    job = jobs[j]
                    r = rs[:, j % 4]
                    v.wait_ge(exp_ready, j + 1)
                    if job["sink"] is not None:
                        chain(nc.vector.tensor_tensor(r[:, 0:1], r[:, 0:1], r[:, 1:2], ALU.add))
                    chain(nc.vector.reciprocal(r[:, 2:3], r[:, 0:1]))
                    if job["gate"] is not None:
                        chain(nc.vector.tensor_tensor(r[:, 2:3], r[:, 2:3], job["gate"], ALU.mult))
                    pr = prob[:, j % NPB, 0:job["n"]]
                    nc.vector.tensor_scalar(pr, pr, r[:, 2:3], None, ALU.mult).then_inc(prob_ready, 1)

                done = 0
                for j in range(n + 4):
                    if j < n:
                        job = jobs[j]
                        m = mx[:, j % 4]
                        v.wait_ge(scores_ready, j + 1)
                        if j >= 4:
                            v.wait_ge(exp_ready, j - 3)
                        chain(nc.vector.tensor_reduce(m[:, 0:1], ps[:, j % NS, 0:job["n"]], AX.X, ALU.max))
                        if job["sink"] is not None:
                            chain(nc.vector.tensor_scalar(m[:, 1:2], m[:, 0:1], job["scale"], job["sink"], ALU.mult, ALU.max))
                            nc.vector.tensor_scalar(m[:, 1:2], m[:, 1:2], -1.0, None, ALU.mult).then_inc(negmax_ready, 1)
                        else:
                            nc.vector.tensor_scalar(m[:, 1:2], m[:, 0:1], -job["scale"], None, ALU.mult).then_inc(negmax_ready, 1)
                    if 1 <= j <= n:
                        finish(j - 1)
                    while done < len(units) and j >= 4 and last_job[units[done]["groups"][-1]] <= j - 4:
                        v.wait_ge(pv_done, 1 + groups.index(units[done]["groups"][-1]))
                        units[done]["evac"](ps[:, 5 + done % 2], chain).then_inc(unit_out, 1)
                        done += 1

            @block.scalar
            def _(act):
                def copy(j):
                    job = jobs[j]
                    g = job["group"]
                    act.wait_ge(turned, j + 1)
                    if g >= 2:
                        act.wait_ge(pv_done, g - 1)
                    q, chunks = job["query"], job["n"] // P
                    c0 = job["chunk0"]
                    nc.scalar.activation(ptT[:, g % 2, c0:c0 + chunks, q * P:(q + 1) * P],
                                         ps[:, 3 + j % NPT, 0:chunks * P].rearrange("p (c q) -> p c q", c=chunks),
                                         ACT.Copy).then_inc(copied, 1)

                for j in range(n + 2):
                    if j < n:
                        job = jobs[j]
                        act.wait_ge(negmax_ready, j + 1)
                        if j >= NPB:
                            act.wait_ge(turned, j - NPB + 1)
                        if j >= 4:
                            act.wait_ge(prob_ready, j - 3)
                        nm, r = mx[:, j % 4, 1:2], rs[:, j % 4]
                        ins = nc.scalar.activation(prob[:, j % NPB, 0:job["n"]], ps[:, j % NS, 0:job["n"]], ACT.Exp,
                                                   bias=nm, scale=job["scale"], accum_out=r[:, 0:1])
                        if job["sink"] is not None:
                            ins.then_inc(sinkexp, 1)
                            ins = nc.scalar.activation(r[:, 1:2], job["sink"], ACT.Exp, bias=nm)
                        ins.then_inc(exp_ready, 1)
                    if j >= 2:
                        copy(j - 2)

    norm_stage("n1", xT, KD, cst("mean1024"), lambda k: vec("norm_mix_g", k), dst_hi=act_hi, dst_lo=act_lo)

    if io["stop"] == "n1":
        return
    b1 = ExitStack()
    y_hi = sb(b1, "y_hi", [P, KD, T], F32R)
    y_lo = sb(b1, "y_lo", [P, KD, T], F32R)
    b1h = ExitStack()
    hq = sb(b1h, "hq", [P, HG, T])
    hf = sb(b1h, "hf", [P, HG, T])
    hv = sb(b1h, "hv", [P, HG, NT, P])
    hg = sb(b1h, "hg", [P, HG, T])
    b1a = ExitStack()
    qT = sb(b1a, "qT", [P, 4, T])
    kT = sb(b1a, "kT", [P, T])
    vt = sb(b1a, "vt", [P, NT, P])

    def use(kind, on, evac, **more):
        return dict(kind=kind, src=act_src, on=on, evac=evac, **more)

    def merged_tiles(x):
        return x.rearrange("p t d -> p (t d)")

    specs = [use("T", "act", a_copy(qT[:, i])) for i in range(4)]
    specs += [use("T", "dve", v_copy(kT[:])), use("V", "dve", v_copy(merged_tiles(vt[:])))]
    specs += [use("T", "act", a_func(hq[:, i], ACT.Silu)) for i in range(4)]
    specs += [use("T", "dve", v_copy(hf[:, i])) for i in range(4)]
    specs += [use("V", "dve", v_copy(merged_tiles(hv[:, i]))) for i in range(4)]
    specs += [use("T", "act", a_func(hg[:, i], ACT.Silu)) for i in range(4)]
    panel_stage("in1", PAN["q"], specs)
    if io["stop"] == "in1":
        return

    with ExitStack() as st:
        sinks = sb(st, "sinks", [P, HEADS])
        (sk,) = sems(st, "sinks_loaded")
        with nc.Block() as block:
            @block.sync
            def _(sp):
                sp.dma_start(sinks[:], io["sinks"].partition_broadcast(P)).then_inc(sk, 16)
                sp.wait_ge(sk, 16)
        yat = sb(st, "yat", [P, 4, T])
        jobs, units = [], []
        order = [h for i in range(4) for h in (i, i + 4)]
        for g, h in enumerate(order):
            base, i = 64 * (h // 4), h % 4
            for b in range(NT):
                k0 = max(b - 1, 0) * P
                nk = (b + 1) * P - k0
                rows = slice(base, base + 64)
                a0 = CSB["alibi"][0] + h * 256 + (256 - nk)
                jobs.append(dict(scores=[(qT[rows, i, b * P:(b + 1) * P], kT[rows, k0:k0 + nk], 0, nk)], n=nk,
                                 scale=0.125, bias=[(cb[:, a0:a0 + nk], 0, nk)], gate=None, sink=sinks[:, h:h + 1],
                                 group=g, query=b, chunk0=2 - nk // P))

        def window_pv():
            def pv(g, bank, pt):
                half = g % 2
                rows = slice(64 * half, 64 * half + 64)
                out = []
                for b in range(NT):
                    for c in ((1,) if b == 0 else (0, 1)):
                        kt = b - 1 + c
                        out.append((vt[:, kt, 64 * half:64 * half + 64], pt[:, c, b * P:(b + 1) * P],
                                    bank[rows, b * P:(b + 1) * P], c == (1 if b == 0 else 0), c == 1))
                return out
            return pv

        for i in range(4):
            units.append(dict(groups=[2 * i, 2 * i + 1], pv=window_pv(),
                              evac=lambda bank, chain, i=i: nc.vector.tensor_copy(yat[:, i], bank)))
        attention_stage("wa", jobs, units)
        hs, ls = sems(st, "wa_hi wa_lo")
        with nc.Block() as block:
            @block.scalar
            def _(act):
                for i in range(4):
                    nc.scalar.activation(y_hi[:, i], yat[:, i], ACT.Copy).then_inc(hs, 1)

            @block.vector
            def _(v):
                for i in range(4):
                    v.wait_ge(hs, i + 1)
                    nc.vector.tensor_tensor(y_lo[:, i], yat[:, i], y_hi[:, i].bitcast(F32), ALU.subtract).then_inc(ls, 1)
    b1a.close()
    if io["stop"] == "wa":
        return

    NC_ = T // CHUNK
    with ExitStack() as st:
        kk = sb(st, "kk", [P, HG, T])
        bA = sb(st, "bA", [P, HG, T])
        bB = sb(st, "bB", [P, HG, T])
        tok = sb(st, "kdec_tok", [P, HG, NT, P])
        state = sb(st, "state", [P, NC_, HG, P])
        at = sb(st, "hgrn_a", [P, 2, HG, P])
        lbx = sb(st, "lbx", [P, 8, HG])
        eb = sb(st, "eb", [P, HG, T])
        kinv = sb(st, "kinv", [P, HG, T])
        d_ = [0]
        names = ("lb e0 f lf b eb e1 e2 kd turned tokc a am ds stt o oe dve actc zero kinvr").split()
        S = dict(zip(names, sems(st, " ".join("hg_" + x for x in names))))
        block = st.enter_context(nc.Block())
        flat = lambda x: x[:].rearrange("p h (c s) -> p (h c) s", s=CHUNK)
        lb0, lb1 = (vecs[:, VEC[n][0]:VEC[n][0] + HG] for n in ("lb0", "lb1"))

        @block.scalar
        def _(act):
            act.wait_ge(S["lb"], 1)
            nc.scalar.activation(lbx[:, 1:3], lbx[:, 1:3], ACT.Exp).then_inc(S["e0"], 1)
            nc.scalar.activation(bA[:], hf[:], ACT.Sigmoid).then_inc(S["e0"], 1)
            act.wait_ge(S["f"], 1)
            nc.scalar.activation(bA[:], bB[:], ACT.Ln).then_inc(S["lf"], 1)
            act.wait_ge(S["b"], 1)
            nc.scalar.activation(eb[:], bB[:], ACT.Exp).then_inc(S["eb"], 1)
            nc.scalar.activation(kinv[:], bB[:], ACT.Exp, scale=-1.0).then_inc(S["eb"], 1)
            act.wait_ge(S["e1"], 1)
            nc.scalar.activation(bA[:], bA[:], ACT.Exp).then_inc(S["e2"], 1)
            for t in range(NT):
                act.wait_ge(S["turned"], t + 1)
                nc.scalar.activation(tok[:, :, t], ps[:, t % 2].rearrange("p (h d) -> p h d", h=HG), ACT.Copy).then_inc(S["tokc"], 1)
            for t in range(NT):
                act.wait_ge(S["o"], t + 1)
                nc.scalar.activation(hf[:, :, t * P:(t + 1) * P], ps[:, 6 + t % 2].rearrange("p (h s) -> p h s", h=HG),
                                     ACT.Copy).then_inc(S["oe"], 1)

        @block.vector
        def _(v):
            step = Chain(v, S["dve"])
            nc.vector.memset(at[:], 0.0).then_inc(S["zero"], 1)
            step(nc.vector.tensor_tensor(lbx[:, 0], lb0, lb1, ALU.max))
            step(nc.vector.tensor_tensor(lbx[:, 1], lb0, lbx[:, 0], ALU.subtract))
            nc.vector.tensor_tensor(lbx[:, 2], lb1, lbx[:, 0], ALU.subtract).then_inc(S["lb"], 1)
            v.wait_ge(S["e0"], 2)
            step(nc.vector.tensor_tensor(lbx[:, 3], lbx[:, 1], lbx[:, 2], ALU.add))
            step(nc.vector.reciprocal(lbx[:, 4], lbx[:, 3]))
            step(nc.vector.tensor_tensor(lbx[:, 5], lbx[:, 1], lbx[:, 4], ALU.mult))
            step(nc.vector.tensor_scalar(lbx[:, 6], lbx[:, 5], -1.0, 1.0, ALU.mult, ALU.add))
            for h in range(HG):
                ins = nc.vector.tensor_scalar(bB[:, h], bA[:, h], lbx[:, 6, h:h + 1], lbx[:, 5, h:h + 1], ALU.mult, ALU.add)
            step(ins)
            nc.vector.tensor_scalar(kk[:], bB[:], -1.0, 1.0, ALU.mult, ALU.add).then_inc(S["f"], 1)
            v.wait_ge(S["f"], 1)
            v.wait_ge(S["lf"], 1)
            src, dst = bA, bB
            for s in (1, 2, 4, 8, 16):
                nc.vector.tensor_copy(flat(dst)[:, :, 0:s], flat(src)[:, :, 0:s])
                ins = nc.vector.tensor_tensor(flat(dst)[:, :, s:], flat(src)[:, :, s:], flat(src)[:, :, :CHUNK - s], ALU.add)
                if s < 16:
                    step(ins)
                src, dst = dst, src
            ins.then_inc(S["b"], 1)
            v.wait_ge(S["b"], 1)
            last = flat(bB)[:, :, CHUNK - 1:CHUNK].broadcast_to([P, HG * NC_, CHUNK])
            nc.vector.tensor_tensor(flat(bA), last, flat(bB), ALU.subtract).then_inc(S["e1"], 1)
            v.wait_ge(S["eb"], 2)
            nc.vector.tensor_tensor(hq[:], hq[:], eb[:], ALU.mult).then_inc(S["kinvr"], 1)
            nc.vector.tensor_tensor(kinv[:], kinv[:], kk[:], ALU.mult).then_inc(S["kinvr"], 1)
            v.wait_ge(S["e2"], 1)
            nc.vector.tensor_tensor(kk[:], kk[:], bA[:], ALU.mult).then_inc(S["kd"], 1)
            v.wait_ge(S["zero"], 1)
            na = 0
            for c in range(NC_):
                if c % 4 == 0:
                    t = c // 4
                    v.wait_ge(S["a"], t + 1)
                    if t >= 2:
                        v.wait_ge(S["o"], t - 1)
                    for h in range(HG):
                        ins = nc.vector.copy_predicated(at[:, t % 2, h], cst("hgrn_mask").bitcast(I32),
                                                        ps[:, 2 + t % 2, h * P:(h + 1) * P])
                    ins.then_inc(S["am"], 1)
                if c < NC_ - 1:
                    v.wait_ge(S["ds"], c + 1)
                    if c >= 1:
                        v.wait_ge(S["stt"], c)
                    for h in range(HG):
                        d = ps[:, 4 + c % 2, h * P:(h + 1) * P]
                        if c == 0:
                            ins = nc.vector.tensor_copy(state[:, 1, h], d)
                        else:
                            ins = nc.vector.scalar_tensor_tensor(
                                out=state[:, c + 1, h], in0=state[:, c, h],
                                scalar=eb[:, h, c * CHUNK + CHUNK - 1:(c + 1) * CHUNK], in1=d, op0=ALU.mult, op1=ALU.add)
                    ins.then_inc(S["stt"], 1)

        @block.tensor
        def _(pe):
            pe.wait_ge(S["kd"], 1)
            for t in range(NT):
                if t >= 2:
                    pe.wait_ge(S["tokc"], t - 1)
                for h in range(HG):
                    mm = nc.tensor.transpose(ps[:, t % 2, h * P:(h + 1) * P], kk[:, h, t * P:(t + 1) * P], ident)
                mm.then_inc(S["turned"], 1)
            pe.wait_ge(S["kinvr"], 2)

            def amat(t):
                if t >= 2:
                    pe.wait_ge(S["am"], t - 1)
                for h in range(HG):
                    s = slice(t * P, (t + 1) * P)
                    mm = nc.tensor.matmul(ps[:, 2 + t % 2, h * P:(h + 1) * P], kinv[:, h, s], hq[:, h, s], start=True, stop=True)
                mm.then_inc(S["a"], 1)

            def ds(c):
                t, r = c // 4, slice(CHUNK * (c % 4), CHUNK * (c % 4) + CHUNK)
                pe.wait_ge(S["tokc"], t + 1)
                if c >= 2:
                    pe.wait_ge(S["stt"], c - 1)
                for h in range(HG):
                    mm = nc.tensor.matmul(ps[:, 4 + c % 2, h * P:(h + 1) * P], tok[r, h, t], hv[r, h, t], start=True, stop=True)
                mm.then_inc(S["ds"], 1)

            def out(t):
                pe.wait_ge(S["am"], t + 1)
                if t >= 2:
                    pe.wait_ge(S["oe"], t - 1)
                pe.wait_ge(S["stt"], 4 * t + 3)
                for h in range(HG):
                    bank = ps[:, 6 + t % 2, h * P:(h + 1) * P]
                    nc.tensor.matmul(bank, hv[:, h, t], at[:, t % 2, h], start=True, stop=False, skip_group_check=True)
                    for c in range(4 * t, 4 * t + 4):
                        if c:
                            s = slice(CHUNK * (c % 4), CHUNK * (c % 4) + CHUNK)
                            mm = nc.tensor.matmul(bank[:, s], state[:, c, h], hq[:, h, c * CHUNK:(c + 1) * CHUNK],
                                                  start=False, stop=c % 4 == 3, skip_group_check=True)
                mm.then_inc(S["o"], 1)

            amat(0)
            for c in range(NC_):
                if c < NC_ - 1:
                    ds(c)
                if c % 4 == 1 and c // 4 + 1 < NT:
                    amat(c // 4 + 1)
                if c % 4 == 3:
                    out(c // 4)
    with ExitStack() as st:
        yt = sb(st, "yt", [P, 2, T])
        rt = sb(st, "rt", [P, 2, T])
        sq = sb(st, "sq", [P, HG, T])
        names = ("sq mean root r y hi lo dve").split()
        S = dict(zip(names, sems(st, " ".join("hn_" + x for x in names))))
        block = st.enter_context(nc.Block())

        @block.scalar
        def _(act):
            nc.scalar.activation(sq[:], hf[:], ACT.Square).then_inc(S["sq"], 1)
            for h in range(HG):
                act.wait_ge(S["mean"], h + 1)
                if h >= 2:
                    act.wait_ge(S["y"], h - 1)
                nc.scalar.activation(rt[:, h % 2], ps[:, h], ACT.Sqrt, bias=cst("eps")).then_inc(S["root"], 1)
            for h in range(HG):
                act.wait_ge(S["y"], h + 1)
                nc.scalar.activation(y_hi[:, 4 + h], hg[:, h], ACT.Copy).then_inc(S["hi"], 1)

        @block.tensor
        def _(pe):
            pe.wait_ge(S["sq"], 1)
            for h in range(HG):
                nc.tensor.matmul(ps[:, h], cst("mean128"), sq[:, h], start=True, stop=True).then_inc(S["mean"], 1)

        @block.vector
        def _(v):
            step = Chain(v, S["dve"])
            for h in range(HG):
                v.wait_ge(S["root"], h + 1)
                step(nc.vector.reciprocal(rt[:, h % 2], rt[:, h % 2]))
                step(nc.vector.scalar_tensor_tensor(out=yt[:, h % 2], in0=hf[:, h], scalar=vec("hgrn_norm_g"),
                                                    in1=rt[:, h % 2], op0=ALU.mult, op1=ALU.mult))
                nc.vector.tensor_tensor(hg[:, h], hg[:, h], yt[:, h % 2], ALU.mult).then_inc(S["y"], 1)
            for h in range(HG):
                v.wait_ge(S["hi"], h + 1)
                nc.vector.tensor_tensor(y_lo[:, 4 + h], hg[:, h], y_hi[:, 4 + h].bitcast(F32), ALU.subtract).then_inc(S["lo"], 1)
    b1h.close()
    if io["stop"] == "hgrn":
        return

    with ExitStack() as st:
        ga = sb(st, "ga", [P, 2, T])
        gh = sb(st, "gh", [P, 2, T])
        part = sb(st, "part", [P, 2, T])
        m_hi = sb(st, "m_hi", [P, KD, T], F32R)
        m_lo = sb(st, "m_lo", [P, KD, T], F32R)
        specs = []

        def merge_a(m):
            return lambda bank, chain: nc.vector.tensor_tensor(part[:, m % 2], bank, ga[:, m % 2], ALU.mult)

        def merge_h(m):
            def f(bank, chain):
                chain(nc.vector.tensor_tensor(gh[:, m % 2], bank, gh[:, m % 2], ALU.mult))
                chain(nc.vector.tensor_tensor(part[:, m % 2], part[:, m % 2], gh[:, m % 2], ALU.add))
                chain(nc.vector.tensor_copy(m_hi[:, m], part[:, m % 2]))
                return nc.vector.tensor_tensor(m_lo[:, m], part[:, m % 2], m_hi[:, m].bitcast(F32), ALU.subtract)
            return f

        for m in range(KD):
            u = 4 * m
            free = [u - 5] if m >= 2 else []
            specs.append(use("T", "act", a_func(ga[:, m % 2], ACT.Sigmoid), pre=free))
            specs.append(use("T", "act", a_func(gh[:, m % 2], ACT.Sigmoid), pre=free))
            specs.append(dict(kind="T", src=(y_hi, y_lo, [0, 1, 2, 3]), on="dve", evac=merge_a(m), pre=[u + 1]))
            specs.append(dict(kind="T", src=(y_hi, y_lo, [4, 5, 6, 7]), w0=4, on="dve", evac=merge_h(m), pre=[u + 1], same=True))
        for m in range(KD):
            specs.append(dict(kind="T", src=(m_hi, m_lo, ALLK), on="dve", after=31,
                              evac=lambda bank, chain, m=m: nc.vector.tensor_tensor(xT[:, m], bank, xT[:, m], ALU.add)))
        panel_stage("mg", PAN["merge"], specs)
    b1.close()
    recycle()
    if io["stop"] == "mix":
        return

    norm_stage("n2", xT, KD, cst("mean1024"), lambda k: vec("norm_ffn_g", k), dst_hi=act_hi, dst_lo=act_lo)
    pr = ExitStack()
    i1T = sb(pr, "i1T", [P, T])
    i2T = sb(pr, "i2T", [P, T])
    gT = sb(pr, "gT", [P, T])
    HP = 2 * HEADS
    with ExitStack() as stq:
        q_all = sb(stq, "q_all", [P, HP, T])
        panel_stage("pq", PAN["peerq"], [use("T", ("act", "dve")[i % 2], (a_copy, v_copy)[i % 2](q_all[:, i])) for i in range(HP)])
        with ExitStack() as st:
            keys = sb(st, "keys", [P, HP, EXP_N])
            val = sb(st, "val", [P, NT, HEADS, 2, TOPK])
            idx = sb(st, "idx", [P, NT, HEADS, 2, TOPK], U32)
            idf = sb(st, "idf", [P, NT, HEADS, 2, TOPK])
            rest = sb(st, "rest", [P, NT, 256])
            cand = sb(st, "cand", [P, NT, 256])
            best = sb(st, "best", [P, NT, HEADS, TOPK])
            pos = sb(st, "pos", [P, NT, HEADS, TOPK], U32)
            posh = sb(st, "posh", [P, NT, HEADS, TOPK], U32)
            posf = sb(st, "posf", [P, 2, NT, HEADS * TOPK])
            onehot = sb(st, "onehot", [P, HEADS, TOPK, TOPK])
            pick = sb(st, "pick", [P, 2, NT, HEADS * TOPK])
            gate = sb(st, "gate", [P, NT, HEADS, TOPK])
            gsum = sb(st, "gsum", [P, NT, HEADS])
            names = "keys sc top dve ex exd gt tr trc".split()
            S = dict(zip(names, sems(st, " ".join("tk_" + x for x in names))))
            block = st.enter_context(nc.Block())

            @block.sync
            def _(sp):
                sp.dma_start(keys[:], io["keys"]).then_inc(S["keys"], 16)

            @block.tensor
            def _(pe):
                pe.wait_ge(S["keys"], 16)
                for i in range(HP):
                    if i >= 4:
                        pe.wait_ge(S["top"], i - 3)
                    for t in range(NT):
                        mm = nc.tensor.matmul(ps[:, i % 4, t * P:(t + 1) * P], q_all[:, i, t * P:(t + 1) * P], keys[:, i],
                                              start=True, stop=True)
                    mm.then_inc(S["sc"], 1)
                pe.wait_ge(S["gt"], 1)
                for a, src in enumerate((pick[:, 0], pick[:, 1], gate[:].rearrange("p t h k -> p t (h k)"))):
                    for t in range(NT):
                        mm = nc.tensor.transpose(ps[:, 4 + a, t * P:(t + 1) * P], src[:, t], ident)
                mm.then_inc(S["tr"], 1)

            @block.vector
            def _(v):
                step = Chain(v, S["dve"])

                def top16(src, values, where):
                    n = src(0).shape[-1]
                    for half in range(2):
                        s = slice(8 * half, 8 * half + 8)
                        for t in range(NT):
                            ins = nc.vector.max(values(t)[:, s], src(t))
                        step(ins)
                        for t in range(NT):
                            ins = nc.vector.max_index(where(t)[:, s], values(t)[:, s], src(t))
                        if half == 0:
                            for t in range(NT):
                                ins = nc.vector.match_replace(rest[:, t, 0:n], values(t)[:, s], src(t), -3.0e38)
                            src = lambda t: rest[:, t, 0:n]
                            step(ins)
                    return ins

                for i in range(HP):
                    h, p = i // 2, i % 2
                    v.wait_ge(S["sc"], i + 1)
                    top16(lambda t: ps[:, i % 4, t * P:(t + 1) * P], lambda t: val[:, t, h, p],
                          lambda t: idx[:, t, h, p]).then_inc(S["top"], 1)
                    v.wait_ge(S["top"], i + 1)
                step(nc.vector.tensor_copy(idf[:], idx[:]))
                for h in range(HEADS):
                    for t in range(NT):
                        ins = nc.vector.tensor_tensor(cand[:, t].rearrange("p (a b) -> p a b", a=TOPK),
                                                      val[:, t, h, 0].unsqueeze(2).broadcast_to([P, TOPK, TOPK]),
                                                      val[:, t, h, 1].unsqueeze(1).broadcast_to([P, TOPK, TOPK]), ALU.add)
                    step(ins)
                    step(top16(lambda t: cand[:, t], lambda t: best[:, t, h], lambda t: pos[:, t, h]))
                for t in range(NT):
                    ins = nc.vector.tensor_tensor(gate[:, t], best[:, t], best[:, t, :, 0:1].broadcast_to([P, HEADS, TOPK]),
                                                  ALU.subtract)
                ins.then_inc(S["ex"], 1)
                step(nc.vector.tensor_scalar(posh[:], pos[:], 4, None, ALU.logical_shift_right))
                step(nc.vector.tensor_copy(posf[:, 0], posh[:].rearrange("p t h k -> p t (h k)")))
                step(nc.vector.tensor_scalar(posh[:], pos[:], 15, None, ALU.bitwise_and))
                step(nc.vector.tensor_copy(posf[:, 1], posh[:].rearrange("p t h k -> p t (h k)")))
                for a in range(2):
                    for t in range(NT):
                        step(nc.vector.tensor_tensor(onehot[:].rearrange("p h k j -> p (h k) j"),
                                                     posf[:, a, t].unsqueeze(2).broadcast_to([P, HEADS * TOPK, TOPK]),
                                                     cst("iota16").unsqueeze(1).broadcast_to([P, HEADS * TOPK, TOPK]), ALU.is_equal))
                        step(nc.vector.tensor_tensor(onehot[:], onehot[:],
                                                     idf[:, t, :, a].unsqueeze(2).broadcast_to([P, HEADS, TOPK, TOPK]), ALU.mult))
                        step(nc.vector.tensor_reduce(pick[:, a, t], onehot[:].rearrange("p h k j -> p (h k) j"), AX.X, ALU.add))
                v.wait_ge(S["exd"], 1)
                step(nc.vector.tensor_reduce(gsum[:], gate[:], AX.X, ALU.add))
                step(nc.vector.reciprocal(gsum[:], gsum[:]))
                for t in range(NT):
                    ins = nc.vector.tensor_tensor(gate[:, t], gate[:, t], gsum[:, t].unsqueeze(2).broadcast_to([P, HEADS, TOPK]), ALU.mult)
                ins.then_inc(S["gt"], 1)
                v.wait_ge(S["tr"], 1)
                for a, dst in enumerate((i1T, i2T, gT)):
                    nc.vector.tensor_copy(dst[:], ps[:, 4 + a])

            @block.scalar
            def _(act):
                act.wait_ge(S["ex"], 1)
                nc.scalar.activation(gate[:], gate[:], ACT.Exp).then_inc(S["exd"], 1)

    if io["stop"] == "topk":
        return
    gates = io["gates"]
    TB = 4
    with ExitStack() as st:
        rows_ = sb(st, "rows_", [P, 2 * TB, EXP_N])
        cols_ = sb(st, "cols_", [P, 2 * TB, EXP_N])
        stage = sb(st, "stage", [P, EXP_N, P])
        hot, built, copied, stored, cleared = sems(st, "g_hot g_built g_copied g_stored g_cleared")
        block = st.enter_context(nc.Block())
        NB_ = P // TB

        @block.vector
        def _(v):
            def body(first, b, wait):
                for half in range(2):
                    if wait:
                        v.wait_ge(built, b * 2 + half - 1)
                    for x in range(TB):
                        s = half * TB + x
                        tok = bass.ds(first + s, 1)
                        nc.vector.tensor_scalar(rows_[:, s], cst("iota"), i1T[:, tok], None, ALU.is_equal)
                        ins = nc.vector.tensor_scalar(cols_[:, s], cst("iota"), i2T[:, tok], gT[:, tok], ALU.is_equal, ALU.mult)
                    ins.then_inc(hot, 1)
            body(0, 0, False)
            with v.Fori(1, T // (2 * TB)) as b:
                body(b * (2 * TB), b, True)

        @block.tensor
        def _(pe):
            def body(b, wait):
                for half in range(2):
                    pe.wait_ge(hot, b * 2 + half + 1)
                    if wait:
                        pe.wait_ge(copied, b * 2 + half - 1)
                    for x in range(TB):
                        s = half * TB + x
                        mm = nc.tensor.matmul(ps[:, half, x * P:(x + 1) * P], rows_[:, s], cols_[:, s], start=True, stop=True)
                    mm.then_inc(built, 1)
            body(0, False)
            with pe.Fori(1, T // (2 * TB)) as b:
                body(b, True)

        @block.scalar
        def _(act):
            for t in range(NT):
                if t:
                    act.wait_ge(stored, 16 * t)
                with act.Fori(0, NB_ // 2) as b:
                    for half in range(2):
                        act.wait_ge(built, b * 2 + (t * NB_ + half + 1))
                        nc.scalar.activation(stage[:, :, bass.ds(b * (2 * TB) + half * TB, TB)].rearrange("p c t -> p t c"),
                                             ps[:, half].rearrange("p (t c) -> p t c", t=TB), ACT.Copy).then_inc(copied, 1)

        @block.sync
        def _(sp):
            for t in range(NT):
                sp.wait_ge(copied, (t + 1) * NB_)
                sp.dma_start(gates.rearrange("c r t -> r c t")[:, :, t * P:(t + 1) * P], stage[:]).then_inc(stored, 16)
            sp.wait_ge(stored, 16 * NT)
    pr.close()
    if io["stop"] == "gates":
        return

    with ExitStack() as st:
        NG = EXP_N // GRP
        uraw = sb(st, "uraw", [P, 2, KD, P])
        uhi = sb(st, "uhi", [P, 2, KD, P], F32R)
        ulo = sb(st, "ulo", [P, 2, KD, P], F32R)
        vraw = sb(st, "vraw", [P, 2, D])
        vhi = sb(st, "vhi", [P, GRP, D], F32R)
        vlo = sb(st, "vlo", [P, GRP, D], F32R)
        gj = sb(st, "gj", [P, 2, T])
        ge = sb(st, "ge", [P, 2, T])
        w_hi = sb(st, "w_hi", [P, 2 * GRP, T], F32R)
        w_lo = sb(st, "w_lo", [P, 2 * GRP, T], F32R)
        names = ("uhi ulo h gelu w0 w whi vhi vlo out added").split()
        S = dict(zip(names, sems(st, " ".join("ex_" + x for x in names))))
        u_loaded = sems(st, "ex_u_loaded0 ex_u_loaded1")
        v_loaded = sems(st, "ex_v_loaded0 ex_v_loaded1")
        g_loaded = sems(st, "ex_g_loaded0 ex_g_loaded1")
        block = st.enter_context(nc.Block())
        OB = 4

        @block.sync
        def _(sp):
            def load(j, k, wait):
                if wait:
                    sp.wait_ge(S["ulo"], j - 1)
                sp.dma_start(uraw[:, k], io["u"][bass.ds(j, 1)].rearrange("o p k e -> (o p) k e")).then_inc(u_loaded[k], 16)
                if wait:
                    sp.wait_ge(S["w"], j - 1)
                sp.dma_start(gj[:, k], gates[bass.ds(j, 1)].rearrange("o r t -> (o r) t")).then_inc(g_loaded[k], 16)
                if wait:
                    sp.wait_ge(S["vlo"], j - 1)
                sp.dma_start(vraw[:, k], io["v"][bass.ds(j, 1)].rearrange("o p d -> (o p) d")).then_inc(v_loaded[k], 16)
            load(0, 0, False)
            load(1, 1, False)
            with sp.Fori(1, EXP_N // 2) as b:
                load(b * 2, 0, True)
                load(b * 2 + 1, 1, True)

        @block.scalar
        def _(act):
            def split_u(j, k, wait):
                act.wait_ge(u_loaded[k % 2], (j - k % 2) * 8 + 16)
                if wait:
                    act.wait_ge(S["h"], j - 1)
                    act.wait_ge(S["ulo"], j - 1)
                nc.scalar.activation(uhi[:, k % 2], uraw[:, k % 2], ACT.Copy).then_inc(S["uhi"], 1)

            def gelu(j, k, wait):
                act.wait_ge(S["h"], j + 1)
                if wait:
                    act.wait_ge(S["w"], j - 1)
                nc.scalar.activation(ge[:, k % 2], ps[:, k % 2], ACT.Gelu).then_inc(S["gelu"], 1)

            def split_v(j, k, n_out, wait):
                act.wait_ge(v_loaded[k % 2], (j - k % 2) * 8 + 16)
                if wait and k == 0:
                    act.wait_ge(S["out"], n_out)
                nc.scalar.activation(vhi[:, k], vraw[:, k % 2], ACT.Copy).then_inc(S["vhi"], 1)

            split_u(0, 0, False)
            split_u(1, 1, False)
            gelu(0, 0, False)

            def group(g, first, last):
                j = g * GRP
                for k in range(GRP):
                    if not (last and k >= 2):
                        split_u(j + (k + 2), k + 2, True)
                    split_v(j + k, k, g * KD, not first)
                    if not (last and k == 3):
                        gelu(j + (k + 1), k + 1, not (first and k == 0))
            group(0, True, False)
            with act.Fori(1, NG - 1) as g:
                group(g, False, False)
            group(NG - 1, False, True)

        @block.gpsimd
        def _(pool):
            def split_v(j, k):
                pool.wait_ge(S["vhi"], j + 1)
                nc.gpsimd.tensor_tensor(vlo[:, k], vraw[:, k % 2], vhi[:, k].bitcast(F32), ALU.subtract).then_inc(S["vlo"], 1)
            with pool.Fori(0, NG) as g:
                for k in range(GRP):
                    split_v(g * GRP + k, k)

        @block.vector
        def _(v):
            def split_u(j, k):
                v.wait_ge(S["uhi"], j + 1)
                nc.vector.tensor_tensor(ulo[:, k % 2], uraw[:, k % 2], uhi[:, k % 2].bitcast(F32), ALU.subtract).then_inc(S["ulo"], 1)

            def weigh(j, k, par, n_out, wait):
                slot = par * GRP + k % GRP
                v.wait_ge(S["gelu"], j + 1)
                v.wait_ge(g_loaded[k % 2], (j - k % 2) * 8 + 16)
                nc.vector.tensor_tensor(ge[:, k % 2], ge[:, k % 2], gj[:, k % 2], ALU.mult).then_inc(S["w0"], 1)
                v.wait_ge(S["w0"], j + 1)
                if wait:
                    v.wait_ge(S["out"], n_out)
                nc.vector.tensor_copy(w_hi[:, slot], ge[:, k % 2]).then_inc(S["whi"], 1)
                v.wait_ge(S["whi"], j + 1)
                nc.vector.tensor_tensor(w_lo[:, slot], ge[:, k % 2], w_hi[:, slot].bitcast(F32), ALU.subtract).then_inc(S["w"], 1)

            def add(g, m):
                v.wait_ge(S["out"], g * KD + m + 1)
                nc.vector.tensor_tensor(xT[:, m], ps[:, 2 + m % OB], xT[:, m], ALU.add).then_inc(S["added"], 1)

            split_u(0, 0)
            split_u(1, 1)
            weigh(0, 0, 0, 0, False)

            def group(g, par, first, last, wait):
                j = g * GRP
                for k in range(GRP):
                    if not (last and k >= 2):
                        split_u(j + (k + 2), k + 2)
                    if not (last and k == 3):
                        p2 = par if k < 3 else 1 - par
                        weigh(j + (k + 1), k + 1, p2, (g - 1) * KD if k < 3 else g * KD, wait if k < 3 else not first)
                for m in range(KD):
                    add(g, m)
            group(0, 0, True, False, False)
            group(1, 1, False, False, False)
            with v.Fori(1, NG // 2 - 1) as b:
                group(b * 2, 0, False, False, True)
                group(b * 2 + 1, 1, False, False, True)
            group(NG - 2, 0, False, False, True)
            group(NG - 1, 1, False, True, True)

        @block.tensor
        def _(pe):
            def hidden(j, k, wait):
                pe.wait_ge(S["uhi"], j + 1)
                pe.wait_ge(S["ulo"], j + 1)
                if wait:
                    pe.wait_ge(S["gelu"], j - 1)
                for x, (w, a) in enumerate(((uhi, act_hi), (uhi, act_lo), (ulo, act_hi))):
                    for d in range(KD):
                        mm = nc.tensor.matmul(ps[:, k % 2], w[:, k % 2, d], a[:, d], start=x == 0 and d == 0, stop=x == 2 and d == KD - 1)
                mm.then_inc(S["h"], 1)

            def outputs(g, par, first):
                pe.wait_ge(S["w"], g * GRP + GRP)
                pe.wait_ge(S["vlo"], g * GRP + GRP)
                for m in range(KD):
                    if not first or m >= OB:
                        pe.wait_ge(S["added"], g * KD + (m - OB + 1))
                    cols = slice(m * P, (m + 1) * P)
                    for k in range(GRP):
                        for x, (w, a) in enumerate(((vhi, w_hi), (vhi, w_lo), (vlo, w_hi))):
                            mm = nc.tensor.matmul(ps[:, 2 + m % OB], w[:, k, cols], a[:, par * GRP + k],
                                                  start=k == 0 and x == 0, stop=k == GRP - 1 and x == 2)
                    mm.then_inc(S["out"], 1)

            hidden(0, 0, False)

            def group(g, par, first, last):
                j = g * GRP
                for k in range(GRP):
                    if not (last and k == 3):
                        hidden(j + (k + 1), k + 1, not (first and k == 0))
                outputs(g, par, first)
            group(0, 0, True, False)
            with pe.Fori(0, (NG - 2) // 2) as b:
                group(b * 2 + 1, 1, False, False)
                group(b * 2 + 2, 0, False, False)
            group(NG - 1, 1, False, True)
    recycle()
    if io["stop"] == "peer":
        return

    norm_stage("nf", xT, KD, cst("mean1024"), lambda k: vec("norm_final_g", k), dst=xT)
    b2 = ExitStack()
    mod = sb(b2, "mod", [P, 24])
    gain2 = sb(b2, "gain2", [P, KD])
    with ExitStack() as st:
        c_act = sb(st, "c_act", [P, KD])
        c_hi = sb(st, "c_hi", [P, KD, 2], F32R)
        c_lo = sb(st, "c_lo", [P, KD, 2], F32R)
        (c_step,) = sems(st, "c_step")
        with nc.Block() as block:
            @block.scalar
            def _(act):
                a = VEC["c"][0]
                nc.scalar.activation(c_act[:], vecs[:, a:a + KD], ACT.Silu).then_inc(c_step, 1)

            @block.vector
            def _(v):
                v.wait_ge(c_step, 1)
                twice = c_act[:].unsqueeze(2).broadcast_to([P, KD, 2])
                nc.vector.tensor_copy(c_hi[:], twice).then_inc(c_step, 1)
                v.wait_ge(c_step, 2)
                nc.vector.tensor_tensor(c_lo[:], twice, c_hi[:].bitcast(F32), ALU.subtract)
        panel_stage("ada", PAN["ada"], [
            dict(kind="C", src=(c_hi, c_lo, ALLK), on="dve",
                 evac=lambda bank, chain, m=m: nc.vector.tensor_tensor(mod[:, m:m + 1], bank[:, 0:1], vec("ada_b", m), ALU.add))
            for m in range(24)])
        (g_step,) = sems(st, "g_step")
        with nc.Block() as block:
            @block.vector
            def _(v):
                a = VEC["norm_g_2"][0]
                nc.vector.tensor_scalar(gain2[:], mod[:, 8:16], 1.0, None, ALU.add).then_inc(g_step, 1)
                v.wait_ge(g_step, 1)
                nc.vector.tensor_tensor(gain2[:], gain2[:], vecs[:, a:a + KD], ALU.mult)
    norm_stage("n3", xT, KD, cst("mean1024"), lambda k: gain2[:, k:k + 1], shift=lambda k: mod[:, k:k + 1],
               dst_hi=act_hi, dst_lo=act_lo)

    q2 = sb(b2, "q2", [P, 4, T])
    kc2, vc2, ks2, kw2, kr2 = (sb(b2, n, [P, T]) for n in ("kc2", "vc2", "ks2", "kw2", "kr2"))
    vs2, vw2, glt = (sb(b2, n, [P, NT, P]) for n in ("vs2", "vw2", "glt"))
    zz = sb(b2, "zz", [P, KD, T])
    cq = sb(b2, "cq", [P, 2, T])
    ckv = sb(b2, "ckv", [P, 1, T])
    specs = [use("T", "act", a_copy(q2[:, i])) for i in range(4)]
    specs += [use("T", "dve", v_copy(kc2[:])), use("T", "dve", v_copy(vc2[:])), use("T", "dve", v_copy(ks2[:])),
              use("V", "dve", v_copy(merged_tiles(vs2[:]))), use("T", "dve", v_copy(kw2[:])),
              use("V", "dve", v_copy(merged_tiles(vw2[:]))), use("V", "act", a_func(merged_tiles(glt[:]), ACT.Sigmoid)),
              use("T", "dve", v_copy(kr2[:]))]
    specs += [use("T", "act", a_func(zz[:, i], ACT.Silu)) for i in range(4)]
    specs += [use("T", "dve", v_copy(cq[:, i])) for i in range(2)] + [use("T", "dve", v_copy(ckv[:, 0]))]
    specs += [use("T", "act", a_func(zz[:, 4 + i], ACT.Silu)) for i in range(4)]
    panel_stage("in2", PAN["q2"], specs)

    tabs = sb(b2, "tabs", [P, 4, T])
    with ExitStack() as st:
        posi = sb(st, "posi", [P, T], I32)
        posf = sb(st, "posf2", [P, T])
        ang = sb(st, "ang", [P, 4, T])
        turn = sb(st, "turn", [P, 4, T])
        tmp = sb(st, "rope_tmp", [P, 2, T])
        pl, dve, reduced, sn, rt, ap = sems(st, "pos_loaded rp_dve rp_reduced rp_sin rp_rot rp_applied")
        with nc.Block() as block:
            TWO_PI = 2 * np.pi
            C1 = 6.28125
            C2 = float(np.float32(np.round((TWO_PI - C1) * 2.0 ** 21) / 2.0 ** 21))
            C3 = float(np.float32(TWO_PI - C1 - C2))
            MAGIC = 1.5 * 2.0 ** 23
            LIM = 3.1415925

            @block.sync
            def _(sp):
                sp.dma_start(posi[:], io["pos"].partition_broadcast(P)).then_inc(pl, 16)

            @block.vector
            def _(v):
                step = Chain(v, dve)
                v.wait_ge(pl, 16)
                step(nc.vector.tensor_copy(posf[:], posi[:]))
                for k in range(4):
                    ins = nc.vector.tensor_scalar(ang[:, k], posf[:], cst("inv64" if k < 2 else "inv32"), None, ALU.mult)
                step(ins)
                for k in range(4):
                    ins = nc.vector.tensor_scalar(turn[:, k], ang[:, k], 1 / TWO_PI, 0.25 * (k % 2), ALU.mult, ALU.add)
                step(ins)
                step(nc.vector.tensor_scalar(turn[:], turn[:], MAGIC, MAGIC, ALU.add, ALU.subtract))
                for c in (C1, C2, C3):
                    step(nc.vector.scalar_tensor_tensor(out=ang[:], in0=turn[:], scalar=-c, in1=ang[:], op0=ALU.mult, op1=ALU.add))
                for k in (1, 3):
                    ins = nc.vector.tensor_scalar(ang[:, k], ang[:, k], float(np.pi / 2), None, ALU.add)
                step(ins)
                nc.vector.tensor_scalar(ang[:], ang[:], LIM, -LIM, ALU.min, ALU.max).then_inc(reduced, 1)
                tiles = [q2[:, i] for i in range(4)] + [ks2[:], kw2[:]]
                v.wait_ge(sn, 1)
                for i, x in enumerate(tiles):
                    v.wait_ge(rt, i + 1)
                    nc.vector.tensor_tensor(tmp[:, i % 2], ps[:, i], tabs[:, 0], ALU.mult)
                    step(nc.vector.tensor_tensor(x, x, tabs[:, 1], ALU.mult))
                    nc.vector.tensor_tensor(x, x, tmp[:, i % 2], ALU.add).then_inc(ap, 1)
                v.wait_ge(rt, 7)
                r = slice(64, 96)
                nc.vector.tensor_tensor(tmp[r, 0], ps[r, 6], tabs[r, 2], ALU.mult)
                step(nc.vector.tensor_tensor(kr2[r], kr2[r], tabs[r, 3], ALU.mult))
                nc.vector.tensor_tensor(kr2[r], kr2[r], tmp[r, 0], ALU.add).then_inc(ap, 1)

            @block.scalar
            def _(act):
                act.wait_ge(reduced, 1)
                nc.scalar.activation(tabs[:], ang[:], ACT.Sin).then_inc(sn, 1)

            @block.tensor
            def _(pe):
                for i, x in enumerate([q2[:, i] for i in range(4)] + [ks2[:], kw2[:]]):
                    nc.tensor.matmul(ps[:, i], cst("rot64"), x, start=True, stop=True).then_inc(rt, 1)
                nc.tensor.matmul(ps[64:96, 6], cst("rot32")[64:96], kr2[64:96], start=True, stop=True).then_inc(rt, 1)

    kcr = sb(b2, "kcr", [P, 32])
    vcr = sb(b2, "vcr", [P, 2, 64])
    pcT = sb(b2, "pcT", [P, 2, T])
    with ExitStack() as st:
        w1 = sb(st, "w1", [P, 2, 32, P])
        w2 = sb(st, "w2", [P, 2, 64])
        cpos = sb(st, "cpos", [P, 32])
        kb = sb(st, "kb", [P, 2, 32, NCMP])
        hid = sb(st, "hid", [P, 2, 2, 32])
        ktmp = sb(st, "ktmp", [P, 32])
        sc = sb(st, "sc", [P, NT, 8, 32])
        stat = sb(st, "stat", [P, NT, 4, 8])
        ld, dve, ready, hp, hs, kv, kvc, kro, krr, scs, sub, ex, pr_, tr, trc = sems(
            st, "c_ld c_dve c_blocks c_hp c_hs c_kv c_kvc c_kro c_krr c_scs c_sub c_ex c_pr c_tr c_trc")
        with nc.Block() as block:
            @block.sync
            def _(sp):
                sp.dma_start(cpos[:], io["cpos"]).then_inc(ld, 16)
                sp.dma_start(w2[:], io["w2"]).then_inc(ld, 16)
                sp.dma_start(w1[:], io["w1"]).then_inc(ld, 16)

            @block.vector
            def _(v):
                step = Chain(v, dve)
                nc.vector.memset(hid[:], 0.0)
                v.wait_ge(ld, 48)
                for a, src in enumerate((kc2, vc2)):
                    r = src[:].rearrange("p (n s) -> p s n", s=16)
                    for half in range(2):
                        ins = nc.vector.tensor_tensor(kb[:, a, 16 * half:16 * half + 16], r[:, :, half:half + NCMP],
                                                      cpos[:, 16 * half:16 * half + 16].unsqueeze(2).broadcast_to([P, 16, NCMP]), ALU.add)
                ins.then_inc(ready, 1)
                v.wait_ge(kv, 1)
                nc.vector.tensor_copy(kcr[:], ps[:, 2, 0:32])
                nc.vector.tensor_copy(vcr[:].rearrange("p g d -> p (g d)"), ps[:, 3, 0:128]).then_inc(kvc, 1)
                v.wait_ge(kro, 1)
                at_ends = lambda k: tabs[:, k, 31::16]
                nc.vector.tensor_tensor(ktmp[:, 0:NCMP], ps[:, 0, 0:NCMP], at_ends(0), ALU.mult)
                step(nc.vector.tensor_tensor(kcr[:, 0:NCMP], kcr[:, 0:NCMP], at_ends(1), ALU.mult))
                nc.vector.tensor_tensor(kcr[:, 0:NCMP], kcr[:, 0:NCMP], ktmp[:, 0:NCMP], ALU.add).then_inc(krr, 1)
                for q in range(NT):
                    v.wait_ge(scs, q + 1)
                    b0 = 4 + 2 * (q % 2)
                    s4 = ps[:, b0:b0 + 2, 0:128].rearrange("p g (h k) -> p g h k", h=4)
                    top = stat[:, q, 0].rearrange("p (g h) -> p g h", g=2)
                    step(nc.vector.tensor_reduce(top, s4, AX.X, ALU.max))
                    nc.vector.tensor_tensor(sc[:, q].rearrange("p (g h) k -> p g h k", g=2), s4,
                                            top.unsqueeze(3).broadcast_to([P, 2, 4, 32]), ALU.subtract).then_inc(sub, 1)
                for q in range(NT):
                    v.wait_ge(ex, q + 1)
                    step(nc.vector.tensor_reduce(stat[:, q, 1], sc[:, q], AX.X, ALU.add))
                    step(nc.vector.reciprocal(stat[:, q, 2], stat[:, q, 1]))
                    gates_q = glt[:, q, 0:24].rearrange("p (h b) -> p h b", b=3)[:, :, 0]
                    nc.vector.tensor_tensor(stat[:, q, 3], stat[:, q, 2], gates_q, ALU.mult)
                    m0 = CST["cmp_mask"][0] + q * 32
                    step(nc.vector.tensor_tensor(sc[:, q], sc[:, q], cf[:, m0:m0 + 32].unsqueeze(1).broadcast_to([P, 8, 32]), ALU.mult))
                    nc.vector.tensor_tensor(sc[:, q], sc[:, q], stat[:, q, 3].unsqueeze(2).broadcast_to([P, 8, 32]), ALU.mult).then_inc(pr_, 1)

            @block.scalar
            def _(act):
                act.wait_ge(hp, 1)
                act.wait_ge(ready, 1)
                nc.scalar.activation(hid[:, :, :, 0:NCMP], ps[:, 0:2, 0:64].rearrange("p g (a n) -> p a g n", a=2)[:, :, :, 0:NCMP],
                                     ACT.Silu).then_inc(hs, 1)
                for q in range(NT):
                    act.wait_ge(sub, q + 1)
                    nc.scalar.activation(sc[:, q], sc[:, q], ACT.Exp, scale=0.125).then_inc(ex, 1)
                for g in range(2):
                    act.wait_ge(tr, g + 1)
                    nc.scalar.activation(pcT[:, g], ps[:, 1 + g], ACT.Copy).then_inc(trc, 1)

            @block.tensor
            def _(pe):
                pe.wait_ge(ready, 1)
                for a in range(2):
                    for g in range(2):
                        r = slice(64 * g, 64 * g + 64)
                        c = a * 32
                        for l in range(32):
                            mm = nc.tensor.matmul(ps[:, g, c:c + NCMP], w1[r, a, l], kb[r, a, l], start=l == 0, stop=l == 31)
                mm.then_inc(hp, 1)
                pe.wait_ge(hs, 1)
                for g in range(2):
                    nc.tensor.matmul(ps[64 * g:64 * g + 64, 2, 0:32], w2[:, 0], hid[:, 0, g], start=True, stop=True)
                for g in range(2):
                    for r in range(4):
                        mm = nc.tensor.matmul(ps[32 * r:32 * r + 32, 3, 64 * g:64 * g + 64], hid[:, 1, g], w2[:, 1], start=True, stop=True)
                mm.then_inc(kv, 1)
                pe.wait_ge(kvc, 1)
                nc.tensor.matmul(ps[:, 0, 0:32], cst("rot64"), kcr[:], start=True, stop=True).then_inc(kro, 1)
                pe.wait_ge(krr, 1)
                for q in range(NT):
                    if q >= 2:
                        pe.wait_ge(sub, q - 1)
                    c0 = CSB["cmp_bias"][0] + q * 256
                    for g in range(2):
                        bank = ps[:, 4 + 2 * (q % 2) + g, 0:128]
                        r = slice(64 * g, 64 * g + 64)
                        for h in range(4):
                            nc.tensor.matmul(bank[:, h * 32:h * 32 + 32], q2[r, h, q * P:(q + 1) * P], kcr[r],
                                             start=h == 0, stop=False, skip_group_check=True)
                        mm = nc.tensor.matmul(bank, identb, cb[:, c0:c0 + 128], start=False, stop=True, skip_group_check=True)
                    mm.then_inc(scs, 1)
                pe.wait_ge(pr_, NT)
                for g in range(2):
                    for q in range(NT):
                        mm = nc.tensor.transpose(ps[:, 1 + g, q * P:(q + 1) * P],
                                                 sc[:, q, 4 * g:4 * g + 4].rearrange("p h k -> p (h k)"), ident)
                    mm.then_inc(tr, 1)

    recycle()
    if io["stop"] == "cmp":
        return
    norm_stage("nq", cq, 2, cst("mean256"), lambda k: vec("q_norm_g", k), dst=cq)
    norm_stage("nk", ckv, 1, cst("mean128"), lambda k: vec("kv_norm_g"), dst=ckv)
    qm = sb(b2, "qm", [P, HEADS, T])
    km = sb(b2, "km", [P, HEADS, T])
    vm = sb(b2, "vm", [P, NT, 512])
    with ExitStack() as st:
        qup = sb(st, "qup", [P, 2, 768])
        kvup = sb(st, "kvup", [P, 2, 512])
        tmp = sb(st, "mla_tmp", [P, 2, T])
        ld, dve, qp, qe, kp, ke, rt, ap, vp, ve, kc_ = sems(st, "m_ld m_dve m_qp m_qe m_kp m_ke m_rt m_ap m_vp m_ve m_kc")
        with nc.Block() as block:
            @block.sync
            def _(sp):
                sp.dma_start(qup[:], io["qup"]).then_inc(ld, 16)
                sp.dma_start(kvup[:], io["kvup"]).then_inc(ld, 16)

            @block.gpsimd
            def _(pool):
                for h in range(HEADS):
                    nc.gpsimd.tensor_copy(km[64:96, h], kr2[64:96]).then_inc(kc_, 1)

            @block.tensor
            def _(pe):
                pe.wait_ge(ld, 32)

                def rotate(h):
                    pe.wait_ge(qe, h + 1)
                    if h >= 2:
                        pe.wait_ge(ap, h - 1)
                    nc.tensor.matmul(ps[64:96, 6 + h % 2], cst("rot32")[64:96], qm[64:96, h], start=True, stop=True).then_inc(rt, 1)

                for h in range(HEADS):
                    if h >= 2:
                        pe.wait_ge(qe, h - 1)
                    for k in range(2):
                        mm = nc.tensor.matmul(ps[0:96, h % 2], qup[:, k, h * 96:h * 96 + 96], cq[:, k], start=k == 0, stop=k == 1)
                    mm.then_inc(qp, 1)
                    if h >= 2:
                        pe.wait_ge(ke, h - 1)
                    nc.tensor.matmul(ps[0:64, 2 + h % 2], kvup[:, 0, h * 64:h * 64 + 64], ckv[:, 0], start=True, stop=True).then_inc(kp, 1)
                    if h:
                        rotate(h - 1)
                rotate(HEADS - 1)
                for t in range(NT):
                    if t >= 2:
                        pe.wait_ge(ve, t - 1)
                    nc.tensor.matmul(ps[:, 4 + t % 2], ckv[:, 0, t * P:(t + 1) * P], kvup[:, 1], start=True, stop=True).then_inc(vp, 1)

            @block.scalar
            def _(act):
                for h in range(HEADS):
                    act.wait_ge(qp, h + 1)
                    nc.scalar.activation(qm[0:96, h], ps[0:96, h % 2], ACT.Copy).then_inc(qe, 1)
                    act.wait_ge(kp, h + 1)
                    nc.scalar.activation(km[0:64, h], ps[0:64, 2 + h % 2], ACT.Copy).then_inc(ke, 1)
                for t in range(NT):
                    act.wait_ge(vp, t + 1)
                    nc.scalar.activation(vm[:, t], ps[:, 4 + t % 2], ACT.Copy).then_inc(ve, 1)

            @block.vector
            def _(v):
                step = Chain(v, dve)
                r = slice(64, 96)
                for h in range(HEADS):
                    v.wait_ge(rt, h + 1)
                    nc.vector.tensor_tensor(tmp[r, h % 2], ps[r, 6 + h % 2], tabs[r, 2], ALU.mult)
                    step(nc.vector.tensor_tensor(qm[r, h], qm[r, h], tabs[r, 3], ALU.mult))
                    nc.vector.tensor_tensor(qm[r, h], qm[r, h], tmp[r, h % 2], ALU.add).then_inc(ap, 1)

    jobs, units = [], []
    branches = (("slc", ks2, vs2, 1), ("win", kw2, vw2, 2))
    g = 0

    def causal_job(lhs, rhs, q, scale, gate, group):
        nk = (q + 1) * P
        return dict(scores=[(lhs[..., q * P:(q + 1) * P], rhs[..., 0:nk], 0, nk)], n=nk, scale=scale,
                    bias=[(causal, q * P, nk)], gate=gate, sink=None, group=group, query=q, chunk0=0)

    def causal_pv(values, rows, bank, pt, first, last):
        return [(values[:, kt], pt[:, kt, kt * P:T], bank[rows, kt * P:T], first and kt == 0, last and kt == NT - 1)
                for kt in range(NT)]

    def out_tile(u):
        def f(bank, chain):
            chain(nc.vector.tensor_tensor(zz[:, u], bank, zz[:, u], ALU.mult))
            chain(nc.vector.tensor_copy(act_hi[:, u], zz[:, u]))
            return nc.vector.tensor_tensor(act_lo[:, u], zz[:, u], act_hi[:, u].bitcast(F32), ALU.subtract)
        return f

    def nsa_pv(i):
        def f(g, bank, pt):
            half, br = (g % 4) // 2, g % 2
            rows = slice(64 * half, 64 * half + 64)
            vals = branches[br][2]
            out = []
            if br == 0:
                r = slice(32 * i, 32 * i + 32)
                out.append((vcr[r, half], pcT[r, half], bank[rows], True, False))
            return out + causal_pv(vals[:, :, 64 * half:64 * half + 64], rows, bank, pt, False, br == 1)
        return f

    for i in range(4):
        for half in range(2):
            h = i + 4 * half
            rows = slice(64 * half, 64 * half + 64)
            for _, keys2, _, b in branches:
                for q in range(NT):
                    jobs.append(causal_job(q2[rows, i], keys2[rows], q, 0.125, glt[:, q, 3 * h + b:3 * h + b + 1], g))
                g += 1
        units.append(dict(groups=list(range(4 * i, 4 * i + 4)), pv=nsa_pv(i), evac=out_tile(i)))

    def mla_pv(g, bank, pt):
        h = g - 16
        return causal_pv(vm[:, :, 64 * h:64 * h + 64], slice(64 * (h % 2), 64 * (h % 2) + 64), bank, pt, True, True)

    for h in range(HEADS):
        for q in range(NT):
            jobs.append(causal_job(qm[0:96, h], km[0:96, h], q, 96 ** -0.5, None, g))
        g += 1
    for i in range(4):
        units.append(dict(groups=[16 + 2 * i, 17 + 2 * i], pv=mla_pv, evac=out_tile(4 + i)))
    attention_stage("ca", jobs, units)

    panel_stage("o2", PAN["out2"], [
        dict(kind="T", src=act_src, on="dve",
             evac=lambda bank, chain, m=m: nc.vector.scalar_tensor_tensor(
                 out=xT[:, m], in0=bank, scalar=mod[:, 16 + m:17 + m], in1=xT[:, m], op0=ALU.mult, op1=ALU.add))
        for m in range(KD)])
    b2.close()
    norm_stage("n4", xT, KD, cst("mean1024"), lambda k: vec("final_norm_g", k), dst=xT)
    with ExitStack() as st:
        (stored,) = sems(st, "out_stored")
        with nc.Block() as block:
            @block.sync
            def _(sp):
                sp.dma_start(io["out"], xT[:]).then_inc(stored, 16)
                sp.wait_ge(stored, 16)


def host_constants():
    cf = np.zeros((P, NCST), np.float32)
    cbt = np.zeros((P, NCSB), np.float32)

    def put(name, a):
        c, w = CST[name]
        cf[:, c:c + w] = a
    r = np.arange(P)
    put("ident", np.eye(P))
    put("mean1024", 1 / 1024)
    put("mean128", 1 / 128)
    put("mean256", 1 / 256)
    same = r[:, None] // CHUNK == r[None, :] // CHUNK
    put("hgrn_mask", (same & (r[:, None] <= r[None, :])).astype(np.float32))
    rot = np.zeros((P, P), np.float32)
    for m in range(P):
        if m % 64 < 32:
            rot[m + 32, m] = -1
        else:
            rot[m - 32, m] = 1
    put("rot64", rot)
    rot = np.zeros((P, 32), np.float32)
    for m in range(32):
        if m < 16:
            rot[64 + m + 16, m] = -1
        else:
            rot[64 + m - 16, m] = 1
    put("rot32", rot)
    put("inv64", (np.float32(10000.0) ** (-(r % 32).astype(np.float32) / np.float32(32)))[:, None])
    put("inv32", (np.float32(10000.0) ** (-(r % 16).astype(np.float32) / np.float32(16)))[:, None])
    put("eps", 1e-6)
    put("iota", r[None, :])
    put("iota16", np.arange(16)[None, :])
    ends = 16 * np.arange(32) + 31
    mask = np.zeros((P, 4, 32), np.float32)
    for q in range(4):
        mask[:, q, :NCMP] = ends[None, :NCMP] <= (q * P + r)[:, None]
    put("cmp_mask", mask.reshape(P, -1))
    cbt[:, 0:128] = np.eye(P)
    cbt[:, 128:256] = np.where(r[None, :] <= r[:, None], 0, NEG)
    dist = (r[:, None] + P) - np.arange(2 * P)[None, :]
    valid = (dist >= 0) & (dist < P)
    for h in range(HEADS):
        slope = 2.0 ** -(h + 1)
        cbt[:, 256 + h * 256:256 + (h + 1) * 256] = np.where(valid, -slope * dist * 8.0, NEG)
    bias = np.where(mask > 0, 0, NEG)
    c0 = CSB["cmp_bias"][0]
    cbt[:, c0:c0 + 1024] = np.broadcast_to(bias[:, :, None, :], (P, 4, 8, 32)).reshape(P, -1)
    return cf, (cbt.view(np.uint32) >> 16).astype(np.uint16)


def panels_of(w):
    return w.reshape(KD, P, -1, P).transpose(2, 1, 0, 3)


def columns(v):
    return np.asarray(v, np.float32).reshape(-1, P).T


def lay_out(a):
    f = lambda x: np.asarray(x)
    heads = [h for i in range(4) for h in (i, i + 4)]
    perm = np.concatenate([np.arange(64) + 64 * h for h in heads])
    w = f(a["w_in"])[0]
    o = np.cumsum([0, 512, 128, 128, 512, 512, 512, 512, 1024, 1024])
    part = [w[:, o[i]:o[i + 1]] for i in range(9)]
    pan = [panels_of(part[0][:, perm])] + [panels_of(part[i]) for i in (1, 2, 3, 4, 5, 6)]
    ga, gh = panels_of(part[7]), panels_of(part[8])
    proj = panels_of(np.concatenate([f(a["w_attn_proj"])[0][perm], f(a["w_hgrn_proj"])[0]], axis=0))
    pan.append(np.stack([ga, gh, proj], axis=1).reshape(24, P, KD, P))
    pan.append(panels_of(f(a["w_out"])[0]))
    pan.append(panels_of(f(a["w_peer_q"])[0]))
    pan.append(panels_of(f(a["ada_w_2"])[0]))
    w = f(a["w_in_2"])[0]
    o = np.cumsum([0, 512, 128, 128, 128, 128, 128, 128, 24, 512, 256, 128, 32, 512])
    part = [w[:, o[i]:o[i + 1]] for i in range(13)]
    gl = np.zeros((D, P), np.float32)
    gl[:, 0:24] = part[7]
    kr = np.zeros((D, P), np.float32)
    kr[:, 64:96] = part[11]
    pan += [panels_of(part[0][:, perm])] + [panels_of(part[i]) for i in range(1, 7)]
    pan += [panels_of(gl), panels_of(kr), panels_of(part[8][:, perm]), panels_of(part[9]), panels_of(part[10]), panels_of(part[12])]
    wo = f(a["w_out_2"])[0]
    pan.append(panels_of(np.concatenate([wo[:512][perm], wo[512:]], axis=0)))
    vecs = np.zeros((P, NVEC), np.float32)
    lb = f(a["hgrn_lb_logits"])
    for name, v in (("norm_mix_g", a["norm_mix_g"]), ("hgrn_norm_g", a["hgrn_norm_g"]), ("norm_ffn_g", a["norm_ffn_g"]),
                    ("norm_final_g", a["norm_final_g"]), ("lb0", lb[0]), ("lb1", lb[1]), ("ada_b", a["ada_b_2"]),
                    ("norm_g_2", a["norm_g_2"]), ("q_norm_g", a["q_norm_g_2"]), ("kv_norm_g", a["kv_norm_g_2"]),
                    ("final_norm_g", a["final_norm_g_2"]), ("c", a["c_2"])):
        c, n = VEC[name]
        vecs[:, c:c + n] = columns(v)
    cf, cbt = host_constants()
    w1 = np.stack([f(a["cmp_k_w1_2"])[0], f(a["cmp_v_w1_2"])[0]])
    w1 = w1.reshape(2, 32, 64, P).transpose(2, 0, 1, 3)
    cpos = f(a["cmp_pos_2"])[0].T
    w2 = np.stack([f(a["cmp_k_w2_2"])[0], f(a["cmp_v_w2_2"])[0]], axis=1)
    kvup = f(a["w_kv_up_2"])[0].reshape(P, 8, 2, 64).transpose(0, 2, 1, 3)
    return {
        "x": f(a["x"])[0].T.reshape(KD, P, T).transpose(1, 0, 2),
        "vecs": vecs, "cf": cf, "cb": cbt,
        "sinks": f(a["attn_sinks"])[0],
        "panels": np.concatenate(pan, axis=0),
        "keys": f(a["peer_keys"])[0].transpose(3, 1, 0, 2).reshape(P, 16, EXP_N),
        "u": f(a["peer_u"])[0].reshape(P, P, KD, P).transpose(1, 3, 2, 0),
        "v": f(a["peer_v"])[0].reshape(P, P, D).transpose(1, 0, 2),
        "pos": f(a["positions_2"])[0],
        "w1": np.concatenate([w1, w1], axis=0), "cpos": np.concatenate([cpos, cpos], axis=0), "w2": w2,
        "qup": f(a["w_q_up_2"])[0].reshape(2, P, 768).transpose(1, 0, 2),
        "kvup": kvup.reshape(P, 2, 512),
    }


def build(nc, shapes, stop=""):
    io = {"stop": stop}
    for name, (shape, dt) in shapes.items():
        io[name] = nc.dram_tensor("in_" + name, shape, dt, kind="ExternalInput").ap()
    io["out"] = nc.dram_tensor("out_0", [P, KD, T], F32, kind="ExternalOutput").ap()
    io["gates"] = nc.dram_tensor("gates", [EXP_N, P, T], F32, kind="Internal").ap()
    program(nc, io)


def kernel(**inputs):
    import concourse.bacc as _bacc
    from concourse.bass_utils import run_bass_kernel_spmd as _run
    nc = _bacc.Bacc("TRN2", target_bir_lowering=False, num_devices=1)
    arrays = {k: np.ascontiguousarray(v) for k, v in lay_out(inputs).items()}
    build(nc, {k: (list(v.shape), mybir.dt.from_np(v.dtype)) for k, v in arrays.items()})
    r = _run(nc, [{"in_" + k: v for k, v in arrays.items()}], core_ids=[0])
    return np.ascontiguousarray(r.results[0]["out_0"].transpose(2, 1, 0)).reshape(1, T, D)
```

```python
from contextlib import ExitStack

import numpy as np
import concourse.bass as bass
from concourse import mybir

F32 = mybir.dt.float32
F32R = mybir.dt.float32r
BF16 = mybir.dt.bfloat16
I32 = mybir.dt.int32
U32 = mybir.dt.uint32
ALU = mybir.AluOpType
ACT = mybir.ActivationFunctionType
AX = mybir.AxisListType

P = 128
T = 512
NT = T // P
D = 1024
KD = D // P
HEADS = 8
NEG = -1e30
HG = 4
CHUNK = 32
EXP_N = 128
TOPK = 16
NCMP = 31
RING = 3
NBANK = 8
GRP = 4

VEC = {}
_at = 0
for _n, _w in (("norm_mix_g", 8), ("hgrn_norm_g", 1), ("norm_ffn_g", 8), ("norm_final_g", 8), ("lb0", 4), ("lb1", 4),
               ("ada_b", 24), ("norm_g_2", 8), ("q_norm_g", 2), ("kv_norm_g", 1), ("final_norm_g", 8), ("c", 8)):
    VEC[_n] = (_at, _w)
    _at += _w
NVEC = _at
CST = {}
_at = 0
for _n, _w in (("ident", 128), ("mean1024", 128), ("mean128", 128), ("mean256", 128), ("hgrn_mask", 128),
               ("rot64", 128), ("rot32", 32), ("inv64", 1), ("inv32", 1), ("eps", 1), ("iota", 128), ("iota16", 16),
               ("cmp_mask", 4 * 32)):
    CST[_n] = (_at, _w)
    _at += _w
NCST = _at
CSB = {"ident": (0, 128), "causal": (128, 128), "alibi": (256, 8 * 256), "cmp_bias": (256 + 2048, 4 * 256)}
NCSB = 256 + 2048 + 1024

PAN = {}
_at = 0
for _n, _w in (("hf", 4), ("hq", 4), ("q", 4), ("k", 1), ("v", 1), ("hi", 4), ("hg", 4),
               ("merge", 24), ("out", 8), ("peerq", 16), ("ada", 24),
               ("q2", 4), ("kc", 1), ("vc", 1), ("ks", 1), ("vs", 1), ("kw", 1), ("vw", 1), ("gl", 1), ("kr", 1),
               ("zn", 4), ("cq", 2), ("ckv", 1), ("zm", 4), ("out2", 8)):
    PAN[_n] = _at
    _at += _w
NPAN = _at


def program(nc, io):
    top = ExitStack()

    def sb(stack, name, shape, dt=F32):
        return stack.enter_context(nc.sbuf_tensor(name, shape, dt))

    used = set()

    def sems(stack, names):
        out = [stack.enter_context(nc.semaphore(n)) for n in names.split()]
        used.update(s.num for s in out)
        return out

    def recycle():
        nums = sorted(used)
        starts = [n for n in nums if n - 1 not in used]
        ends = [n for n in nums if n + 1 not in used]
        with nc.Block() as block:
            @block.sync
            def _(sp):
                for lo, hi in zip(starts, ends):
                    sp.sem_clear(range(lo, hi + 1))
        used.clear()

    ps = top.enter_context(nc.psum_tensor("ps", [P, 8, 512], F32))
    xT = sb(top, "xT", [P, KD, T])
    act_hi = sb(top, "act_hi", [P, KD, T], F32R)
    act_lo = sb(top, "act_lo", [P, KD, T], F32R)
    cf = sb(top, "cf", [P, NCST])
    cb = sb(top, "cb", [P, NCSB], BF16)
    vecs = sb(top, "vecs", [P, NVEC])
    mod = sb(top, "mod", [P, 24])
    gain2 = sb(top, "gain2", [P, KD])

    def cst(name):
        a, w = CST[name]
        return cf[:, a:a + w]

    def vec(name, k=0):
        a = VEC[name][0] + k
        return vecs[:, a:a + 1]

    ident = cst("ident")
    identb = cb[:, 0:128]
    causal = cb[:, 128:256]

    class Chain:

        def __init__(self, eng, sem):
            self.eng, self.sem, self.n = eng, sem, 0

        def __call__(self, ins):
            self.n += 1
            ins.then_inc(self.sem, 1)
            self.eng.wait_ge(self.sem, self.n)

    with ExitStack() as st:
        (loaded,) = sems(st, "const_loaded")
        block = st.enter_context(nc.Block())

        @block.sync
        def _(sp):
            sp.dma_start(xT[:], io["x"]).then_inc(loaded, 16)
            sp.dma_start(vecs[:], io["vecs"]).then_inc(loaded, 16)
            sp.dma_start(cf[:], io["cf"]).then_inc(loaded, 16)
            sp.dma_start(cb[:].bitcast(mybir.dt.uint16), io["cb"]).then_inc(loaded, 16)
            sp.wait_ge(loaded, 64)

    def norm_stage(name, src, kt, mean, gain, shift=None, dst_hi=None, dst_lo=None, dst=None):
        with ExitStack() as st:
            sq = sb(st, name + "_sq", [P, 2, T])
            y = sb(st, name + "_y", [P, 2, T])
            rstd = sb(st, name + "_rstd", [P, T])
            sq_ready, sum_step, root_ready, y_ready, hi_ready, lo_done, dve, actc = sems(
                st, " ".join(name + s for s in ("_sq_ready", "_sum_step", "_root", "_y", "_hi", "_lo", "_dve", "_act")))
            block = st.enter_context(nc.Block())

            @block.scalar
            def _(act):
                for k in range(kt):
                    if k >= 2:
                        act.wait_ge(sum_step, k - 1)
                    nc.scalar.activation(sq[:, k % 2], src[:, k], ACT.Square).then_inc(sq_ready, 1)
                act.wait_ge(sum_step, kt)
                nc.scalar.activation(rstd[:], ps[:, 0], ACT.Sqrt, bias=cst("eps")).then_inc(root_ready, 1)
                if dst is None:
                    for k in range(kt):
                        act.wait_ge(y_ready, k + 1)
                        nc.scalar.activation(dst_hi[:, k], y[:, k % 2], ACT.Copy).then_inc(hi_ready, 1)

            @block.tensor
            def _(pe):
                for k in range(kt):
                    pe.wait_ge(sq_ready, k + 1)
                    nc.tensor.matmul(ps[:, 0], mean, sq[:, k % 2], start=k == 0, stop=k == kt - 1).then_inc(sum_step, 1)

            @block.vector
            def _(v):
                step = Chain(v, dve)
                v.wait_ge(root_ready, 1)
                step(nc.vector.reciprocal(rstd[:], rstd[:]))
                for k in range(kt):
                    if dst is None and k >= 2:
                        v.wait_ge(lo_done, k - 1)
                        v.wait_ge(hi_ready, k - 1)
                    out = y[:, k % 2] if dst is None else dst[:, k]
                    ins = nc.vector.scalar_tensor_tensor(out=out, in0=src[:, k], scalar=gain(k), in1=rstd[:],
                                                         op0=ALU.mult, op1=ALU.mult)
                    if shift is not None:
                        step(ins)
                        ins = nc.vector.tensor_scalar(out, out, shift(k), None, ALU.add)
                    ins.then_inc(y_ready, 1)

            if dst is None:
                @block.gpsimd
                def _(pool):
                    for k in range(kt):
                        pool.wait_ge(hi_ready, k + 1)
                        nc.gpsimd.tensor_tensor(dst_lo[:, k], y[:, k % 2], dst_hi[:, k].bitcast(F32),
                                                ALU.subtract).then_inc(lo_done, 1)

    def panel_stage(name, first, specs, side_load=None):
        panel_of, banks, order, n = [], [], {}, 0
        for u, s in enumerate(specs):
            n += s["kind"] in "TV" and not s.get("same")
            panel_of.append(n - 1)
            banks.append(sum(x["kind"] != "N" for x in specs[:u]))
            order[s.get("name", u)] = u
        last_use = {p: banks[u] for u, p in enumerate(panel_of) if specs[u]["kind"] in "TV"}
        holders = [u for u, s in enumerate(specs) if s["kind"] != "N"]
        with ExitStack() as st:
            raw = sb(st, name + "_raw", [P, RING, KD, P])
            whi = sb(st, name + "_whi", [P, 2, KD, P], F32R)
            wlo = sb(st, name + "_wlo", [P, 2, KD, P], F32R)
            hi_ready, lo_ready, bank_ready, evac_act, evac_dve, dve, actc = sems(
                st, " ".join(f"{name}_{x}" for x in "hi_ready lo_ready bank_ready evac_act evac_dve dve act".split()))
            loaded = sems(st, " ".join(f"{name}_loaded{i}" for i in range(RING)))
            block = st.enter_context(nc.Block())

            def wait_out(eng, u):
                on = specs[u]["on"]
                eng.wait_ge(evac_act if on == "act" else evac_dve, sum(s["on"] == on for s in specs[:u + 1]))

            def evac(eng, u, chain):
                s = specs[u]
                for w in s.get("pre", ()):
                    wait_out(eng, order[w])
                if s["kind"] != "N":
                    eng.wait_ge(bank_ready, banks[u] + 1)
                s["evac"](ps[:, banks[u] % NBANK], chain).then_inc(evac_act if s["on"] == "act" else evac_dve, 1)

            @block.sync
            def _(sp):
                for i in range(n):
                    if i >= RING:
                        sp.wait_ge(lo_ready, i - RING + 1)
                    sp.dma_start(raw[:, i % RING], io["panels"][first + i]).then_inc(loaded[i % RING], 16)
                    if i == RING - 1 and side_load:
                        side_load(sp)

            @block.scalar
            def _(act):
                chain = Chain(act, actc)
                for i in range(n + 2):
                    if i < n:
                        act.wait_ge(loaded[i % RING], 16 * (i // RING + 1))
                        if i >= 2:
                            act.wait_ge(bank_ready, last_use[i - 2] + 1)
                            act.wait_ge(lo_ready, i - 1)
                        nc.scalar.activation(whi[:, i % 2], raw[:, i % RING], ACT.Copy).then_inc(hi_ready, 1)
                    for u, p in enumerate(panel_of):
                        if i == (p + 2 if p >= 0 else 0) and specs[u]["on"] == "act":
                            evac(act, u, chain)

            @block.gpsimd
            def _(pool):
                for i in range(n):
                    pool.wait_ge(hi_ready, i + 1)
                    nc.gpsimd.tensor_tensor(wlo[:, i % 2], raw[:, i % RING], whi[:, i % 2].bitcast(F32),
                                            ALU.subtract).then_inc(lo_ready, 1)

            @block.vector
            def _(v):
                chain = Chain(v, dve)
                for u, s in enumerate(specs):
                    if s["on"] == "dve":
                        evac(v, u, chain)

            @block.tensor
            def _(pe):
                for u, s in enumerate(specs):
                    if s["kind"] == "N":
                        continue
                    for w in s.get("after", ()):
                        wait_out(pe, order[w])
                    if banks[u] >= NBANK:
                        wait_out(pe, holders[banks[u] - NBANK])
                    bank = ps[:, banks[u] % NBANK]
                    if s["kind"] == "X":
                        s["pe"](bank).then_inc(bank_ready, 1)
                        continue
                    i = panel_of[u]
                    pe.wait_ge(hi_ready, i + 1)
                    pe.wait_ge(lo_ready, i + 1)
                    ahi, alo, ks = s["src"]
                    passes = ((whi, ahi), (whi, alo), (wlo, ahi))
                    tiles = range(NT) if s["kind"] == "V" else (0,)
                    for t in tiles:
                        for x, (w, a) in enumerate(passes):
                            for k in ks:
                                weight = w[:, i % 2, k - ks[0] + s.get("w0", 0)]
                                if s["kind"] == "V":
                                    tok = slice(t * P, (t + 1) * P)
                                    out, lhsT, rhs = bank[:, tok], a[:, k, tok], weight
                                else:
                                    out, lhsT, rhs = bank, weight, a[:, k]
                                mm = nc.tensor.matmul(out, lhsT, rhs, start=x == 0 and k == ks[0],
                                                      stop=x == 2 and k == ks[-1])
                    mm.then_inc(bank_ready, 1)

    ALLK = list(range(KD))
    act_src = (act_hi, act_lo, ALLK)

    def a_copy(dst):
        return lambda bank, chain: nc.scalar.activation(dst, bank, ACT.Copy)

    def a_func(dst, f):
        return lambda bank, chain: nc.scalar.activation(dst, bank, f)

    def v_copy(dst):
        return lambda bank, chain: nc.vector.tensor_copy(dst, bank)

    def attention_stage(name, jobs, units, chunks=NT):
        n = len(jobs)
        NS, NPB, NPT = 3, 3, 2
        with ExitStack() as st:
            prob = sb(st, name + "_prob", [P, NPB, T])
            ptT = sb(st, name + "_ptT", [P, 2, chunks, T])
            mx = sb(st, name + "_mx", [P, 4, 4])
            rs = sb(st, name + "_rs", [P, 4, 4])
            names = ["scores", "negmax", "expd", "prob", "turned", "copied", "pv", "unit_out", "dve", "sinkexp"]
            scores_ready, negmax_ready, exp_ready, prob_ready, turned, copied, pv_done, unit_out, dve, sinkexp = sems(
                st, " ".join(f"{name}_{x}" for x in names))
            block = st.enter_context(nc.Block())
            groups = sorted({j["group"] for j in jobs})
            last_job = {g: max(i for i, j in enumerate(jobs) if j["group"] == g) for g in groups}
            unit_of = {g: u for u, un in enumerate(units) for g in un["groups"]}

            @block.tensor
            def _(pe):
                def pv(g):
                    u = unit_of[g]
                    un = units[u]
                    if u >= 2 and g == un["groups"][0]:
                        pe.wait_ge(unit_out, u - 1)
                    pe.wait_ge(copied, last_job[g] + 1)
                    bank = ps[:, 5 + u % 2]
                    mms = un["pv"](g, bank, ptT[:, g % 2])
                    for lhsT, rhs, out, start, stop in mms:
                        mm = nc.tensor.matmul(out, lhsT, rhs, start=start, stop=stop)
                    mm.then_inc(pv_done, 1)

                for i in range(n + 3):
                    if i < n:
                        job = jobs[i]
                        if i >= NS:
                            pe.wait_ge(exp_ready, i - NS + 1)
                        bank = ps[:, i % NS]
                        bias = job["bias"]
                        mms = [(l, r, a, b) for l, r, a, b in job["scores"]]
                        mms += [(identb, r, a, b) for r, a, b in bias]
                        for x, (l, r, a, b) in enumerate(mms):
                            mm = nc.tensor.matmul(bank[:, a:b], l, r, start=x == 0, stop=x == len(mms) - 1,
                                                  skip_group_check=True)
                        mm.then_inc(scores_ready, 1)
                    if i >= 2 and i - 2 < n:
                        j = i - 2
                        job = jobs[j]
                        pe.wait_ge(prob_ready, j + 1)
                        if j >= NPT:
                            pe.wait_ge(copied, j - NPT + 1)
                        bank = ps[:, 3 + j % NPT]
                        for c in range(job["n"] // P):
                            mm = nc.tensor.transpose(bank[:, c * P:(c + 1) * P], prob[:, j % NPB, c * P:(c + 1) * P], ident)
                        mm.then_inc(turned, 1)
                    if i >= 3:
                        for g in groups:
                            if last_job[g] == i - 3:
                                pv(g)

            @block.vector
            def _(v):
                chain = Chain(v, dve)

                def finish(j):
                    job = jobs[j]
                    r = rs[:, j % 4]
                    v.wait_ge(exp_ready, j + 1)
                    if job["sink"] is not None:
                        chain(nc.vector.tensor_tensor(r[:, 0:1], r[:, 0:1], r[:, 1:2], ALU.add))
                    chain(nc.vector.reciprocal(r[:, 2:3], r[:, 0:1]))
                    if job["gate"] is not None:
                        chain(nc.vector.tensor_tensor(r[:, 2:3], r[:, 2:3], job["gate"], ALU.mult))
                    pr = prob[:, j % NPB, 0:job["n"]]
                    nc.vector.tensor_scalar(pr, pr, r[:, 2:3], None, ALU.mult).then_inc(prob_ready, 1)

                done = 0
                for j in range(n + 4):
                    if j < n:
                        job = jobs[j]
                        m = mx[:, j % 4]
                        v.wait_ge(scores_ready, j + 1)
                        if j >= 4:
                            v.wait_ge(exp_ready, j - 3)
                        chain(nc.vector.tensor_reduce(m[:, 0:1], ps[:, j % NS, 0:job["n"]], AX.X, ALU.max))
                        if job["sink"] is not None:
                            chain(nc.vector.tensor_scalar(m[:, 1:2], m[:, 0:1], job["scale"], job["sink"], ALU.mult, ALU.max))
                            nc.vector.tensor_scalar(m[:, 1:2], m[:, 1:2], -1.0, None, ALU.mult).then_inc(negmax_ready, 1)
                        else:
                            nc.vector.tensor_scalar(m[:, 1:2], m[:, 0:1], -job["scale"], None, ALU.mult).then_inc(negmax_ready, 1)
                    if 1 <= j <= n:
                        finish(j - 1)
                    while done < len(units) and j >= 4 and last_job[units[done]["groups"][-1]] <= j - 4:
                        v.wait_ge(pv_done, 1 + groups.index(units[done]["groups"][-1]))
                        units[done]["evac"](ps[:, 5 + done % 2], chain).then_inc(unit_out, 1)
                        done += 1

            @block.scalar
            def _(act):
                def copy(j):
                    job = jobs[j]
                    g = job["group"]
                    act.wait_ge(turned, j + 1)
                    if g >= 2:
                        act.wait_ge(pv_done, g - 1)
                    q, chunks = job["query"], job["n"] // P
                    c0 = job["chunk0"]
                    nc.scalar.activation(ptT[:, g % 2, c0:c0 + chunks, q * P:(q + 1) * P],
                                         ps[:, 3 + j % NPT, 0:chunks * P].rearrange("p (c q) -> p c q", c=chunks),
                                         ACT.Copy).then_inc(copied, 1)

                for j in range(n + 2):
                    if j < n:
                        job = jobs[j]
                        act.wait_ge(negmax_ready, j + 1)
                        if j >= NPB:
                            act.wait_ge(turned, j - NPB + 1)
                        if j >= 4:
                            act.wait_ge(prob_ready, j - 3)
                        nm, r = mx[:, j % 4, 1:2], rs[:, j % 4]
                        ins = nc.scalar.activation(prob[:, j % NPB, 0:job["n"]], ps[:, j % NS, 0:job["n"]], ACT.Exp,
                                                   bias=nm, scale=job["scale"], accum_out=r[:, 0:1])
                        if job["sink"] is not None:
                            ins.then_inc(sinkexp, 1)
                            ins = nc.scalar.activation(r[:, 1:2], job["sink"], ACT.Exp, bias=nm)
                        ins.then_inc(exp_ready, 1)
                    if j >= 2:
                        copy(j - 2)

    norm_stage("n1", xT, KD, cst("mean1024"), lambda k: vec("norm_mix_g", k), dst_hi=act_hi, dst_lo=act_lo)

    if io["stop"] == "n1":
        return
    b1 = ExitStack()
    y_hi = sb(b1, "y_hi", [P, KD, T], F32R)
    y_lo = sb(b1, "y_lo", [P, KD, T], F32R)
    b1h = ExitStack()
    hq = sb(b1h, "hq", [P, HG, T])
    hf = sb(b1h, "hf", [P, HG, T])
    hv = sb(b1h, "hv", [P, HG, NT, P])
    hg = sb(b1h, "hg", [P, HG, T])
    kk = sb(b1h, "kk", [P, HG, T])
    bA = sb(b1h, "bA", [P, HG, T])
    bB = sb(b1h, "bB", [P, HG, T])
    eb = sb(b1h, "eb", [P, HG, T])
    kinv = sb(b1h, "kinv", [P, HG, T])
    lbx = sb(b1h, "lbx", [P, 8, HG])
    b1a = ExitStack()
    qT = sb(b1a, "qT", [P, 4, T])
    kT = sb(b1a, "kT", [P, T])
    vt = sb(b1a, "vt", [P, NT, P])

    def use(kind, on, evac, **more):
        return dict(kind=kind, src=act_src, on=on, evac=evac, **more)

    def merged_tiles(x):
        return x.rearrange("p t d -> p (t d)")

    flat = lambda x: x[:].rearrange("p h (c s) -> p (h c) s", s=CHUNK)
    lb0, lb1 = (vecs[:, VEC[n][0]:VEC[n][0] + HG] for n in ("lb0", "lb1"))

    def lower_logits(_, chain):
        chain(nc.vector.tensor_tensor(lbx[:, 0], lb0, lb1, ALU.max))
        nc.vector.tensor_tensor(lbx[:, 1], lb0, lbx[:, 0], ALU.subtract)
        return nc.vector.tensor_tensor(lbx[:, 2], lb1, lbx[:, 0], ALU.subtract)

    def lower_bound(_, chain):
        chain(nc.vector.tensor_tensor(lbx[:, 3], lbx[:, 1], lbx[:, 2], ALU.add))
        chain(nc.vector.reciprocal(lbx[:, 4], lbx[:, 3]))
        chain(nc.vector.tensor_tensor(lbx[:, 5], lbx[:, 1], lbx[:, 4], ALU.mult))
        return nc.vector.tensor_scalar(lbx[:, 6], lbx[:, 5], -1.0, 1.0, ALU.mult, ALU.add)

    def forget(_, chain):
        for h in range(HG):
            ins = nc.vector.tensor_scalar(bB[:, h], bA[:, h], lbx[:, 6, h:h + 1], lbx[:, 5, h:h + 1], ALU.mult, ALU.add)
        chain(ins)
        return nc.vector.tensor_scalar(kk[:], bB[:], -1.0, 1.0, ALU.mult, ALU.add)

    def running_sum(_, chain):
        src, dst = bA, bB
        for s in (1, 2, 4, 8, 16):
            nc.vector.tensor_copy(flat(dst)[:, :, 0:s], flat(src)[:, :, 0:s])
            ins = nc.vector.tensor_tensor(flat(dst)[:, :, s:], flat(src)[:, :, s:], flat(src)[:, :, :CHUNK - s], ALU.add)
            if s < 16:
                chain(ins)
            src, dst = dst, src
        return ins

    def to_last(_, chain):
        last = flat(bB)[:, :, CHUNK - 1:CHUNK].broadcast_to([P, HG * T // CHUNK, CHUNK])
        return nc.vector.tensor_tensor(flat(bA), last, flat(bB), ALU.subtract)

    def both_exps(_, chain):
        nc.scalar.activation(eb[:], bB[:], ACT.Exp)
        return nc.scalar.activation(kinv[:], bB[:], ACT.Exp, scale=-1.0)

    def decayed(_, chain):
        nc.vector.tensor_tensor(hq[:], hq[:], eb[:], ALU.mult)
        return nc.vector.tensor_tensor(kinv[:], kinv[:], kk[:], ALU.mult)

    def own(name, on, evac, *pre):
        return dict(kind="N", name=name, on=on, evac=evac, pre=pre)

    specs = [own("lb logits", "dve", lower_logits),
             own("lb exps", "act", lambda _, c: nc.scalar.activation(lbx[:, 1:3], lbx[:, 1:3], ACT.Exp), "lb logits"),
             own("lb", "dve", lower_bound, "lb exps")]
    specs += [use("T", "act", a_func(bA[:, i], ACT.Sigmoid), name=f"sigmoid {i}") for i in range(4)]
    specs += [use("T", "act", a_func(hq[:, i], ACT.Silu), name=f"hq {i}") for i in range(4)]
    specs += [own("f", "dve", forget, "lb", "sigmoid 3")]
    specs += [use("T", "act", a_copy(qT[:, i])) for i in range(2)]
    specs += [own("log f", "act", lambda _, c: nc.scalar.activation(bA[:], bB[:], ACT.Ln), "f")]
    specs += [own("b", "dve", running_sum, "log f")]
    specs += [use("T", "act", a_copy(qT[:, i])) for i in range(2, 4)]
    specs += [use("T", "dve", v_copy(kT[:])), use("V", "dve", v_copy(merged_tiles(vt[:])))]
    specs += [own("b last - b", "dve", to_last, "b")]
    specs += [use("V", "dve", v_copy(merged_tiles(hv[:, i]))) for i in range(2)]
    specs += [own("exps", "act", both_exps, "b"),
              own("exp last", "act", lambda _, c: nc.scalar.activation(bA[:], bA[:], ACT.Exp), "b last - b")]
    specs += [use("V", "dve", v_copy(merged_tiles(hv[:, i]))) for i in range(2, 4)]
    specs += [own("q and k decayed", "dve", decayed, "exps", "f"),
              own("k to last", "dve", lambda _, c: nc.vector.tensor_tensor(kk[:], kk[:], bA[:], ALU.mult), "exp last", "q and k decayed")]
    specs += [use("T", "act", a_func(hg[:, i], ACT.Silu)) for i in range(4)]
    panel_stage("in1", PAN["hf"], specs)
    if io["stop"] == "in1":
        return

    with ExitStack() as st:
        sinks = sb(st, "sinks", [P, HEADS])
        (sk,) = sems(st, "sinks_loaded")
        with nc.Block() as block:
            @block.sync
            def _(sp):
                sp.dma_start(sinks[:], io["sinks"].partition_broadcast(P)).then_inc(sk, 16)
                sp.wait_ge(sk, 16)
        yat = sb(st, "yat", [P, T])
        jobs, units = [], []
        order = [h for i in range(4) for h in (i, i + 4)]
        for g, h in enumerate(order):
            base, i = 64 * (h // 4), h % 4
            for b in range(NT):
                k0 = max(b - 1, 0) * P
                nk = (b + 1) * P - k0
                rows = slice(base, base + 64)
                a0 = CSB["alibi"][0] + h * 256 + (256 - nk)
                jobs.append(dict(scores=[(qT[rows, i, b * P:(b + 1) * P], kT[rows, k0:k0 + nk], 0, nk)], n=nk,
                                 scale=0.125, bias=[(cb[:, a0:a0 + nk], 0, nk)], gate=None, sink=sinks[:, h:h + 1],
                                 group=g, query=b, chunk0=2 - nk // P))

        def window_pv():
            def pv(g, bank, pt):
                half = g % 2
                rows = slice(64 * half, 64 * half + 64)
                out = []
                for b in range(NT):
                    for c in ((1,) if b == 0 else (0, 1)):
                        kt = b - 1 + c
                        out.append((vt[:, kt, 64 * half:64 * half + 64], pt[:, c, b * P:(b + 1) * P],
                                    bank[rows, b * P:(b + 1) * P], c == (1 if b == 0 else 0), c == 1))
                return out
            return pv

        def out_parts(i):
            def f(bank, chain):
                chain(nc.vector.tensor_copy(yat[:], bank))
                chain(nc.vector.tensor_copy(y_hi[:, i], yat[:]))
                return nc.vector.tensor_tensor(y_lo[:, i], yat[:], y_hi[:, i].bitcast(F32), ALU.subtract)
            return f

        for i in range(4):
            units.append(dict(groups=[2 * i, 2 * i + 1], pv=window_pv(), evac=out_parts(i)))
        attention_stage("wa", jobs, units, 2)
    b1a.close()
    if io["stop"] == "wa":
        return

    NC_ = T // CHUNK
    with ExitStack() as st:
        tok = sb(st, "kdec_tok", [P, HG, NT, P])
        NST = 8
        state = sb(st, "state", [P, NST, HG, P])
        at = sb(st, "hgrn_a", [P, 2, HG, P])
        names = ("turned tokc a am ds stt o oe zero").split()
        S = dict(zip(names, sems(st, " ".join("hg_" + x for x in names))))
        block = st.enter_context(nc.Block())

        @block.scalar
        def _(act):
            for t in range(NT):
                act.wait_ge(S["turned"], t + 1)
                nc.scalar.activation(tok[:, :, t], ps[:, t % 2].rearrange("p (h d) -> p h d", h=HG), ACT.Copy).then_inc(S["tokc"], 1)
            for t in range(NT):
                act.wait_ge(S["o"], t + 1)
                nc.scalar.activation(hf[:, :, t * P:(t + 1) * P], ps[:, 6 + t % 2].rearrange("p (h s) -> p h s", h=HG),
                                     ACT.Copy).then_inc(S["oe"], 1)

        @block.vector
        def _(v):
            nc.vector.memset(at[:], 0.0).then_inc(S["zero"], 1)
            v.wait_ge(S["zero"], 1)
            na = 0
            for c in range(NC_):
                if c % 4 == 0:
                    t = c // 4
                    v.wait_ge(S["a"], t + 1)
                    if t >= 2:
                        v.wait_ge(S["o"], t - 1)
                    for h in range(HG):
                        ins = nc.vector.copy_predicated(at[:, t % 2, h], cst("hgrn_mask").bitcast(I32),
                                                        ps[:, 2 + t % 2, h * P:(h + 1) * P])
                    ins.then_inc(S["am"], 1)
                if c < NC_ - 1:
                    v.wait_ge(S["ds"], c + 1)
                    if c >= 1:
                        v.wait_ge(S["stt"], c)
                    if (c + 1) % 4 == 0 and c + 1 >= NST:
                        v.wait_ge(S["o"], (c + 1 - NST) // 4 + 1)
                    for h in range(HG):
                        d = ps[:, 4 + c % 2, h * P:(h + 1) * P]
                        if c == 0:
                            ins = nc.vector.tensor_copy(state[:, 1, h], d)
                        else:
                            ins = nc.vector.scalar_tensor_tensor(
                                out=state[:, (c + 1) % NST, h], in0=state[:, c % NST, h],
                                scalar=eb[:, h, c * CHUNK + CHUNK - 1:(c + 1) * CHUNK], in1=d, op0=ALU.mult, op1=ALU.add)
                    ins.then_inc(S["stt"], 1)

        @block.tensor
        def _(pe):
            for t in range(NT):
                if t >= 2:
                    pe.wait_ge(S["tokc"], t - 1)
                for h in range(HG):
                    mm = nc.tensor.transpose(ps[:, t % 2, h * P:(h + 1) * P], kk[:, h, t * P:(t + 1) * P], ident)
                mm.then_inc(S["turned"], 1)

            def amat(t):
                if t >= 2:
                    pe.wait_ge(S["am"], t - 1)
                for h in range(HG):
                    s = slice(t * P, (t + 1) * P)
                    mm = nc.tensor.matmul(ps[:, 2 + t % 2, h * P:(h + 1) * P], kinv[:, h, s], hq[:, h, s], start=True, stop=True)
                mm.then_inc(S["a"], 1)

            def ds(c):
                t, r = c // 4, slice(CHUNK * (c % 4), CHUNK * (c % 4) + CHUNK)
                pe.wait_ge(S["tokc"], t + 1)
                if c >= 2:
                    pe.wait_ge(S["stt"], c - 1)
                for h in range(HG):
                    mm = nc.tensor.matmul(ps[:, 4 + c % 2, h * P:(h + 1) * P], tok[r, h, t], hv[r, h, t], start=True, stop=True)
                mm.then_inc(S["ds"], 1)

            def out(t):
                pe.wait_ge(S["am"], t + 1)
                if t >= 2:
                    pe.wait_ge(S["oe"], t - 1)
                pe.wait_ge(S["stt"], 4 * t + 3)
                for h in range(HG):
                    bank = ps[:, 6 + t % 2, h * P:(h + 1) * P]
                    nc.tensor.matmul(bank, hv[:, h, t], at[:, t % 2, h], start=True, stop=False, skip_group_check=True)
                    for c in range(4 * t, 4 * t + 4):
                        if c:
                            s = slice(CHUNK * (c % 4), CHUNK * (c % 4) + CHUNK)
                            mm = nc.tensor.matmul(bank[:, s], state[:, c % NST, h], hq[:, h, c * CHUNK:(c + 1) * CHUNK],
                                                  start=False, stop=c % 4 == 3, skip_group_check=True)
                mm.then_inc(S["o"], 1)

            amat(0)
            for c in range(NC_):
                if c < NC_ - 1:
                    ds(c)
                if c % 4 == 1 and c // 4 + 1 < NT:
                    amat(c // 4 + 1)
                if c % 4 == 3:
                    out(c // 4)
    with ExitStack() as st:
        yt = sb(st, "yt", [P, 2, T])
        rt = sb(st, "rt", [P, 2, T])
        sq = sb(st, "sq", [P, HG, T])
        names = ("sq mean root r y hi lo dve").split()
        S = dict(zip(names, sems(st, " ".join("hn_" + x for x in names))))
        block = st.enter_context(nc.Block())

        @block.scalar
        def _(act):
            nc.scalar.activation(sq[:], hf[:], ACT.Square).then_inc(S["sq"], 1)
            for h in range(HG):
                act.wait_ge(S["mean"], h + 1)
                if h >= 2:
                    act.wait_ge(S["y"], h - 1)
                nc.scalar.activation(rt[:, h % 2], ps[:, h], ACT.Sqrt, bias=cst("eps")).then_inc(S["root"], 1)
            for h in range(HG):
                act.wait_ge(S["y"], h + 1)
                nc.scalar.activation(y_hi[:, 4 + h], hg[:, h], ACT.Copy).then_inc(S["hi"], 1)

        @block.tensor
        def _(pe):
            pe.wait_ge(S["sq"], 1)
            for h in range(HG):
                nc.tensor.matmul(ps[:, h], cst("mean128"), sq[:, h], start=True, stop=True).then_inc(S["mean"], 1)

        @block.vector
        def _(v):
            step = Chain(v, S["dve"])
            for h in range(HG):
                v.wait_ge(S["root"], h + 1)
                step(nc.vector.reciprocal(rt[:, h % 2], rt[:, h % 2]))
                step(nc.vector.scalar_tensor_tensor(out=yt[:, h % 2], in0=hf[:, h], scalar=vec("hgrn_norm_g"),
                                                    in1=rt[:, h % 2], op0=ALU.mult, op1=ALU.mult))
                nc.vector.tensor_tensor(hg[:, h], hg[:, h], yt[:, h % 2], ALU.mult).then_inc(S["y"], 1)
            for h in range(HG):
                v.wait_ge(S["hi"], h + 1)
                nc.vector.tensor_tensor(y_lo[:, 4 + h], hg[:, h], y_hi[:, 4 + h].bitcast(F32), ALU.subtract).then_inc(S["lo"], 1)
    b1h.close()
    if io["stop"] == "hgrn":
        return

    with ExitStack() as st:
        ga = sb(st, "ga", [P, 2, T])
        gh = sb(st, "gh", [P, 2, T])
        part = sb(st, "part", [P, 2, T])
        m_hi = sb(st, "m_hi", [P, KD, T], F32R)
        m_lo = sb(st, "m_lo", [P, KD, T], F32R)
        specs = []

        def merge_a(m):
            return lambda bank, chain: nc.vector.tensor_tensor(part[:, m % 2], bank, ga[:, m % 2], ALU.mult)

        def merge_h(m):
            def f(bank, chain):
                chain(nc.vector.tensor_tensor(gh[:, m % 2], bank, gh[:, m % 2], ALU.mult))
                chain(nc.vector.tensor_tensor(part[:, m % 2], part[:, m % 2], gh[:, m % 2], ALU.add))
                chain(nc.vector.tensor_copy(m_hi[:, m], part[:, m % 2]))
                return nc.vector.tensor_tensor(m_lo[:, m], part[:, m % 2], m_hi[:, m].bitcast(F32), ALU.subtract)
            return f

        for m in range(KD):
            u = 4 * m
            free = [u - 5] if m >= 2 else []
            specs.append(use("T", "act", a_func(ga[:, m % 2], ACT.Sigmoid), pre=free))
            specs.append(use("T", "act", a_func(gh[:, m % 2], ACT.Sigmoid), pre=free))
            specs.append(dict(kind="T", src=(y_hi, y_lo, [0, 1, 2, 3]), on="dve", evac=merge_a(m), pre=[u + 1]))
            specs.append(dict(kind="T", src=(y_hi, y_lo, [4, 5, 6, 7]), w0=4, on="dve", evac=merge_h(m), pre=[u + 1], same=True))
        for m in range(KD):
            specs.append(dict(kind="T", src=(m_hi, m_lo, ALLK), on="dve", after=[31],
                              evac=lambda bank, chain, m=m: nc.vector.tensor_tensor(xT[:, m], bank, xT[:, m], ALU.add)))
        panel_stage("mg", PAN["merge"], specs)
    b1.close()
    recycle()
    if io["stop"] == "mix":
        return

    norm_stage("n2", xT, KD, cst("mean1024"), lambda k: vec("norm_ffn_g", k), dst_hi=act_hi, dst_lo=act_lo)
    pr = ExitStack()
    i1T = sb(pr, "i1T", [P, T])
    i2T = sb(pr, "i2T", [P, T])
    gT = sb(pr, "gT", [P, T])
    HP = 2 * HEADS
    with ExitStack() as st:
        val = sb(st, "val", [P, NT, HEADS, 2, TOPK])
        idx = sb(st, "idx", [P, NT, HEADS, 2, TOPK], U32)
        rest = sb(st, "rest", [P, HEADS, 256])

        def top16(chain, n, src, values, where):
            width = src(0).shape[-1]
            for half in range(2):
                s = slice(8 * half, 8 * half + 8)
                for r in range(n):
                    ins = nc.vector.max(values(r)[:, s], src(r))
                chain(ins)
                for r in range(n):
                    ins = nc.vector.max_index(where(r)[:, s], values(r)[:, s], src(r))
                if half == 0:
                    for r in range(n):
                        ins = nc.vector.match_replace(rest[:, r, 0:width], values(r)[:, s], src(r), -3.0e38)
                    src = lambda r: rest[:, r, 0:width]
                    chain(ins)
            return ins

        with ExitStack() as stq:
            NQ = 4
            q_ring = sb(stq, "q_ring", [P, NQ, T])
            keys = sb(stq, "keys", [P, HP, EXP_N])
            (keys_loaded,) = sems(stq, "keys_loaded")

            def scores(i):
                def f(bank):
                    if i == 0:
                        nc.tensor.wait_ge(keys_loaded, 16)
                    for t in range(NT):
                        mm = nc.tensor.matmul(bank[:, t * P:(t + 1) * P], q_ring[:, i % NQ, t * P:(t + 1) * P], keys[:, i],
                                              start=True, stop=True)
                    return mm
                return f

            def rank(i):
                return lambda bank, chain: top16(chain, NT, lambda t: bank[:, t * P:(t + 1) * P],
                                                 lambda t: val[:, t, i // 2, i % 2], lambda t: idx[:, t, i // 2, i % 2])

            with nc.Block() as block:
                @block.sync
                def _(sp):
                    sp.dma_start(keys[:], io["keys"]).then_inc(keys_loaded, 16)
            specs = []
            place = {}
            order = [("q", 0)] + [x for i in range(1, HP) for x in (("q", i), ("s", i - 1))] + [("s", HP - 1)]
            for u, x in enumerate(order):
                place[x] = u
            for kind, i in order:
                if kind == "q":
                    pre = [place["s", i - NQ]] if i >= NQ else []
                    specs.append(use("T", "act", a_copy(q_ring[:, i % NQ]), pre=pre))
                else:
                    specs.append(dict(kind="X", pe=scores(i), on="dve", evac=rank(i), after=[place["q", i]]))
            panel_stage("pq", PAN["peerq"], specs)

        with ExitStack() as stq:
            idf = sb(stq, "idf", [P, NT, HEADS, 2, TOPK])
            cand = sb(stq, "cand", [P, HEADS, 256])
            best = sb(stq, "best", [P, NT, HEADS, TOPK])
            pos = sb(stq, "pos", [P, HEADS, TOPK], U32)
            posh = sb(stq, "posh", [P, 2, HEADS, TOPK], U32)
            posf = sb(stq, "posf", [P, 2, HEADS * TOPK])
            onehot = sb(stq, "onehot", [P, 2, 2, HEADS, TOPK, TOPK])
            pick = sb(stq, "pick", [P, 2, NT, HEADS * TOPK])
            gate = sb(stq, "gate", [P, NT, HEADS, TOPK])
            gsum = sb(stq, "gsum", [P, NT, HEADS])
            c_act = sb(stq, "c_act", [P, KD])
            ada_w = sb(stq, "ada_w", [P, RING, KD, P])
            c_ready, ada_done, ada_out = sems(stq, "c_ready ada_done ada_out")
            ada_loaded = sems(stq, " ".join(f"ada_loaded{i}" for i in range(RING)))
            names = "dve place eq picked shifted expd gates turned".split()
            S = dict(zip(names, sems(stq, " ".join("tk_" + x for x in names))))
            block = stq.enter_context(nc.Block())

            @block.sync
            def _(sp):
                for i in range(24):
                    if i >= RING:
                        sp.wait_ge(ada_done, i - RING + 1)
                    sp.dma_start(ada_w[:, i % RING], io["panels"][PAN["ada"] + i]).then_inc(ada_loaded[i % RING], 16)

            @block.vector
            def _(v):
                step = Chain(v, S["dve"])

                def pick_sum(t):
                    v.wait_ge(S["eq"], t + 1)
                    for a in range(2):
                        ins = nc.vector.tensor_reduce(pick[:, a, t], onehot[:, t % 2, a].rearrange("p h k j -> p (h k) j"),
                                                      AX.X, ALU.add)
                    ins.then_inc(S["picked"], 1)

                step(nc.vector.tensor_copy(idf[:], idx[:]))
                for t in range(NT):
                    step(nc.vector.tensor_tensor(cand[:].rearrange("p h (a b) -> p h a b", a=TOPK),
                                                 val[:, t, :, 0].unsqueeze(3).broadcast_to([P, HEADS, TOPK, TOPK]),
                                                 val[:, t, :, 1].unsqueeze(2).broadcast_to([P, HEADS, TOPK, TOPK]), ALU.add))
                    step(top16(step, HEADS, lambda h: cand[:, h], lambda h: best[:, t, h], lambda h: pos[:, h]))
                    nc.vector.tensor_scalar(posh[:, 0], pos[:], 4, None, ALU.logical_shift_right)
                    step(nc.vector.tensor_scalar(posh[:, 1], pos[:], 15, None, ALU.bitwise_and))
                    step(nc.vector.tensor_copy(posf[:], posh[:].rearrange("p a h k -> p a (h k)")))
                    for a in range(2):
                        ins = nc.vector.tensor_tensor(onehot[:, t % 2, a].rearrange("p h k j -> p (h k) j"),
                                                      posf[:, a].unsqueeze(2).broadcast_to([P, HEADS * TOPK, TOPK]),
                                                      cst("iota16").unsqueeze(1).broadcast_to([P, HEADS * TOPK, TOPK]), ALU.is_equal)
                    ins.then_inc(S["place"], 1)
                    nc.vector.tensor_tensor(gate[:, t], best[:, t], best[:, t, :, 0:1].broadcast_to([P, HEADS, TOPK]),
                                            ALU.subtract).then_inc(S["shifted"], 1)
                    if t:
                        pick_sum(t - 1)
                v.wait_ge(S["expd"], 1)
                step(nc.vector.tensor_reduce(gsum[:], gate[:], AX.X, ALU.add))
                step(nc.vector.reciprocal(gsum[:], gsum[:]))
                for t in range(NT):
                    ins = nc.vector.tensor_tensor(gate[:, t], gate[:, t], gsum[:, t].unsqueeze(2).broadcast_to([P, HEADS, TOPK]), ALU.mult)
                ins.then_inc(S["gates"], 1)
                pick_sum(NT - 1)
                v.wait_ge(ada_done, 24)
                a, b = VEC["ada_b"][0], VEC["norm_g_2"][0]
                step(nc.vector.tensor_tensor(mod[:], ps[:, 7, 0:24], vecs[:, a:a + 24], ALU.add))
                step(nc.vector.tensor_scalar(gain2[:], mod[:, 8:16], 1.0, None, ALU.add))
                nc.vector.tensor_tensor(gain2[:], gain2[:], vecs[:, b:b + KD], ALU.mult)
                v.wait_ge(S["turned"], 1)
                for a, dst in enumerate((i1T, i2T, gT)):
                    nc.vector.tensor_copy(dst[:], ps[:, 4 + a])

            @block.gpsimd
            def _(pool):
                for t in range(NT):
                    pool.wait_ge(S["place"], t + 1)
                    for a in range(2):
                        ins = nc.gpsimd.tensor_tensor(onehot[:, t % 2, a], onehot[:, t % 2, a],
                                                      idf[:, t, :, a].unsqueeze(2).broadcast_to([P, HEADS, TOPK, TOPK]), ALU.mult)
                    ins.then_inc(S["eq"], 1)

            @block.scalar
            def _(act):
                a = VEC["c"][0]
                nc.scalar.activation(c_act[:], vecs[:, a:a + KD], ACT.Silu).then_inc(c_ready, 1)
                act.wait_ge(S["shifted"], NT)
                nc.scalar.activation(gate[:], gate[:], ACT.Exp).then_inc(S["expd"], 1)

            @block.tensor
            def _(pe):
                def turn(a, src):
                    for t in range(NT):
                        mm = nc.tensor.transpose(ps[:, 4 + a, t * P:(t + 1) * P], src[:, t], ident)
                    return mm
                pe.wait_ge(c_ready, 1)
                for i in range(24):
                    pe.wait_ge(ada_loaded[i % RING], 16 * (i // RING + 1))
                    for k in range(KD):
                        mm = nc.tensor.matmul(ps[:, 7, i:i + 1], ada_w[:, i % RING, k], c_act[:, k:k + 1],
                                              start=k == 0, stop=k == KD - 1)
                    mm.then_inc(ada_done, 1)
                pe.wait_ge(S["gates"], 1)
                turn(2, gate[:].rearrange("p t h k -> p t (h k)"))
                pe.wait_ge(S["picked"], NT)
                turn(0, pick[:, 0])
                turn(1, pick[:, 1]).then_inc(S["turned"], 1)

    if io["stop"] == "topk":
        return
    gates = io["gates"]
    TB = 4
    with ExitStack() as st:
        rows_ = sb(st, "rows_", [P, 2, TB, EXP_N])
        hots_ = sb(st, "hots_", [P, 2, TB, EXP_N])
        cols_ = sb(st, "cols_", [P, 2, TB, EXP_N])
        stage = sb(st, "stage", [P, 2, EXP_N, P])
        row_hot, col_hot, hot, built, copied = sems(st, "g_row_hot g_col_hot g_hot g_built g_copied")
        stored = sems(st, "g_stored0 g_stored1")
        block = st.enter_context(nc.Block())
        NSTEP = T // TB
        PER = P // TB
        shape = [P, TB, EXP_N]
        iota_b = cst("iota").unsqueeze(1).broadcast_to(shape)

        def per_token(x, step):
            return x[:, bass.ds(step * TB, TB)].unsqueeze(2).broadcast_to(shape)

        @block.gpsimd
        def _(pool):
            def body(n, b, wait):
                pool.wait_ge(col_hot, n + 1)
                if wait:
                    pool.wait_ge(built, n - 1)
                nc.gpsimd.tensor_tensor(cols_[:, b], hots_[:, b], per_token(gT, n), ALU.mult).then_inc(hot, 1)
            body(0, 0, False)
            body(1, 1, False)
            with pool.Fori(1, NSTEP // 2) as i:
                body(i * 2, 0, True)
                body(i * 2 + 1, 1, True)

        @block.vector
        def _(v):
            def body(n, b, wait):
                if wait:
                    v.wait_ge(hot, n - 1)
                nc.vector.tensor_tensor(hots_[:, b], iota_b, per_token(i2T, n), ALU.is_equal).then_inc(col_hot, 1)
                if wait:
                    v.wait_ge(built, n - 1)
                nc.vector.tensor_tensor(rows_[:, b], iota_b, per_token(i1T, n), ALU.is_equal).then_inc(row_hot, 1)
            body(0, 0, False)
            body(1, 1, False)
            with v.Fori(1, NSTEP // 2) as i:
                body(i * 2, 0, True)
                body(i * 2 + 1, 1, True)

        @block.tensor
        def _(pe):
            def body(n, b, wait):
                pe.wait_ge(row_hot, n + 1)
                pe.wait_ge(hot, n + 1)
                if wait:
                    pe.wait_ge(copied, n - 1)
                for x in range(TB):
                    mm = nc.tensor.matmul(ps[:, b, x * P:(x + 1) * P], rows_[:, b, x], cols_[:, b, x], start=True, stop=True)
                mm.then_inc(built, 1)
            body(0, 0, False)
            body(1, 1, False)
            with pe.Fori(1, NSTEP // 2) as i:
                body(i * 2, 0, True)
                body(i * 2 + 1, 1, True)

        @block.scalar
        def _(act):
            for t in range(NT):
                if t >= 2:
                    act.wait_ge(stored[t % 2], 16)
                with act.Fori(0, PER // 2) as i:
                    for b in range(2):
                        act.wait_ge(built, i * 2 + (t * PER + b + 1))
                        nc.scalar.activation(stage[:, t % 2, :, bass.ds(i * (2 * TB) + b * TB, TB)].rearrange("p c t -> p t c"),
                                             ps[:, b].rearrange("p (t c) -> p t c", t=TB), ACT.Copy).then_inc(copied, 1)

        @block.sync
        def _(sp):
            for t in range(NT):
                sp.wait_ge(copied, (t + 1) * PER)
                sp.dma_start(gates.rearrange("c r t -> r c t")[:, :, t * P:(t + 1) * P], stage[:, t % 2]).then_inc(stored[t % 2], 16)
            for k in range(2):
                sp.wait_ge(stored[k], 16 * NT // 2)
    pr.close()
    if io["stop"] == "gates":
        return

    with ExitStack() as st:
        NG = EXP_N // GRP
        uraw = sb(st, "uraw", [P, GRP, KD, P])
        uhi = sb(st, "uhi", [P, 2, KD, P], F32R)
        ulo = sb(st, "ulo", [P, 2, KD, P], F32R)
        vraw = sb(st, "vraw", [P, GRP, D])
        vhi = sb(st, "vhi", [P, GRP, D], F32R)
        vlo = sb(st, "vlo", [P, GRP, D], F32R)
        gj = sb(st, "gj", [P, GRP, T])
        ge = sb(st, "ge", [P, 2, T])
        w_hi = sb(st, "w_hi", [P, 2 * GRP, T], F32R)
        w_lo = sb(st, "w_lo", [P, 2 * GRP, T], F32R)
        names = ("uhi ulo h gelu w0 w whi vhi vlo out added").split()
        S = dict(zip(names, sems(st, " ".join("ex_" + x for x in names))))
        u_loaded = sems(st, " ".join(f"ex_u_loaded{k}" for k in range(GRP)))
        v_loaded = sems(st, " ".join(f"ex_v_loaded{k}" for k in range(GRP)))
        g_loaded = sems(st, " ".join(f"ex_g_loaded{k}" for k in range(GRP)))
        block = st.enter_context(nc.Block())
        OB = 4

        @block.sync
        def _(sp):
            def load(j, k, wait):
                if wait:
                    sp.wait_ge(S["ulo"], j - (GRP - 1))
                sp.dma_start(uraw[:, k], io["u"][bass.ds(j, 1)].rearrange("o p k e -> (o p) k e")).then_inc(u_loaded[k], 16)
                if wait:
                    sp.wait_ge(S["w0"], j - (GRP - 1))
                sp.dma_start(gj[:, k], gates[bass.ds(j, 1)].rearrange("o r t -> (o r) t")).then_inc(g_loaded[k], 16)
                if wait:
                    sp.wait_ge(S["vlo"], j - (GRP - 1))
                sp.dma_start(vraw[:, k], io["v"][bass.ds(j, 1)].rearrange("o p d -> (o p) d")).then_inc(v_loaded[k], 16)
            for k in range(GRP):
                load(k, k, False)
            with sp.Fori(1, EXP_N // GRP) as b:
                for k in range(GRP):
                    load(b * GRP + k, k, True)

        @block.scalar
        def _(act):
            def split_u(j, k, wait):
                act.wait_ge(u_loaded[k % GRP], (j - k % GRP) * 4 + 16)
                if wait:
                    act.wait_ge(S["h"], j - 1)
                    act.wait_ge(S["ulo"], j - 1)
                nc.scalar.activation(uhi[:, k % 2], uraw[:, k % GRP], ACT.Copy).then_inc(S["uhi"], 1)

            def gelu(j, k, wait):
                act.wait_ge(S["h"], j + 1)
                if wait:
                    act.wait_ge(S["w"], j - 1)
                nc.scalar.activation(ge[:, k % 2], ps[:, k % 2], ACT.Gelu).then_inc(S["gelu"], 1)

            def split_v(j, k, n_out, wait):
                act.wait_ge(v_loaded[k % GRP], (j - k % GRP) * 4 + 16)
                if wait and k == 0:
                    act.wait_ge(S["out"], n_out)
                nc.scalar.activation(vhi[:, k], vraw[:, k % GRP], ACT.Copy).then_inc(S["vhi"], 1)

            split_u(0, 0, False)
            split_u(1, 1, False)
            gelu(0, 0, False)

            def group(g, first, last):
                j = g * GRP
                for k in range(GRP):
                    split_v(j + k, k, g * KD, not first)
                    if not (last and k >= 2):
                        split_u(j + (k + 2), k + 2, True)
                    if not (last and k == 3):
                        gelu(j + (k + 1), k + 1, not (first and k == 0))
            group(0, True, False)
            with act.Fori(1, NG - 1) as g:
                group(g, False, False)
            group(NG - 1, False, True)

        @block.gpsimd
        def _(pool):
            def split_v(j, k):
                pool.wait_ge(S["vhi"], j + 1)
                nc.gpsimd.tensor_tensor(vlo[:, k], vraw[:, k % GRP], vhi[:, k].bitcast(F32), ALU.subtract).then_inc(S["vlo"], 1)
            with pool.Fori(0, NG) as g:
                for k in range(GRP):
                    split_v(g * GRP + k, k)

        @block.vector
        def _(v):
            def split_u(j, k):
                v.wait_ge(S["uhi"], j + 1)
                nc.vector.tensor_tensor(ulo[:, k % 2], uraw[:, k % GRP], uhi[:, k % 2].bitcast(F32), ALU.subtract).then_inc(S["ulo"], 1)

            def weigh(j, k, par, n_out, wait):
                slot = par * GRP + k % GRP
                v.wait_ge(S["gelu"], j + 1)
                v.wait_ge(g_loaded[k % GRP], (j - k % GRP) * 4 + 16)
                nc.vector.tensor_tensor(ge[:, k % 2], ge[:, k % 2], gj[:, k % GRP], ALU.mult).then_inc(S["w0"], 1)
                v.wait_ge(S["w0"], j + 1)
                if wait:
                    v.wait_ge(S["out"], n_out)
                nc.vector.tensor_copy(w_hi[:, slot], ge[:, k % 2]).then_inc(S["whi"], 1)
                v.wait_ge(S["whi"], j + 1)
                nc.vector.tensor_tensor(w_lo[:, slot], ge[:, k % 2], w_hi[:, slot].bitcast(F32), ALU.subtract).then_inc(S["w"], 1)

            def add(g, m):
                v.wait_ge(S["out"], g * KD + m + 1)
                nc.vector.tensor_tensor(xT[:, m], ps[:, 2 + m % OB], xT[:, m], ALU.add).then_inc(S["added"], 1)

            split_u(0, 0)
            split_u(1, 1)
            weigh(0, 0, 0, 0, False)

            def group(g, par, first, last, wait):
                j = g * GRP
                for k in range(GRP):
                    if not (last and k >= 2):
                        split_u(j + (k + 2), k + 2)
                    if not (last and k == 3):
                        p2 = par if k < 3 else 1 - par
                        weigh(j + (k + 1), k + 1, p2, (g - 1) * KD if k < 3 else g * KD, wait if k < 3 else not first)
                for m in range(KD):
                    add(g, m)
            group(0, 0, True, False, False)
            group(1, 1, False, False, False)
            with v.Fori(1, NG // 2 - 1) as b:
                group(b * 2, 0, False, False, True)
                group(b * 2 + 1, 1, False, False, True)
            group(NG - 2, 0, False, False, True)
            group(NG - 1, 1, False, True, True)

        @block.tensor
        def _(pe):
            def hidden(j, k, wait):
                pe.wait_ge(S["uhi"], j + 1)
                pe.wait_ge(S["ulo"], j + 1)
                if wait:
                    pe.wait_ge(S["gelu"], j - 1)
                for x, (w, a) in enumerate(((uhi, act_hi), (uhi, act_lo), (ulo, act_hi))):
                    for d in range(KD):
                        mm = nc.tensor.matmul(ps[:, k % 2], w[:, k % 2, d], a[:, d], start=x == 0 and d == 0, stop=x == 2 and d == KD - 1)
                mm.then_inc(S["h"], 1)

            def outputs(g, par, first):
                pe.wait_ge(S["w"], g * GRP + GRP)
                pe.wait_ge(S["vlo"], g * GRP + GRP)
                for m in range(KD):
                    if not first or m >= OB:
                        pe.wait_ge(S["added"], g * KD + (m - OB + 1))
                    cols = slice(m * P, (m + 1) * P)
                    for k in range(GRP):
                        for x, (w, a) in enumerate(((vhi, w_hi), (vhi, w_lo), (vlo, w_hi))):
                            mm = nc.tensor.matmul(ps[:, 2 + m % OB], w[:, k, cols], a[:, par * GRP + k],
                                                  start=k == 0 and x == 0, stop=k == GRP - 1 and x == 2)
                    mm.then_inc(S["out"], 1)

            hidden(0, 0, False)

            def group(g, par, first, last):
                j = g * GRP
                for k in range(GRP):
                    if not (last and k == 3):
                        hidden(j + (k + 1), k + 1, not (first and k == 0))
                outputs(g, par, first)
            group(0, 0, True, False)
            with pe.Fori(0, (NG - 2) // 2) as b:
                group(b * 2 + 1, 1, False, False)
                group(b * 2 + 2, 0, False, False)
            group(NG - 1, 1, False, True)
    recycle()
    if io["stop"] == "peer":
        return

    norm_stage("nf", xT, KD, cst("mean1024"), lambda k: vec("norm_final_g", k), dst=xT)
    b2 = ExitStack()
    norm_stage("n3", xT, KD, cst("mean1024"), lambda k: gain2[:, k:k + 1], shift=lambda k: mod[:, k:k + 1],
               dst_hi=act_hi, dst_lo=act_lo)

    q2 = sb(b2, "q2", [P, 4, T])
    kc2, vc2, ks2, kw2, kr2 = (sb(b2, n, [P, T]) for n in ("kc2", "vc2", "ks2", "kw2", "kr2"))
    vs2, vw2, glt = (sb(b2, n, [P, NT, P]) for n in ("vs2", "vw2", "glt"))
    zz = sb(b2, "zz", [P, KD, T])
    cq = sb(b2, "cq", [P, 2, T])
    ckv = sb(b2, "ckv", [P, 1, T])
    specs = [use("T", "act", a_copy(q2[:, i])) for i in range(4)]
    specs += [use("T", "dve", v_copy(kc2[:])), use("T", "dve", v_copy(vc2[:])), use("T", "dve", v_copy(ks2[:])),
              use("V", "dve", v_copy(merged_tiles(vs2[:]))), use("T", "dve", v_copy(kw2[:])),
              use("V", "dve", v_copy(merged_tiles(vw2[:]))), use("V", "act", a_func(merged_tiles(glt[:]), ACT.Sigmoid)),
              use("T", "dve", v_copy(kr2[:]))]
    specs += [use("T", "act", a_func(zz[:, i], ACT.Silu)) for i in range(4)]
    specs += [use("T", "dve", v_copy(cq[:, i])) for i in range(2)] + [use("T", "dve", v_copy(ckv[:, 0]))]
    specs += [use("T", "act", a_func(zz[:, 4 + i], ACT.Silu)) for i in range(4)]
    panel_stage("in2", PAN["q2"], specs)

    tabs = sb(b2, "tabs", [P, 4, T])
    with ExitStack() as st:
        posi = sb(st, "posi", [P, T], I32)
        posf = sb(st, "posf2", [P, T])
        ang = sb(st, "ang", [P, 4, T])
        turn = sb(st, "turn", [P, 4, T])
        tmp = sb(st, "rope_tmp", [P, 2, T])
        pl, dve, reduced, sn, rt, ap = sems(st, "pos_loaded rp_dve rp_reduced rp_sin rp_rot rp_applied")
        with nc.Block() as block:
            TWO_PI = 2 * np.pi
            C1 = 6.28125
            C2 = float(np.float32(np.round((TWO_PI - C1) * 2.0 ** 21) / 2.0 ** 21))
            C3 = float(np.float32(TWO_PI - C1 - C2))
            MAGIC = 1.5 * 2.0 ** 23
            LIM = 3.1415925

            @block.sync
            def _(sp):
                sp.dma_start(posi[:], io["pos"].partition_broadcast(P)).then_inc(pl, 16)

            @block.vector
            def _(v):
                step = Chain(v, dve)
                v.wait_ge(pl, 16)
                step(nc.vector.tensor_copy(posf[:], posi[:]))
                for k in range(4):
                    ins = nc.vector.tensor_scalar(ang[:, k], posf[:], cst("inv64" if k < 2 else "inv32"), None, ALU.mult)
                step(ins)
                for k in range(4):
                    ins = nc.vector.tensor_scalar(turn[:, k], ang[:, k], 1 / TWO_PI, 0.25 * (k % 2), ALU.mult, ALU.add)
                step(ins)
                step(nc.vector.tensor_scalar(turn[:], turn[:], MAGIC, MAGIC, ALU.add, ALU.subtract))
                for c in (C1, C2, C3):
                    step(nc.vector.scalar_tensor_tensor(out=ang[:], in0=turn[:], scalar=-c, in1=ang[:], op0=ALU.mult, op1=ALU.add))
                for k in (1, 3):
                    ins = nc.vector.tensor_scalar(ang[:, k], ang[:, k], float(np.pi / 2), None, ALU.add)
                step(ins)
                nc.vector.tensor_scalar(ang[:], ang[:], LIM, -LIM, ALU.min, ALU.max).then_inc(reduced, 1)
                tiles = [q2[:, i] for i in range(4)] + [ks2[:], kw2[:]]
                v.wait_ge(sn, 1)
                for i, x in enumerate(tiles):
                    v.wait_ge(rt, i + 1)
                    nc.vector.tensor_tensor(tmp[:, i % 2], ps[:, i], tabs[:, 0], ALU.mult)
                    step(nc.vector.tensor_tensor(x, x, tabs[:, 1], ALU.mult))
                    nc.vector.tensor_tensor(x, x, tmp[:, i % 2], ALU.add).then_inc(ap, 1)
                v.wait_ge(rt, 7)
                r = slice(64, 96)
                nc.vector.tensor_tensor(tmp[r, 0], ps[r, 6], tabs[r, 2], ALU.mult)
                step(nc.vector.tensor_tensor(kr2[r], kr2[r], tabs[r, 3], ALU.mult))
                nc.vector.tensor_tensor(kr2[r], kr2[r], tmp[r, 0], ALU.add).then_inc(ap, 1)

            @block.scalar
            def _(act):
                act.wait_ge(reduced, 1)
                nc.scalar.activation(tabs[:], ang[:], ACT.Sin).then_inc(sn, 1)

            @block.tensor
            def _(pe):
                for i, x in enumerate([q2[:, i] for i in range(4)] + [ks2[:], kw2[:]]):
                    nc.tensor.matmul(ps[:, i], cst("rot64"), x, start=True, stop=True).then_inc(rt, 1)
                nc.tensor.matmul(ps[64:96, 6], cst("rot32")[64:96], kr2[64:96], start=True, stop=True).then_inc(rt, 1)

    kcr = sb(b2, "kcr", [P, 32])
    vcr = sb(b2, "vcr", [P, 2, 64])
    pcT = sb(b2, "pcT", [P, 2, T])
    with ExitStack() as st:
        w1 = sb(st, "w1", [P, 2, 32, P])
        w2 = sb(st, "w2", [P, 2, 64])
        cpos = sb(st, "cpos", [P, 32])
        kb = sb(st, "kb", [P, 2, 32, NCMP])
        hid = sb(st, "hid", [P, 2, 2, 32])
        ktmp = sb(st, "ktmp", [P, 32])
        sc = sb(st, "sc", [P, NT, 8, 32])
        stat = sb(st, "stat", [P, NT, 4, 8])
        ld, dve, ready, hp, hs, kv, kvc, kro, krr, scs, sub, ex, pr_, tr, trc = sems(
            st, "c_ld c_dve c_blocks c_hp c_hs c_kv c_kvc c_kro c_krr c_scs c_sub c_ex c_pr c_tr c_trc")
        with nc.Block() as block:
            @block.sync
            def _(sp):
                sp.dma_start(cpos[:], io["cpos"]).then_inc(ld, 16)
                sp.dma_start(w2[:], io["w2"]).then_inc(ld, 16)
                sp.dma_start(w1[:], io["w1"]).then_inc(ld, 16)

            @block.vector
            def _(v):
                step = Chain(v, dve)
                nc.vector.memset(hid[:], 0.0)
                v.wait_ge(ld, 48)
                for a, src in enumerate((kc2, vc2)):
                    r = src[:].rearrange("p (n s) -> p s n", s=16)
                    for half in range(2):
                        ins = nc.vector.tensor_tensor(kb[:, a, 16 * half:16 * half + 16], r[:, :, half:half + NCMP],
                                                      cpos[:, 16 * half:16 * half + 16].unsqueeze(2).broadcast_to([P, 16, NCMP]), ALU.add)
                ins.then_inc(ready, 1)
                v.wait_ge(kv, 1)
                nc.vector.tensor_copy(kcr[:], ps[:, 2, 0:32])
                nc.vector.tensor_copy(vcr[:].rearrange("p g d -> p (g d)"), ps[:, 3, 0:128]).then_inc(kvc, 1)
                v.wait_ge(kro, 1)
                at_ends = lambda k: tabs[:, k, 31::16]
                nc.vector.tensor_tensor(ktmp[:, 0:NCMP], ps[:, 0, 0:NCMP], at_ends(0), ALU.mult)
                step(nc.vector.tensor_tensor(kcr[:, 0:NCMP], kcr[:, 0:NCMP], at_ends(1), ALU.mult))
                nc.vector.tensor_tensor(kcr[:, 0:NCMP], kcr[:, 0:NCMP], ktmp[:, 0:NCMP], ALU.add).then_inc(krr, 1)
                for q in range(NT):
                    v.wait_ge(scs, q + 1)
                    b0 = 4 + 2 * (q % 2)
                    s4 = ps[:, b0:b0 + 2, 0:128].rearrange("p g (h k) -> p g h k", h=4)
                    top = stat[:, q, 0].rearrange("p (g h) -> p g h", g=2)
                    step(nc.vector.tensor_reduce(top, s4, AX.X, ALU.max))
                    nc.vector.tensor_tensor(sc[:, q].rearrange("p (g h) k -> p g h k", g=2), s4,
                                            top.unsqueeze(3).broadcast_to([P, 2, 4, 32]), ALU.subtract).then_inc(sub, 1)
                for q in range(NT):
                    v.wait_ge(ex, q + 1)
                    step(nc.vector.tensor_reduce(stat[:, q, 1], sc[:, q], AX.X, ALU.add))
                    step(nc.vector.reciprocal(stat[:, q, 2], stat[:, q, 1]))
                    gates_q = glt[:, q, 0:24].rearrange("p (h b) -> p h b", b=3)[:, :, 0]
                    nc.vector.tensor_tensor(stat[:, q, 3], stat[:, q, 2], gates_q, ALU.mult)
                    m0 = CST["cmp_mask"][0] + q * 32
                    step(nc.vector.tensor_tensor(sc[:, q], sc[:, q], cf[:, m0:m0 + 32].unsqueeze(1).broadcast_to([P, 8, 32]), ALU.mult))
                    nc.vector.tensor_tensor(sc[:, q], sc[:, q], stat[:, q, 3].unsqueeze(2).broadcast_to([P, 8, 32]), ALU.mult).then_inc(pr_, 1)

            @block.scalar
            def _(act):
                act.wait_ge(hp, 1)
                act.wait_ge(ready, 1)
                nc.scalar.activation(hid[:, :, :, 0:NCMP], ps[:, 0:2, 0:64].rearrange("p g (a n) -> p a g n", a=2)[:, :, :, 0:NCMP],
                                     ACT.Silu).then_inc(hs, 1)
                for q in range(NT):
                    act.wait_ge(sub, q + 1)
                    nc.scalar.activation(sc[:, q], sc[:, q], ACT.Exp, scale=0.125).then_inc(ex, 1)
                for g in range(2):
                    act.wait_ge(tr, g + 1)
                    nc.scalar.activation(pcT[:, g], ps[:, 1 + g], ACT.Copy).then_inc(trc, 1)

            @block.tensor
            def _(pe):
                pe.wait_ge(ready, 1)
                for a in range(2):
                    for g in range(2):
                        r = slice(64 * g, 64 * g + 64)
                        c = a * 32
                        for l in range(32):
                            mm = nc.tensor.matmul(ps[:, g, c:c + NCMP], w1[r, a, l], kb[r, a, l], start=l == 0, stop=l == 31)
                mm.then_inc(hp, 1)
                pe.wait_ge(hs, 1)
                for g in range(2):
                    nc.tensor.matmul(ps[64 * g:64 * g + 64, 2, 0:32], w2[:, 0], hid[:, 0, g], start=True, stop=True)
                for g in range(2):
                    for r in range(4):
                        mm = nc.tensor.matmul(ps[32 * r:32 * r + 32, 3, 64 * g:64 * g + 64], hid[:, 1, g], w2[:, 1], start=True, stop=True)
                mm.then_inc(kv, 1)
                pe.wait_ge(kvc, 1)
                nc.tensor.matmul(ps[:, 0, 0:32], cst("rot64"), kcr[:], start=True, stop=True).then_inc(kro, 1)
                pe.wait_ge(krr, 1)
                for q in range(NT):
                    if q >= 2:
                        pe.wait_ge(sub, q - 1)
                    c0 = CSB["cmp_bias"][0] + q * 256
                    for g in range(2):
                        bank = ps[:, 4 + 2 * (q % 2) + g, 0:128]
                        r = slice(64 * g, 64 * g + 64)
                        for h in range(4):
                            nc.tensor.matmul(bank[:, h * 32:h * 32 + 32], q2[r, h, q * P:(q + 1) * P], kcr[r],
                                             start=h == 0, stop=False, skip_group_check=True)
                        mm = nc.tensor.matmul(bank, identb, cb[:, c0:c0 + 128], start=False, stop=True, skip_group_check=True)
                    mm.then_inc(scs, 1)
                pe.wait_ge(pr_, NT)
                for g in range(2):
                    for q in range(NT):
                        mm = nc.tensor.transpose(ps[:, 1 + g, q * P:(q + 1) * P],
                                                 sc[:, q, 4 * g:4 * g + 4].rearrange("p h k -> p (h k)"), ident)
                    mm.then_inc(tr, 1)

    recycle()
    if io["stop"] == "cmp":
        return
    norm_stage("nq", cq, 2, cst("mean256"), lambda k: vec("q_norm_g", k), dst=cq)
    norm_stage("nk", ckv, 1, cst("mean128"), lambda k: vec("kv_norm_g"), dst=ckv)
    qm = sb(b2, "qm", [P, HEADS, T])
    km = sb(b2, "km", [P, HEADS, T])
    vm = sb(b2, "vm", [P, NT, 512])
    with ExitStack() as st:
        qup = sb(st, "qup", [P, 2, 768])
        kvup = sb(st, "kvup", [P, 2, 512])
        tmp = sb(st, "mla_tmp", [P, 2, T])
        ld, dve, qp, qe, kp, ke, rt, ap, vp, ve, kc_ = sems(st, "m_ld m_dve m_qp m_qe m_kp m_ke m_rt m_ap m_vp m_ve m_kc")
        with nc.Block() as block:
            @block.sync
            def _(sp):
                sp.dma_start(qup[:], io["qup"]).then_inc(ld, 16)
                sp.dma_start(kvup[:], io["kvup"]).then_inc(ld, 16)

            @block.gpsimd
            def _(pool):
                for h in range(HEADS):
                    nc.gpsimd.tensor_copy(km[64:96, h], kr2[64:96]).then_inc(kc_, 1)

            @block.tensor
            def _(pe):
                pe.wait_ge(ld, 32)

                def rotate(h):
                    pe.wait_ge(qe, h + 1)
                    if h >= 2:
                        pe.wait_ge(ap, h - 1)
                    nc.tensor.matmul(ps[64:96, 6 + h % 2], cst("rot32")[64:96], qm[64:96, h], start=True, stop=True).then_inc(rt, 1)

                for h in range(HEADS):
                    if h >= 2:
                        pe.wait_ge(qe, h - 1)
                    for k in range(2):
                        mm = nc.tensor.matmul(ps[0:96, h % 2], qup[:, k, h * 96:h * 96 + 96], cq[:, k], start=k == 0, stop=k == 1)
                    mm.then_inc(qp, 1)
                    if h >= 2:
                        pe.wait_ge(ke, h - 1)
                    nc.tensor.matmul(ps[0:64, 2 + h % 2], kvup[:, 0, h * 64:h * 64 + 64], ckv[:, 0], start=True, stop=True).then_inc(kp, 1)
                    if h:
                        rotate(h - 1)
                rotate(HEADS - 1)
                for t in range(NT):
                    if t >= 2:
                        pe.wait_ge(ve, t - 1)
                    nc.tensor.matmul(ps[:, 4 + t % 2], ckv[:, 0, t * P:(t + 1) * P], kvup[:, 1], start=True, stop=True).then_inc(vp, 1)

            @block.scalar
            def _(act):
                for h in range(HEADS):
                    act.wait_ge(qp, h + 1)
                    nc.scalar.activation(qm[0:96, h], ps[0:96, h % 2], ACT.Copy).then_inc(qe, 1)
                    act.wait_ge(kp, h + 1)
                    nc.scalar.activation(km[0:64, h], ps[0:64, 2 + h % 2], ACT.Copy).then_inc(ke, 1)
                for t in range(NT):
                    act.wait_ge(vp, t + 1)
                    nc.scalar.activation(vm[:, t], ps[:, 4 + t % 2], ACT.Copy).then_inc(ve, 1)

            @block.vector
            def _(v):
                step = Chain(v, dve)
                r = slice(64, 96)
                for h in range(HEADS):
                    v.wait_ge(rt, h + 1)
                    nc.vector.tensor_tensor(tmp[r, h % 2], ps[r, 6 + h % 2], tabs[r, 2], ALU.mult)
                    step(nc.vector.tensor_tensor(qm[r, h], qm[r, h], tabs[r, 3], ALU.mult))
                    nc.vector.tensor_tensor(qm[r, h], qm[r, h], tmp[r, h % 2], ALU.add).then_inc(ap, 1)

    jobs, units = [], []
    branches = (("slc", ks2, vs2, 1), ("win", kw2, vw2, 2))
    g = 0

    def causal_job(lhs, rhs, q, scale, gate, group):
        nk = (q + 1) * P
        return dict(scores=[(lhs[..., q * P:(q + 1) * P], rhs[..., 0:nk], 0, nk)], n=nk, scale=scale,
                    bias=[(causal, q * P, nk)], gate=gate, sink=None, group=group, query=q, chunk0=0)

    def causal_pv(values, rows, bank, pt, first, last):
        return [(values[:, kt], pt[:, kt, kt * P:T], bank[rows, kt * P:T], first and kt == 0, last and kt == NT - 1)
                for kt in range(NT)]

    def out_tile(u):
        def f(bank, chain):
            chain(nc.vector.tensor_tensor(zz[:, u], bank, zz[:, u], ALU.mult))
            chain(nc.vector.tensor_copy(act_hi[:, u], zz[:, u]))
            return nc.vector.tensor_tensor(act_lo[:, u], zz[:, u], act_hi[:, u].bitcast(F32), ALU.subtract)
        return f

    def nsa_pv(i):
        def f(g, bank, pt):
            half, br = (g % 4) // 2, g % 2
            rows = slice(64 * half, 64 * half + 64)
            vals = branches[br][2]
            out = []
            if br == 0:
                r = slice(32 * i, 32 * i + 32)
                out.append((vcr[r, half], pcT[r, half], bank[rows], True, False))
            return out + causal_pv(vals[:, :, 64 * half:64 * half + 64], rows, bank, pt, False, br == 1)
        return f

    for i in range(4):
        for half in range(2):
            h = i + 4 * half
            rows = slice(64 * half, 64 * half + 64)
            for _, keys2, _, b in branches:
                for q in range(NT):
                    jobs.append(causal_job(q2[rows, i], keys2[rows], q, 0.125, glt[:, q, 3 * h + b:3 * h + b + 1], g))
                g += 1
        units.append(dict(groups=list(range(4 * i, 4 * i + 4)), pv=nsa_pv(i), evac=out_tile(i)))

    def mla_pv(g, bank, pt):
        h = g - 16
        return causal_pv(vm[:, :, 64 * h:64 * h + 64], slice(64 * (h % 2), 64 * (h % 2) + 64), bank, pt, True, True)

    for h in range(HEADS):
        for q in range(NT):
            jobs.append(causal_job(qm[0:96, h], km[0:96, h], q, 96 ** -0.5, None, g))
        g += 1
    for i in range(4):
        units.append(dict(groups=[16 + 2 * i, 17 + 2 * i], pv=mla_pv, evac=out_tile(4 + i)))
    attention_stage("ca", jobs, units)

    panel_stage("o2", PAN["out2"], [
        dict(kind="T", src=act_src, on="dve",
             evac=lambda bank, chain, m=m: nc.vector.scalar_tensor_tensor(
                 out=xT[:, m], in0=bank, scalar=mod[:, 16 + m:17 + m], in1=xT[:, m], op0=ALU.mult, op1=ALU.add))
        for m in range(KD)])
    b2.close()
    norm_stage("n4", xT, KD, cst("mean1024"), lambda k: vec("final_norm_g", k), dst=xT)
    with ExitStack() as st:
        (stored,) = sems(st, "out_stored")
        with nc.Block() as block:
            @block.sync
            def _(sp):
                sp.dma_start(io["out"], xT[:]).then_inc(stored, 16)
                sp.wait_ge(stored, 16)


def host_constants():
    cf = np.zeros((P, NCST), np.float32)
    cbt = np.zeros((P, NCSB), np.float32)

    def put(name, a):
        c, w = CST[name]
        cf[:, c:c + w] = a
    r = np.arange(P)
    put("ident", np.eye(P))
    put("mean1024", 1 / 1024)
    put("mean128", 1 / 128)
    put("mean256", 1 / 256)
    same = r[:, None] // CHUNK == r[None, :] // CHUNK
    put("hgrn_mask", (same & (r[:, None] <= r[None, :])).astype(np.float32))
    rot = np.zeros((P, P), np.float32)
    for m in range(P):
        if m % 64 < 32:
            rot[m + 32, m] = -1
        else:
            rot[m - 32, m] = 1
    put("rot64", rot)
    rot = np.zeros((P, 32), np.float32)
    for m in range(32):
        if m < 16:
            rot[64 + m + 16, m] = -1
        else:
            rot[64 + m - 16, m] = 1
    put("rot32", rot)
    put("inv64", (np.float32(10000.0) ** (-(r % 32).astype(np.float32) / np.float32(32)))[:, None])
    put("inv32", (np.float32(10000.0) ** (-(r % 16).astype(np.float32) / np.float32(16)))[:, None])
    put("eps", 1e-6)
    put("iota", r[None, :])
    put("iota16", np.arange(16)[None, :])
    ends = 16 * np.arange(32) + 31
    mask = np.zeros((P, 4, 32), np.float32)
    for q in range(4):
        mask[:, q, :NCMP] = ends[None, :NCMP] <= (q * P + r)[:, None]
    put("cmp_mask", mask.reshape(P, -1))
    cbt[:, 0:128] = np.eye(P)
    cbt[:, 128:256] = np.where(r[None, :] <= r[:, None], 0, NEG)
    dist = (r[:, None] + P) - np.arange(2 * P)[None, :]
    valid = (dist >= 0) & (dist < P)
    for h in range(HEADS):
        slope = 2.0 ** -(h + 1)
        cbt[:, 256 + h * 256:256 + (h + 1) * 256] = np.where(valid, -slope * dist * 8.0, NEG)
    bias = np.where(mask > 0, 0, NEG)
    c0 = CSB["cmp_bias"][0]
    cbt[:, c0:c0 + 1024] = np.broadcast_to(bias[:, :, None, :], (P, 4, 8, 32)).reshape(P, -1)
    return cf, (cbt.view(np.uint32) >> 16).astype(np.uint16)


def panels_of(w):
    return w.reshape(KD, P, -1, P).transpose(2, 1, 0, 3)


def columns(v):
    return np.asarray(v, np.float32).reshape(-1, P).T


def lay_out(a):
    f = lambda x: np.asarray(x)
    heads = [h for i in range(4) for h in (i, i + 4)]
    perm = np.concatenate([np.arange(64) + 64 * h for h in heads])
    w = f(a["w_in"])[0]
    o = np.cumsum([0, 512, 128, 128, 512, 512, 512, 512, 1024, 1024])
    part = [w[:, o[i]:o[i + 1]] for i in range(9)]
    pan = [panels_of(part[4]), panels_of(part[3]), panels_of(part[0][:, perm])] + [panels_of(part[i]) for i in (1, 2, 5, 6)]
    ga, gh = panels_of(part[7]), panels_of(part[8])
    proj = panels_of(np.concatenate([f(a["w_attn_proj"])[0][perm], f(a["w_hgrn_proj"])[0]], axis=0))
    pan.append(np.stack([ga, gh, proj], axis=1).reshape(24, P, KD, P))
    pan.append(panels_of(f(a["w_out"])[0]))
    pan.append(panels_of(f(a["w_peer_q"])[0]))
    pan.append(panels_of(f(a["ada_w_2"])[0]))
    w = f(a["w_in_2"])[0]
    o = np.cumsum([0, 512, 128, 128, 128, 128, 128, 128, 24, 512, 256, 128, 32, 512])
    part = [w[:, o[i]:o[i + 1]] for i in range(13)]
    gl = np.zeros((D, P), np.float32)
    gl[:, 0:24] = part[7]
    kr = np.zeros((D, P), np.float32)
    kr[:, 64:96] = part[11]
    pan += [panels_of(part[0][:, perm])] + [panels_of(part[i]) for i in range(1, 7)]
    pan += [panels_of(gl), panels_of(kr), panels_of(part[8][:, perm]), panels_of(part[9]), panels_of(part[10]), panels_of(part[12])]
    wo = f(a["w_out_2"])[0]
    pan.append(panels_of(np.concatenate([wo[:512][perm], wo[512:]], axis=0)))
    vecs = np.zeros((P, NVEC), np.float32)
    lb = f(a["hgrn_lb_logits"])
    for name, v in (("norm_mix_g", a["norm_mix_g"]), ("hgrn_norm_g", a["hgrn_norm_g"]), ("norm_ffn_g", a["norm_ffn_g"]),
                    ("norm_final_g", a["norm_final_g"]), ("lb0", lb[0]), ("lb1", lb[1]), ("ada_b", a["ada_b_2"]),
                    ("norm_g_2", a["norm_g_2"]), ("q_norm_g", a["q_norm_g_2"]), ("kv_norm_g", a["kv_norm_g_2"]),
                    ("final_norm_g", a["final_norm_g_2"]), ("c", a["c_2"])):
        c, n = VEC[name]
        vecs[:, c:c + n] = columns(v)
    cf, cbt = host_constants()
    w1 = np.stack([f(a["cmp_k_w1_2"])[0], f(a["cmp_v_w1_2"])[0]])
    w1 = w1.reshape(2, 32, 64, P).transpose(2, 0, 1, 3)
    cpos = f(a["cmp_pos_2"])[0].T
    w2 = np.stack([f(a["cmp_k_w2_2"])[0], f(a["cmp_v_w2_2"])[0]], axis=1)
    kvup = f(a["w_kv_up_2"])[0].reshape(P, 8, 2, 64).transpose(0, 2, 1, 3)
    return {
        "x": f(a["x"])[0].T.reshape(KD, P, T).transpose(1, 0, 2),
        "vecs": vecs, "cf": cf, "cb": cbt,
        "sinks": f(a["attn_sinks"])[0],
        "panels": np.concatenate(pan, axis=0),
        "keys": f(a["peer_keys"])[0].transpose(3, 1, 0, 2).reshape(P, 16, EXP_N),
        "u": f(a["peer_u"])[0].reshape(P, P, KD, P).transpose(1, 3, 2, 0),
        "v": f(a["peer_v"])[0].reshape(P, P, D).transpose(1, 0, 2),
        "pos": f(a["positions_2"])[0],
        "w1": np.concatenate([w1, w1], axis=0), "cpos": np.concatenate([cpos, cpos], axis=0), "w2": w2,
        "qup": f(a["w_q_up_2"])[0].reshape(2, P, 768).transpose(1, 0, 2),
        "kvup": kvup.reshape(P, 2, 512),
    }


def build(nc, shapes, stop=""):
    io = {"stop": stop}
    for name, (shape, dt) in shapes.items():
        io[name] = nc.dram_tensor("in_" + name, shape, dt, kind="ExternalInput").ap()
    io["out"] = nc.dram_tensor("out_0", [P, KD, T], F32, kind="ExternalOutput").ap()
    io["gates"] = nc.dram_tensor("gates", [EXP_N, P, T], F32, kind="Internal").ap()
    program(nc, io)


def kernel(**inputs):
    import concourse.bacc as _bacc
    from concourse.bass_utils import run_bass_kernel_spmd as _run
    nc = _bacc.Bacc("TRN2", target_bir_lowering=False, num_devices=1)
    arrays = {k: np.ascontiguousarray(v) for k, v in lay_out(inputs).items()}
    build(nc, {k: (list(v.shape), mybir.dt.from_np(v.dtype)) for k, v in arrays.items()})
    r = _run(nc, [{"in_" + k: v for k, v in arrays.items()}], core_ids=[0])
    return np.ascontiguousarray(r.results[0]["out_0"].transpose(2, 1, 0)).reshape(1, T, D)
```

```python
from contextlib import ExitStack

import numpy as np
import concourse.bass as bass
from concourse import mybir

F32 = mybir.dt.float32
F32R = mybir.dt.float32r
BF16 = mybir.dt.bfloat16
I32 = mybir.dt.int32
U32 = mybir.dt.uint32
ALU = mybir.AluOpType
ACT = mybir.ActivationFunctionType
AX = mybir.AxisListType

P = 128
T = 512
NT = T // P
D = 1024
KD = D // P
HEADS = 8
NEG = -1e30
HG = 4
CHUNK = 32
EXP_N = 128
TOPK = 16
NCMP = 31
RING = 3
NBANK = 8
GRP = 4

VEC = {}
_at = 0
for _n, _w in (("norm_mix_g", 8), ("hgrn_norm_g", 1), ("norm_ffn_g", 8), ("norm_final_g", 8), ("lb0", 4), ("lb1", 4),
               ("ada_b", 24), ("norm_g_2", 8), ("q_norm_g", 2), ("kv_norm_g", 1), ("final_norm_g", 8), ("c", 8)):
    VEC[_n] = (_at, _w)
    _at += _w
NVEC = _at
CST = {}
_at = 0
for _n, _w in (("ident", 128), ("mean1024", 128), ("mean128", 128), ("mean256", 128), ("hgrn_mask", 128),
               ("rot64", 128), ("exchange", 128), ("rot32", 32), ("inv64", 1), ("inv32", 1), ("eps", 1), ("iota", 128), ("iota16", 16),
               ("cmp_mask", 4 * 32)):
    CST[_n] = (_at, _w)
    _at += _w
NCST = _at
CSB = {"ident": (0, 128), "causal": (128, 128), "alibi": (256, 8 * 256), "cmp_bias": (256 + 2048, 4 * 256)}
NCSB = 256 + 2048 + 1024

PAN = {}
_at = 0
for _n, _w in (("hf", 4), ("hq", 4), ("q", 4), ("k", 1), ("v", 1), ("hi", 4), ("hg", 4),
               ("merge", 24), ("out", 8), ("peerq", 16), ("ada", 24),
               ("kc", 1), ("vc", 1), ("q2", 4), ("ks", 1), ("kw", 1), ("kr", 1), ("gl", 1), ("cq", 2), ("ckv", 1),
               ("vs", 1), ("vw", 1), ("zn", 4), ("zm", 4), ("out2", 8)):
    PAN[_n] = _at
    _at += _w
NPAN = _at


def program(nc, io):
    top = ExitStack()

    def sb(stack, name, shape, dt=F32):
        return stack.enter_context(nc.sbuf_tensor(name, shape, dt))

    used = set()

    def sems(stack, names):
        out = [stack.enter_context(nc.semaphore(n)) for n in names.split()]
        used.update(s.num for s in out)
        return out

    def recycle():
        nums = sorted(used)
        starts = [n for n in nums if n - 1 not in used]
        ends = [n for n in nums if n + 1 not in used]
        with nc.Block() as block:
            @block.sync
            def _(sp):
                for lo, hi in zip(starts, ends):
                    sp.sem_clear(range(lo, hi + 1))
        used.clear()

    ps = top.enter_context(nc.psum_tensor("ps", [P, 8, 512], F32))
    xT = sb(top, "xT", [P, KD, T])
    act_hi = sb(top, "act_hi", [P, KD, T], F32R)
    act_lo = sb(top, "act_lo", [P, KD, T], F32R)
    cf = sb(top, "cf", [P, NCST])
    cb = sb(top, "cb", [P, NCSB], BF16)
    vecs = sb(top, "vecs", [P, NVEC])
    mod = sb(top, "mod", [P, 24])
    gain2 = sb(top, "gain2", [P, KD])

    def cst(name):
        a, w = CST[name]
        return cf[:, a:a + w]

    def vec(name, k=0):
        a = VEC[name][0] + k
        return vecs[:, a:a + 1]

    ident = cst("ident")
    identb = cb[:, 0:128]
    causal = cb[:, 128:256]

    class Chain:

        def __init__(self, eng, sem):
            self.eng, self.sem, self.n = eng, sem, 0

        def __call__(self, ins):
            self.n += 1
            ins.then_inc(self.sem, 1)
            self.eng.wait_ge(self.sem, self.n)

    with ExitStack() as st:
        (loaded,) = sems(st, "const_loaded")
        block = st.enter_context(nc.Block())

        @block.sync
        def _(sp):
            sp.dma_start(xT[:], io["x"]).then_inc(loaded, 16)
            sp.dma_start(vecs[:], io["vecs"]).then_inc(loaded, 16)
            sp.dma_start(cf[:], io["cf"]).then_inc(loaded, 16)
            sp.dma_start(cb[:].bitcast(mybir.dt.uint16), io["cb"]).then_inc(loaded, 16)
            sp.wait_ge(loaded, 64)

    class Weights:

        def __init__(self, st, name, first):
            self.first, self.begun = first, False
            self.raw = sb(st, name + "_raw", [P, RING, KD, P])
            self.hi = sb(st, name + "_whi", [P, 2, KD, P], F32R)
            self.lo = sb(st, name + "_wlo", [P, 2, KD, P], F32R)
            self.hi_ready, self.lo_ready = sems(st, f"{name}_hi_ready {name}_lo_ready")
            self.loaded = sems(st, " ".join(f"{name}_loaded{i}" for i in range(RING)))

        def load(self, sp, i):
            sp.dma_start(self.raw[:, i % RING], io["panels"][self.first + i]).then_inc(self.loaded[i % RING], 16)

        def make_hi(self, act, i):
            act.wait_ge(self.loaded[i % RING], 16 * (i // RING + 1))
            nc.scalar.activation(self.hi[:, i % 2], self.raw[:, i % RING], ACT.Copy).then_inc(self.hi_ready, 1)

        def make_lo(self, pool, i):
            pool.wait_ge(self.hi_ready, i + 1)
            nc.gpsimd.tensor_tensor(self.lo[:, i % 2], self.raw[:, i % RING], self.hi[:, i % 2].bitcast(F32),
                                    ALU.subtract).then_inc(self.lo_ready, 1)

    def norm_stage(name, src, kt, mean, gain, shift=None, dst_hi=None, dst_lo=None, dst=None, ahead=None, store=None):
        with ExitStack() as st:
            sq = sb(st, name + "_sq", [P, 2, T])
            y = sb(st, name + "_y", [P, 2, T])
            rstd = sb(st, name + "_rstd", [P, T])
            sq_ready, sum_step, root_ready, y_ready, hi_ready, lo_pool, lo_dve, dve, stored = sems(
                st, " ".join(name + s for s in ("_sq_ready", "_sum_step", "_root", "_y", "_hi", "_lo_pool", "_lo_dve", "_dve", "_stored")))
            block = st.enter_context(nc.Block())

            if ahead is not None or store is not None:
                @block.sync
                def _(sp):
                    if ahead is not None:
                        ahead.begun = True
                        for i in range(RING):
                            ahead.load(sp, i)
                    if store is not None:
                        for k in range(kt):
                            sp.wait_ge(y_ready, k + 1)
                            sp.dma_start(store[:, k], dst[:, k]).then_inc(stored, 16)
                        sp.wait_ge(stored, 16 * kt)

            @block.scalar
            def _(act):
                for k in range(kt):
                    if k >= 2:
                        act.wait_ge(sum_step, k - 1)
                    nc.scalar.activation(sq[:, k % 2], src[:, k], ACT.Square).then_inc(sq_ready, 1)
                if ahead is not None:
                    for i in range(2):
                        ahead.make_hi(act, i)
                act.wait_ge(sum_step, kt)
                nc.scalar.activation(rstd[:], ps[:, 0], ACT.Sqrt, bias=cst("eps")).then_inc(root_ready, 1)
                if dst is None:
                    for k in range(kt):
                        act.wait_ge(y_ready, k + 1)
                        nc.scalar.activation(dst_hi[:, k], y[:, k % 2], ACT.Copy).then_inc(hi_ready, 1)

            @block.tensor
            def _(pe):
                for k in range(kt):
                    pe.wait_ge(sq_ready, k + 1)
                    nc.tensor.matmul(ps[:, 0], mean, sq[:, k % 2], start=k == 0, stop=k == kt - 1).then_inc(sum_step, 1)

            @block.vector
            def _(v):
                step = Chain(v, dve)

                def make_lo(k):
                    nc.vector.tensor_tensor(dst_lo[:, k], y[:, k % 2], dst_hi[:, k].bitcast(F32), ALU.subtract).then_inc(lo_dve, 1)
                v.wait_ge(root_ready, 1)
                step(nc.vector.reciprocal(rstd[:], rstd[:]))
                for k in range(kt):
                    if dst is None and k >= 2:
                        v.wait_ge(hi_ready, k - 1)
                        if k % 2 == 0:
                            v.wait_ge(lo_pool, k // 2)
                        else:
                            make_lo(k - 2)
                            v.wait_ge(lo_dve, (k - 1) // 2)
                    out = y[:, k % 2] if dst is None else dst[:, k]
                    ins = nc.vector.scalar_tensor_tensor(out=out, in0=src[:, k], scalar=gain(k), in1=rstd[:],
                                                         op0=ALU.mult, op1=ALU.mult)
                    if shift is not None:
                        step(ins)
                        ins = nc.vector.tensor_scalar(out, out, shift(k), None, ALU.add)
                    ins.then_inc(y_ready, 1)
                if dst is None:
                    v.wait_ge(hi_ready, kt)
                    make_lo(kt - 1)

            if dst is None:
                @block.gpsimd
                def _(pool):
                    if ahead is not None:
                        for i in range(2):
                            ahead.make_lo(pool, i)
                    for k in range(0, kt, 2):
                        pool.wait_ge(hi_ready, k + 1)
                        nc.gpsimd.tensor_tensor(dst_lo[:, k], y[:, k % 2], dst_hi[:, k].bitcast(F32),
                                                ALU.subtract).then_inc(lo_pool, 1)

    def panel_stage(name, first, specs, side_load=None, weights=None):
        panel_of, banks, order, n = [], [], {}, 0
        for u, s in enumerate(specs):
            n += s["kind"] == "T" and not s.get("same")
            panel_of.append(n - 1)
            banks.append(sum(x["kind"] != "N" for x in specs[:u]))
            order[s.get("name", u)] = u
        last_use = {p: banks[u] for u, p in enumerate(panel_of) if specs[u]["kind"] == "T"}
        holders = [u for u, s in enumerate(specs) if s["kind"] != "N"]
        with ExitStack() as st:
            weights = weights or Weights(st, name, first)
            whi, wlo, hi_ready, lo_ready = weights.hi, weights.lo, weights.hi_ready, weights.lo_ready
            bank_ready, evac_act, evac_dve, dve, actc = sems(
                st, " ".join(f"{name}_{x}" for x in "bank_ready evac_act evac_dve dve act".split()))
            block = st.enter_context(nc.Block())

            def wait_out(eng, u):
                on = specs[u]["on"]
                eng.wait_ge(evac_act if on == "act" else evac_dve, sum(s["on"] == on for s in specs[:u + 1]))

            def evac(eng, u, chain):
                s = specs[u]
                for w in s.get("pre", ()):
                    wait_out(eng, order[w])
                if s["kind"] != "N":
                    eng.wait_ge(bank_ready, banks[u] + 1)
                s["evac"](ps[:, banks[u] % NBANK], chain).then_inc(evac_act if s["on"] == "act" else evac_dve, 1)

            @block.sync
            def _(sp):
                for i in range(n):
                    if i >= RING:
                        sp.wait_ge(lo_ready, i - RING + 1)
                    if i >= RING or not weights.begun:
                        weights.load(sp, i)
                    if i == RING - 1 and side_load:
                        side_load(sp)

            @block.scalar
            def _(act):
                chain = Chain(act, actc)
                for i in range(n + 2):
                    if i < n:
                        if i >= 2:
                            act.wait_ge(bank_ready, last_use[i - 2] + 1)
                            act.wait_ge(lo_ready, i - 1)
                        if i >= 2 or not weights.begun:
                            weights.make_hi(act, i)
                    for u, p in enumerate(panel_of):
                        if i == (p + 2 if p >= 0 else 0) and specs[u]["on"] == "act":
                            evac(act, u, chain)

            @block.gpsimd
            def _(pool):
                for i in range(2 if weights.begun else 0, n):
                    weights.make_lo(pool, i)

            @block.vector
            def _(v):
                chain = Chain(v, dve)
                for u, s in enumerate(specs):
                    if s["on"] == "dve":
                        evac(v, u, chain)

            @block.tensor
            def _(pe):
                for u, s in enumerate(specs):
                    if s["kind"] == "N":
                        continue
                    for w in s.get("after", ()):
                        wait_out(pe, order[w])
                    if banks[u] >= NBANK:
                        wait_out(pe, holders[banks[u] - NBANK])
                    bank = ps[:, banks[u] % NBANK]
                    if s["kind"] == "X":
                        s["pe"](bank).then_inc(bank_ready, 1)
                        continue
                    i = panel_of[u]
                    pe.wait_ge(hi_ready, i + 1)
                    pe.wait_ge(lo_ready, i + 1)
                    ahi, alo, ks = s["src"]
                    passes = ((whi, ahi), (whi, alo), (wlo, ahi))
                    for x, (w, a) in enumerate(passes):
                        for k in ks:
                            mm = nc.tensor.matmul(bank, w[:, i % 2, k - ks[0] + s.get("w0", 0)], a[:, k],
                                                  start=x == 0 and k == ks[0], stop=x == 2 and k == ks[-1])
                    mm.then_inc(bank_ready, 1)

    ALLK = list(range(KD))
    act_src = (act_hi, act_lo, ALLK)

    def a_copy(dst):
        return lambda bank, chain: nc.scalar.activation(dst, bank, ACT.Copy)

    def a_func(dst, f):
        return lambda bank, chain: nc.scalar.activation(dst, bank, f)

    def v_copy(dst):
        return lambda bank, chain: nc.vector.tensor_copy(dst, bank)

    def attention_stage(name, jobs, units, chunks=NT):
        n = len(jobs)
        NS, NPB, NPT = 4, 4, 2
        score_banks = (0, 1, 2, 7)
        with ExitStack() as st:
            prob = sb(st, name + "_prob", [P, NPB, T])
            ptT = sb(st, name + "_ptT", [P, 2, chunks, T])
            mx = sb(st, name + "_mx", [P, 4, 4])
            rs = sb(st, name + "_rs", [P, 4, 4])
            names = ["scores", "negmax", "expd", "prob", "turned", "copied", "pv", "unit_out", "dve", "sinkexp"]
            scores_ready, negmax_ready, exp_ready, prob_ready, turned, copied, pv_done, unit_out, dve, sinkexp = sems(
                st, " ".join(f"{name}_{x}" for x in names))
            block = st.enter_context(nc.Block())
            groups = sorted({j["group"] for j in jobs})
            last_job = {g: max(i for i, j in enumerate(jobs) if j["group"] == g) for g in groups}
            unit_of = {g: u for u, un in enumerate(units) for g in un["groups"]}

            @block.tensor
            def _(pe):
                def pv(g):
                    u = unit_of[g]
                    un = units[u]
                    if u >= 2 and g == un["groups"][0]:
                        pe.wait_ge(unit_out, u - 1)
                    pe.wait_ge(copied, last_job[g] + 1)
                    bank = ps[:, 5 + u % 2]
                    mms = un["pv"](g, bank, ptT[:, g % 2])
                    for lhsT, rhs, out, start, stop in mms:
                        mm = nc.tensor.matmul(out, lhsT, rhs, start=start, stop=stop)
                    mm.then_inc(pv_done, 1)

                for i in range(n + 4):
                    if i < n:
                        job = jobs[i]
                        if i >= NS:
                            pe.wait_ge(exp_ready, i - NS + 1)
                        bank = ps[:, score_banks[i % NS]]
                        bias = job["bias"]
                        mms = [(l, r, a, b) for l, r, a, b in job["scores"]]
                        mms += [(identb, r, a, b) for r, a, b in bias]
                        for x, (l, r, a, b) in enumerate(mms):
                            mm = nc.tensor.matmul(bank[:, a:b], l, r, start=x == 0, stop=x == len(mms) - 1,
                                                  skip_group_check=True)
                        mm.then_inc(scores_ready, 1)
                    if i >= 3 and i - 3 < n:
                        j = i - 3
                        job = jobs[j]
                        pe.wait_ge(prob_ready, j + 1)
                        if j >= NPT:
                            pe.wait_ge(copied, j - NPT + 1)
                        bank = ps[:, 3 + j % NPT]
                        for c in range(job["n"] // P):
                            mm = nc.tensor.transpose(bank[:, c * P:(c + 1) * P], prob[:, j % NPB, c * P:(c + 1) * P], ident)
                        mm.then_inc(turned, 1)
                    if i >= 4:
                        for g in groups:
                            if last_job[g] == i - 4:
                                pv(g)

            @block.vector
            def _(v):
                chain = Chain(v, dve)

                def finish(j):
                    job = jobs[j]
                    r = rs[:, j % 4]
                    v.wait_ge(exp_ready, j + 1)
                    if job["sink"] is not None:
                        chain(nc.vector.tensor_tensor(r[:, 0:1], r[:, 0:1], r[:, 1:2], ALU.add))
                    chain(nc.vector.reciprocal(r[:, 2:3], r[:, 0:1]))
                    if job["gate"] is not None:
                        chain(nc.vector.tensor_tensor(r[:, 2:3], r[:, 2:3], job["gate"], ALU.mult))
                    pr = prob[:, j % NPB, 0:job["n"]]
                    nc.vector.tensor_scalar(pr, pr, r[:, 2:3], None, ALU.mult).then_inc(prob_ready, 1)

                done = 0
                for j in range(n + 4):
                    if j < n:
                        job = jobs[j]
                        m = mx[:, j % 4]
                        v.wait_ge(scores_ready, j + 1)
                        if j >= 4:
                            v.wait_ge(exp_ready, j - 3)
                        chain(nc.vector.tensor_reduce(m[:, 0:1], ps[:, score_banks[j % NS], 0:job["n"]], AX.X, ALU.max))
                        if job["sink"] is not None:
                            chain(nc.vector.tensor_scalar(m[:, 1:2], m[:, 0:1], job["scale"], job["sink"], ALU.mult, ALU.max))
                            nc.vector.tensor_scalar(m[:, 1:2], m[:, 1:2], -1.0, None, ALU.mult).then_inc(negmax_ready, 1)
                        else:
                            nc.vector.tensor_scalar(m[:, 1:2], m[:, 0:1], -job["scale"], None, ALU.mult).then_inc(negmax_ready, 1)
                    if 1 <= j <= n:
                        finish(j - 1)
                    while done < len(units) and j >= 4 and last_job[units[done]["groups"][-1]] <= j - 4:
                        v.wait_ge(pv_done, 1 + groups.index(units[done]["groups"][-1]))
                        units[done]["evac"](ps[:, 5 + done % 2], chain).then_inc(unit_out, 1)
                        done += 1

            @block.scalar
            def _(act):
                def copy(j):
                    job = jobs[j]
                    g = job["group"]
                    act.wait_ge(turned, j + 1)
                    if g >= 2:
                        act.wait_ge(pv_done, g - 1)
                    q, chunks = job["query"], job["n"] // P
                    c0 = job["chunk0"]
                    nc.scalar.activation(ptT[:, g % 2, c0:c0 + chunks, q * P:(q + 1) * P],
                                         ps[:, 3 + j % NPT, 0:chunks * P].rearrange("p (c q) -> p c q", c=chunks),
                                         ACT.Copy).then_inc(copied, 1)

                for j in range(n + 2):
                    if j < n:
                        job = jobs[j]
                        act.wait_ge(negmax_ready, j + 1)
                        if j >= NPB:
                            act.wait_ge(turned, j - NPB + 1)
                        if j >= 4:
                            act.wait_ge(prob_ready, j - 3)
                        nm, r = mx[:, j % 4, 1:2], rs[:, j % 4]
                        ins = nc.scalar.activation(prob[:, j % NPB, 0:job["n"]], ps[:, score_banks[j % NS], 0:job["n"]], ACT.Exp,
                                                   bias=nm, scale=job["scale"], accum_out=r[:, 0:1])
                        if job["sink"] is not None:
                            ins.then_inc(sinkexp, 1)
                            ins = nc.scalar.activation(r[:, 1:2], job["sink"], ACT.Exp, bias=nm)
                        ins.then_inc(exp_ready, 1)
                    if j >= 2:
                        copy(j - 2)

    norm_stage("n1", xT, KD, cst("mean1024"), lambda k: vec("norm_mix_g", k), dst_hi=act_hi, dst_lo=act_lo)

    if io["stop"] == "n1":
        return
    b1 = ExitStack()
    y_hi = sb(b1, "y_hi", [P, KD, T], F32R)
    y_lo = sb(b1, "y_lo", [P, KD, T], F32R)
    b1h = ExitStack()
    hq = sb(b1h, "hq", [P, HG, T])
    hf = sb(b1h, "hf", [P, HG, T])
    hv = sb(b1h, "hv", [P, HG, NT, P])
    hg = sb(b1h, "hg", [P, HG, T])
    kk = sb(b1h, "kk", [P, HG, T])
    bA = sb(b1h, "bA", [P, HG, T])
    bB = sb(b1h, "bB", [P, HG, T])
    eb = sb(b1h, "eb", [P, HG, T])
    kinv = sb(b1h, "kinv", [P, HG, T])
    lbx = sb(b1h, "lbx", [P, 8, HG])
    b1a = ExitStack()
    qT = sb(b1a, "qT", [P, 4, T])
    kT = sb(b1a, "kT", [P, T])
    vt = sb(b1a, "vt", [P, NT, P])

    def use(kind, on, evac, **more):
        return dict(kind=kind, src=act_src, on=on, evac=evac, **more)

    def emit(name, on, pe, evac, after, *pre):
        return dict(kind="X", name=name, on=on, pe=pe, evac=evac, after=after, pre=pre)

    def with_turns(panels, flip, func=ACT.Copy):
        out, turns = [], []
        for i, (name, dst) in enumerate(panels):
            buf = flip[:, i % 2]
            reuse = (f"turn {panels[i - 2][0]}",) if i >= 2 else ()
            out.append(use("T", "dve", v_copy(buf), name=name, pre=reuse))

            def turn(bank, buf=buf):
                for t in range(NT):
                    mm = nc.tensor.transpose(bank[:, t * P:(t + 1) * P], buf[:, t * P:(t + 1) * P], ident)
                return mm
            turns.append(emit("turn " + name, "act", turn, a_func(merged_tiles(dst), func), [name]))
            if i:
                out.append(turns[i - 1])
        return out, turns[-1]

    def merged_tiles(x):
        return x.rearrange("p t d -> p (t d)")

    flat = lambda x: x[:].rearrange("p h (c s) -> p (h c) s", s=CHUNK)
    lb0, lb1 = (vecs[:, VEC[n][0]:VEC[n][0] + HG] for n in ("lb0", "lb1"))

    def lower_logits(_, chain):
        chain(nc.vector.tensor_tensor(lbx[:, 0], lb0, lb1, ALU.max))
        nc.vector.tensor_tensor(lbx[:, 1], lb0, lbx[:, 0], ALU.subtract)
        return nc.vector.tensor_tensor(lbx[:, 2], lb1, lbx[:, 0], ALU.subtract)

    def lower_bound(_, chain):
        chain(nc.vector.tensor_tensor(lbx[:, 3], lbx[:, 1], lbx[:, 2], ALU.add))
        chain(nc.vector.reciprocal(lbx[:, 4], lbx[:, 3]))
        chain(nc.vector.tensor_tensor(lbx[:, 5], lbx[:, 1], lbx[:, 4], ALU.mult))
        return nc.vector.tensor_scalar(lbx[:, 6], lbx[:, 5], -1.0, 1.0, ALU.mult, ALU.add)

    def forget(_, chain):
        for h in range(HG):
            ins = nc.vector.tensor_scalar(bB[:, h], bA[:, h], lbx[:, 6, h:h + 1], lbx[:, 5, h:h + 1], ALU.mult, ALU.add)
        chain(ins)
        return nc.vector.tensor_scalar(kk[:], bB[:], -1.0, 1.0, ALU.mult, ALU.add)

    def running_sum(_, chain):
        src, dst = bA, bB
        for s in (1, 2, 4, 8, 16):
            nc.vector.tensor_copy(flat(dst)[:, :, 0:s], flat(src)[:, :, 0:s])
            ins = nc.vector.tensor_tensor(flat(dst)[:, :, s:], flat(src)[:, :, s:], flat(src)[:, :, :CHUNK - s], ALU.add)
            if s < 16:
                chain(ins)
            src, dst = dst, src
        return ins

    def to_last(_, chain):
        last = flat(bB)[:, :, CHUNK - 1:CHUNK].broadcast_to([P, HG * T // CHUNK, CHUNK])
        return nc.vector.tensor_tensor(flat(bA), last, flat(bB), ALU.subtract)

    def both_exps(_, chain):
        nc.scalar.activation(eb[:], bB[:], ACT.Exp)
        return nc.scalar.activation(kinv[:], bB[:], ACT.Exp, scale=-1.0)

    def decayed(_, chain):
        nc.vector.tensor_tensor(hq[:], hq[:], eb[:], ALU.mult)
        return nc.vector.tensor_tensor(kinv[:], kinv[:], kk[:], ALU.mult)

    def own(name, on, evac, *pre):
        return dict(kind="N", name=name, on=on, evac=evac, pre=pre)

    specs = [own("lb logits", "dve", lower_logits),
             own("lb exps", "act", lambda _, c: nc.scalar.activation(lbx[:, 1:3], lbx[:, 1:3], ACT.Exp), "lb logits"),
             own("lb", "dve", lower_bound, "lb exps")]
    specs += [use("T", "act", a_func(bA[:, i], ACT.Sigmoid), name=f"sigmoid {i}") for i in range(4)]
    specs += [use("T", "act", a_func(hq[:, i], ACT.Silu), name=f"hq {i}") for i in range(4)]
    specs += [own("f", "dve", forget, "lb", "sigmoid 3")]
    specs += [use("T", "act", a_copy(qT[:, i])) for i in range(2)]
    specs += [own("log f", "act", lambda _, c: nc.scalar.activation(bA[:], bB[:], ACT.Ln), "f")]
    specs += [own("b", "dve", running_sum, "log f")]
    specs += [use("T", "act", a_copy(qT[:, i])) for i in range(2, 4)]
    specs += [use("T", "dve", v_copy(kT[:]))]
    specs += [own("b last - b", "dve", to_last, "b")]
    turned, last_turn = with_turns([("v", vt[:])] + [(f"hv {i}", hv[:, i]) for i in range(4)], hg[:, 2:4])
    specs += turned[:4]
    specs += [own("exps", "act", both_exps, "b"),
              own("exp last", "act", lambda _, c: nc.scalar.activation(bA[:], bA[:], ACT.Exp), "b last - b")]
    specs += turned[4:]
    specs += [own("q and k decayed", "dve", decayed, "exps", "f"),
              own("k to last", "dve", lambda _, c: nc.vector.tensor_tensor(kk[:], kk[:], bA[:], ALU.mult), "exp last", "q and k decayed")]
    specs += [use("T", "act", a_func(hg[:, 0], ACT.Silu)), last_turn]
    specs += [use("T", "act", a_func(hg[:, 1], ACT.Silu))]
    specs += [use("T", "act", a_func(hg[:, i], ACT.Silu), pre=[f"turn hv {i}", "turn hv 3"]) for i in (2, 3)]
    panel_stage("in1", PAN["hf"], specs)
    if io["stop"] == "in1":
        return

    with ExitStack() as st:
        sinks = sb(st, "sinks", [P, HEADS])
        (sk,) = sems(st, "sinks_loaded")
        with nc.Block() as block:
            @block.sync
            def _(sp):
                sp.dma_start(sinks[:], io["sinks"].partition_broadcast(P)).then_inc(sk, 16)
                sp.wait_ge(sk, 16)
        yat = sb(st, "yat", [P, T])
        jobs, units = [], []
        order = [h for i in range(4) for h in (i, i + 4)]
        for g, h in enumerate(order):
            base, i = 64 * (h // 4), h % 4
            for b in range(NT):
                k0 = max(b - 1, 0) * P
                nk = (b + 1) * P - k0
                rows = slice(base, base + 64)
                a0 = CSB["alibi"][0] + h * 256 + (256 - nk)
                jobs.append(dict(scores=[(qT[rows, i, b * P:(b + 1) * P], kT[rows, k0:k0 + nk], 0, nk)], n=nk,
                                 scale=0.125, bias=[(cb[:, a0:a0 + nk], 0, nk)], gate=None, sink=sinks[:, h:h + 1],
                                 group=g, query=b, chunk0=2 - nk // P))

        def window_pv():
            def pv(g, bank, pt):
                half = g % 2
                rows = slice(64 * half, 64 * half + 64)
                out = []
                for b in range(NT):
                    for c in ((1,) if b == 0 else (0, 1)):
                        kt = b - 1 + c
                        out.append((vt[:, kt, 64 * half:64 * half + 64], pt[:, c, b * P:(b + 1) * P],
                                    bank[rows, b * P:(b + 1) * P], c == (1 if b == 0 else 0), c == 1))
                return out
            return pv

        def out_parts(i):
            def f(bank, chain):
                chain(nc.vector.tensor_copy(yat[:], bank))
                chain(nc.vector.tensor_copy(y_hi[:, i], yat[:]))
                return nc.vector.tensor_tensor(y_lo[:, i], yat[:], y_hi[:, i].bitcast(F32), ALU.subtract)
            return f

        for i in range(4):
            units.append(dict(groups=[2 * i, 2 * i + 1], pv=window_pv(), evac=out_parts(i)))
        attention_stage("wa", jobs, units, 2)
    b1a.close()
    if io["stop"] == "wa":
        return

    NC_ = T // CHUNK
    with ExitStack() as st:
        tok = sb(st, "kdec_tok", [P, HG, NT, P])
        NST = 8
        state = sb(st, "state", [P, NST, HG, P])
        at = sb(st, "hgrn_a", [P, 2, HG, P])
        names = ("turned tokc a am ds stt o oe zero").split()
        S = dict(zip(names, sems(st, " ".join("hg_" + x for x in names))))
        block = st.enter_context(nc.Block())

        @block.scalar
        def _(act):
            for t in range(NT):
                act.wait_ge(S["turned"], t + 1)
                nc.scalar.activation(tok[:, :, t], ps[:, t % 2].rearrange("p (h d) -> p h d", h=HG), ACT.Copy).then_inc(S["tokc"], 1)
            for t in range(NT):
                act.wait_ge(S["o"], t + 1)
                nc.scalar.activation(hf[:, :, t * P:(t + 1) * P], ps[:, 6 + t % 2].rearrange("p (h s) -> p h s", h=HG),
                                     ACT.Copy).then_inc(S["oe"], 1)

        @block.vector
        def _(v):
            nc.vector.memset(at[:], 0.0).then_inc(S["zero"], 1)
            v.wait_ge(S["zero"], 1)
            na = 0
            for c in range(NC_):
                if c % 4 == 0:
                    t = c // 4
                    v.wait_ge(S["a"], t + 1)
                    if t >= 2:
                        v.wait_ge(S["o"], t - 1)
                    for h in range(HG):
                        ins = nc.vector.copy_predicated(at[:, t % 2, h], cst("hgrn_mask").bitcast(I32),
                                                        ps[:, 2 + t % 2, h * P:(h + 1) * P])
                    ins.then_inc(S["am"], 1)
                if c < NC_ - 1:
                    v.wait_ge(S["ds"], c + 1)
                    if c >= 1:
                        v.wait_ge(S["stt"], c)
                    if (c + 1) % 4 == 0 and c + 1 >= NST:
                        v.wait_ge(S["o"], (c + 1 - NST) // 4 + 1)
                    for h in range(HG):
                        d = ps[:, 4 + c % 2, h * P:(h + 1) * P]
                        if c == 0:
                            ins = nc.vector.tensor_copy(state[:, 1, h], d)
                        else:
                            ins = nc.vector.scalar_tensor_tensor(
                                out=state[:, (c + 1) % NST, h], in0=state[:, c % NST, h],
                                scalar=eb[:, h, c * CHUNK + CHUNK - 1:(c + 1) * CHUNK], in1=d, op0=ALU.mult, op1=ALU.add)
                    ins.then_inc(S["stt"], 1)

        @block.tensor
        def _(pe):
            for t in range(NT):
                if t >= 2:
                    pe.wait_ge(S["tokc"], t - 1)
                for h in range(HG):
                    mm = nc.tensor.transpose(ps[:, t % 2, h * P:(h + 1) * P], kk[:, h, t * P:(t + 1) * P], ident)
                mm.then_inc(S["turned"], 1)

            def amat(t):
                if t >= 2:
                    pe.wait_ge(S["am"], t - 1)
                for h in range(HG):
                    s = slice(t * P, (t + 1) * P)
                    mm = nc.tensor.matmul(ps[:, 2 + t % 2, h * P:(h + 1) * P], kinv[:, h, s], hq[:, h, s], start=True, stop=True)
                mm.then_inc(S["a"], 1)

            def ds(c):
                t, r = c // 4, slice(CHUNK * (c % 4), CHUNK * (c % 4) + CHUNK)
                pe.wait_ge(S["tokc"], t + 1)
                if c >= 2:
                    pe.wait_ge(S["stt"], c - 1)
                for h in range(HG):
                    mm = nc.tensor.matmul(ps[:, 4 + c % 2, h * P:(h + 1) * P], tok[r, h, t], hv[r, h, t], start=True, stop=True)
                mm.then_inc(S["ds"], 1)

            def out(t):
                pe.wait_ge(S["am"], t + 1)
                if t >= 2:
                    pe.wait_ge(S["oe"], t - 1)
                pe.wait_ge(S["stt"], 4 * t + 3)
                for h in range(HG):
                    bank = ps[:, 6 + t % 2, h * P:(h + 1) * P]
                    nc.tensor.matmul(bank, hv[:, h, t], at[:, t % 2, h], start=True, stop=False, skip_group_check=True)
                    for c in range(4 * t, 4 * t + 4):
                        if c:
                            s = slice(CHUNK * (c % 4), CHUNK * (c % 4) + CHUNK)
                            mm = nc.tensor.matmul(bank[:, s], state[:, c % NST, h], hq[:, h, c * CHUNK:(c + 1) * CHUNK],
                                                  start=False, stop=c % 4 == 3, skip_group_check=True)
                mm.then_inc(S["o"], 1)

            amat(0)
            for c in range(NC_):
                if c < NC_ - 1:
                    ds(c)
                if c % 4 == 1 and c // 4 + 1 < NT:
                    amat(c // 4 + 1)
                if c % 4 == 3:
                    out(c // 4)
    with ExitStack() as st:
        yt = sb(st, "yt", [P, 2, T])
        rt = sb(st, "rt", [P, 2, T])
        sq = sb(st, "sq", [P, HG, T])
        names = ("sq mean root r y hi lo dve").split()
        S = dict(zip(names, sems(st, " ".join("hn_" + x for x in names))))
        block = st.enter_context(nc.Block())

        @block.scalar
        def _(act):
            nc.scalar.activation(sq[:], hf[:], ACT.Square).then_inc(S["sq"], 1)
            for h in range(HG):
                act.wait_ge(S["mean"], h + 1)
                if h >= 2:
                    act.wait_ge(S["y"], h - 1)
                nc.scalar.activation(rt[:, h % 2], ps[:, h], ACT.Sqrt, bias=cst("eps")).then_inc(S["root"], 1)
            for h in range(HG):
                act.wait_ge(S["y"], h + 1)
                nc.scalar.activation(y_hi[:, 4 + h], hg[:, h], ACT.Copy).then_inc(S["hi"], 1)

        @block.tensor
        def _(pe):
            pe.wait_ge(S["sq"], 1)
            for h in range(HG):
                nc.tensor.matmul(ps[:, h], cst("mean128"), sq[:, h], start=True, stop=True).then_inc(S["mean"], 1)

        @block.vector
        def _(v):
            step = Chain(v, S["dve"])
            for h in range(HG):
                v.wait_ge(S["root"], h + 1)
                step(nc.vector.reciprocal(rt[:, h % 2], rt[:, h % 2]))
                step(nc.vector.scalar_tensor_tensor(out=yt[:, h % 2], in0=hf[:, h], scalar=vec("hgrn_norm_g"),
                                                    in1=rt[:, h % 2], op0=ALU.mult, op1=ALU.mult))
                nc.vector.tensor_tensor(hg[:, h], hg[:, h], yt[:, h % 2], ALU.mult).then_inc(S["y"], 1)
            for h in range(HG):
                v.wait_ge(S["hi"], h + 1)
                nc.vector.tensor_tensor(y_lo[:, 4 + h], hg[:, h], y_hi[:, 4 + h].bitcast(F32), ALU.subtract).then_inc(S["lo"], 1)
    b1h.close()
    if io["stop"] == "hgrn":
        return

    with ExitStack() as st:
        ga = sb(st, "ga", [P, 2, T])
        gh = sb(st, "gh", [P, 2, T])
        part = sb(st, "part", [P, 2, T])
        m_hi = sb(st, "m_hi", [P, KD, T], F32R)
        m_lo = sb(st, "m_lo", [P, KD, T], F32R)
        specs = []

        def merge_a(m):
            return lambda bank, chain: nc.vector.tensor_tensor(part[:, m % 2], bank, ga[:, m % 2], ALU.mult)

        def merge_h(m):
            def f(bank, chain):
                chain(nc.vector.tensor_tensor(gh[:, m % 2], bank, gh[:, m % 2], ALU.mult))
                chain(nc.vector.tensor_tensor(part[:, m % 2], part[:, m % 2], gh[:, m % 2], ALU.add))
                chain(nc.vector.tensor_copy(m_hi[:, m], part[:, m % 2]))
                return nc.vector.tensor_tensor(m_lo[:, m], part[:, m % 2], m_hi[:, m].bitcast(F32), ALU.subtract)
            return f

        for m in range(KD):
            u = 4 * m
            free = [u - 5] if m >= 2 else []
            specs.append(use("T", "act", a_func(ga[:, m % 2], ACT.Sigmoid), pre=free))
            specs.append(use("T", "act", a_func(gh[:, m % 2], ACT.Sigmoid), pre=free))
            specs.append(dict(kind="T", src=(y_hi, y_lo, [0, 1, 2, 3]), on="dve", evac=merge_a(m), pre=[u + 1]))
            specs.append(dict(kind="T", src=(y_hi, y_lo, [4, 5, 6, 7]), w0=4, on="dve", evac=merge_h(m), pre=[u + 1], same=True))
        for m in range(KD):
            specs.append(dict(kind="T", src=(m_hi, m_lo, ALLK), on="dve", after=[31],
                              evac=lambda bank, chain, m=m: nc.vector.tensor_tensor(xT[:, m], bank, xT[:, m], ALU.add)))
        panel_stage("mg", PAN["merge"], specs)
    b1.close()
    recycle()
    if io["stop"] == "mix":
        return

    pr = ExitStack()
    i1T = sb(pr, "i1T", [P, T])
    i2T = sb(pr, "i2T", [P, T])
    gT = sb(pr, "gT", [P, T])
    HP = 2 * HEADS
    with ExitStack() as st:
        val = sb(st, "val", [P, NT, HEADS, 2, TOPK])
        idx = sb(st, "idx", [P, NT, HEADS, 2, TOPK], U32)
        rest = sb(st, "rest", [P, HEADS, 256])

        def top16(chain, n, src, values, where):
            width = src(0).shape[-1]
            for half in range(2):
                s = slice(8 * half, 8 * half + 8)
                for r in range(n):
                    ins = nc.vector.max(values(r)[:, s], src(r))
                chain(ins)
                for r in range(n):
                    ins = nc.vector.max_index(where(r)[:, s], values(r)[:, s], src(r))
                if half == 0:
                    for r in range(n):
                        ins = nc.vector.match_replace(rest[:, r, 0:width], values(r)[:, s], src(r), -3.0e38)
                    src = lambda r: rest[:, r, 0:width]
                    chain(ins)
            return ins

        with ExitStack() as stq:
            NQ = 4
            q_ring = sb(stq, "q_ring", [P, NQ, T])
            keys = sb(stq, "keys", [P, HP, EXP_N])
            (keys_loaded,) = sems(stq, "keys_loaded")

            def scores(i):
                def f(bank):
                    if i == 0:
                        nc.tensor.wait_ge(keys_loaded, 16)
                    for t in range(NT):
                        mm = nc.tensor.matmul(bank[:, t * P:(t + 1) * P], q_ring[:, i % NQ, t * P:(t + 1) * P], keys[:, i],
                                              start=True, stop=True)
                    return mm
                return f

            def rank(i):
                return lambda bank, chain: top16(chain, NT, lambda t: bank[:, t * P:(t + 1) * P],
                                                 lambda t: val[:, t, i // 2, i % 2], lambda t: idx[:, t, i // 2, i % 2])

            with nc.Block() as block:
                @block.sync
                def _(sp):
                    sp.dma_start(keys[:], io["keys"]).then_inc(keys_loaded, 16)
            weights = Weights(stq, "pq", PAN["peerq"])
            norm_stage("n2", xT, KD, cst("mean1024"), lambda k: vec("norm_ffn_g", k), dst_hi=act_hi, dst_lo=act_lo, ahead=weights)
            specs = []
            place = {}
            order = [("q", 0)] + [x for i in range(1, HP) for x in (("q", i), ("s", i - 1))] + [("s", HP - 1)]
            for u, x in enumerate(order):
                place[x] = u
            for kind, i in order:
                if kind == "q":
                    pre = [place["s", i - NQ]] if i >= NQ else []
                    specs.append(use("T", "act", a_copy(q_ring[:, i % NQ]), pre=pre))
                else:
                    specs.append(dict(kind="X", pe=scores(i), on="dve", evac=rank(i), after=[place["q", i]]))
            panel_stage("pq", PAN["peerq"], specs, weights=weights)

        with ExitStack() as stq:
            idf = sb(stq, "idf", [P, NT, HEADS, 2, TOPK])
            NCAND = 4 * TOPK + 4 * (TOPK - 4)
            cand = sb(stq, "cand", [P, HEADS, NCAND])
            best = sb(stq, "best", [P, NT, HEADS, TOPK])
            pos = sb(stq, "pos", [P, HEADS, TOPK], U32)
            posh = sb(stq, "posh", [P, 2, HEADS, TOPK], U32)
            posx = sb(stq, "posx", [P, 4, HEADS * TOPK])
            posf = sb(stq, "posf", [P, 2, HEADS * TOPK])
            onehot = sb(stq, "onehot", [P, 2, 2, HEADS, TOPK, TOPK])
            pick = sb(stq, "pick", [P, 2, NT, HEADS * TOPK])
            gate = sb(stq, "gate", [P, NT, HEADS, TOPK])
            gsum = sb(stq, "gsum", [P, NT, HEADS])
            c_act = sb(stq, "c_act", [P, KD])
            ada_w = sb(stq, "ada_w", [P, RING, KD, P])
            c_ready, ada_done, ada_out = sems(stq, "c_ready ada_done ada_out")
            ada_loaded = sems(stq, " ".join(f"ada_loaded{i}" for i in range(RING)))
            names = "dve place eq picked shifted expd gates turned".split()
            S = dict(zip(names, sems(stq, " ".join("tk_" + x for x in names))))
            block = stq.enter_context(nc.Block())

            @block.sync
            def _(sp):
                for i in range(24):
                    if i >= RING:
                        sp.wait_ge(ada_done, i - RING + 1)
                    sp.dma_start(ada_w[:, i % RING], io["panels"][PAN["ada"] + i]).then_inc(ada_loaded[i % RING], 16)

            @block.vector
            def _(v):
                step = Chain(v, S["dve"])

                def pick_sum(t):
                    v.wait_ge(S["eq"], t + 1)
                    for a in range(2):
                        ins = nc.vector.tensor_reduce(pick[:, a, t], onehot[:, t % 2, a].rearrange("p h k j -> p (h k) j"),
                                                      AX.X, ALU.add)
                    ins.then_inc(S["picked"], 1)

                step(nc.vector.tensor_copy(idf[:], idx[:]))
                for t in range(NT):
                    for a0, a1, nb, at in ((0, 4, TOPK, 0), (4, TOPK, 4, 4 * TOPK)):
                        shape = [P, HEADS, a1 - a0, nb]
                        ins = nc.vector.tensor_tensor(cand[:, :, at:at + (a1 - a0) * nb].rearrange("p h (a b) -> p h a b", b=nb),
                                                      val[:, t, :, 0, a0:a1].unsqueeze(3).broadcast_to(shape),
                                                      val[:, t, :, 1, 0:nb].unsqueeze(2).broadcast_to(shape), ALU.add)
                    step(ins)
                    step(top16(step, HEADS, lambda h: cand[:, h], lambda h: best[:, t, h], lambda h: pos[:, h]))
                    nc.vector.tensor_scalar(posh[:, 0], pos[:], 4, None, ALU.logical_shift_right)
                    nc.vector.tensor_copy(posx[:, 2], pos[:].rearrange("p h k -> p (h k)"))
                    step(nc.vector.tensor_scalar(posh[:, 1], pos[:], 2, None, ALU.logical_shift_right))
                    step(nc.vector.tensor_copy(posx[:, 0:2], posh[:].rearrange("p a h k -> p a (h k)")))
                    step(nc.vector.tensor_scalar(posx[:, 1], posx[:, 1], 12.0, None, ALU.subtract))
                    step(nc.vector.tensor_tensor(posf[:, 0], posx[:, 0], posx[:, 1], ALU.max))
                    step(nc.vector.tensor_scalar(posx[:, 3], posf[:, 0], 4.0, 48.0, ALU.mult, ALU.add))
                    step(nc.vector.scalar_tensor_tensor(out=posx[:, 3], in0=posf[:, 0], scalar=16.0, in1=posx[:, 3],
                                                        op0=ALU.mult, op1=ALU.min))
                    step(nc.vector.tensor_tensor(posf[:, 1], posx[:, 2], posx[:, 3], ALU.subtract))
                    for a in range(2):
                        ins = nc.vector.tensor_tensor(onehot[:, t % 2, a].rearrange("p h k j -> p (h k) j"),
                                                      posf[:, a].unsqueeze(2).broadcast_to([P, HEADS * TOPK, TOPK]),
                                                      cst("iota16").unsqueeze(1).broadcast_to([P, HEADS * TOPK, TOPK]), ALU.is_equal)
                    ins.then_inc(S["place"], 1)
                    nc.vector.tensor_tensor(gate[:, t], best[:, t], best[:, t, :, 0:1].broadcast_to([P, HEADS, TOPK]),
                                            ALU.subtract).then_inc(S["shifted"], 1)
                    if t:
                        pick_sum(t - 1)
                v.wait_ge(S["expd"], 1)
                step(nc.vector.tensor_reduce(gsum[:], gate[:], AX.X, ALU.add))
                step(nc.vector.reciprocal(gsum[:], gsum[:]))
                for t in range(NT):
                    ins = nc.vector.tensor_tensor(gate[:, t], gate[:, t], gsum[:, t].unsqueeze(2).broadcast_to([P, HEADS, TOPK]), ALU.mult)
                ins.then_inc(S["gates"], 1)
                pick_sum(NT - 1)
                v.wait_ge(ada_done, 24)
                a, b = VEC["ada_b"][0], VEC["norm_g_2"][0]
                step(nc.vector.tensor_tensor(mod[:], ps[:, 7, 0:24], vecs[:, a:a + 24], ALU.add))
                step(nc.vector.tensor_scalar(gain2[:], mod[:, 8:16], 1.0, None, ALU.add))
                nc.vector.tensor_tensor(gain2[:], gain2[:], vecs[:, b:b + KD], ALU.mult)
                v.wait_ge(S["turned"], 1)
                for a, dst in enumerate((i1T, i2T, gT)):
                    nc.vector.tensor_copy(dst[:], ps[:, 4 + a])

            @block.gpsimd
            def _(pool):
                for t in range(NT):
                    pool.wait_ge(S["place"], t + 1)
                    for a in range(2):
                        ins = nc.gpsimd.tensor_tensor(onehot[:, t % 2, a], onehot[:, t % 2, a],
                                                      idf[:, t, :, a].unsqueeze(2).broadcast_to([P, HEADS, TOPK, TOPK]), ALU.mult)
                    ins.then_inc(S["eq"], 1)

            @block.scalar
            def _(act):
                a = VEC["c"][0]
                nc.scalar.activation(c_act[:], vecs[:, a:a + KD], ACT.Silu).then_inc(c_ready, 1)
                act.wait_ge(S["shifted"], NT)
                nc.scalar.activation(gate[:], gate[:], ACT.Exp).then_inc(S["expd"], 1)

            @block.tensor
            def _(pe):
                def turn(a, src):
                    for t in range(NT):
                        mm = nc.tensor.transpose(ps[:, 4 + a, t * P:(t + 1) * P], src[:, t], ident)
                    return mm
                pe.wait_ge(c_ready, 1)
                for i in range(24):
                    pe.wait_ge(ada_loaded[i % RING], 16 * (i // RING + 1))
                    for k in range(KD):
                        mm = nc.tensor.matmul(ps[:, 7, i:i + 1], ada_w[:, i % RING, k], c_act[:, k:k + 1],
                                              start=k == 0, stop=k == KD - 1)
                    mm.then_inc(ada_done, 1)
                pe.wait_ge(S["gates"], 1)
                turn(2, gate[:].rearrange("p t h k -> p t (h k)"))
                pe.wait_ge(S["picked"], NT)
                turn(0, pick[:, 0])
                turn(1, pick[:, 1]).then_inc(S["turned"], 1)

    if io["stop"] == "topk":
        return
    gates = io["gates"]
    TB = 4
    with ExitStack() as st:
        rows_ = sb(st, "rows_", [P, 2, TB, EXP_N])
        hots_ = sb(st, "hots_", [P, 2, TB, EXP_N])
        cols_ = sb(st, "cols_", [P, 2, TB, EXP_N])
        stage = sb(st, "stage", [P, 2, EXP_N, P])
        row_hot, col_hot, hot, built, copied = sems(st, "g_row_hot g_col_hot g_hot g_built g_copied")
        stored = sems(st, "g_stored0 g_stored1")
        block = st.enter_context(nc.Block())
        NSTEP = T // TB
        PER = P // TB
        shape = [P, TB, EXP_N]
        iota_b = cst("iota").unsqueeze(1).broadcast_to(shape)

        def per_token(x, step):
            return x[:, bass.ds(step * TB, TB)].unsqueeze(2).broadcast_to(shape)

        @block.gpsimd
        def _(pool):
            def body(n, b, wait):
                pool.wait_ge(col_hot, n + 1)
                if wait:
                    pool.wait_ge(built, n - 1)
                nc.gpsimd.tensor_tensor(cols_[:, b], hots_[:, b], per_token(gT, n), ALU.mult).then_inc(hot, 1)
            body(0, 0, False)
            body(1, 1, False)
            with pool.Fori(1, NSTEP // 2) as i:
                body(i * 2, 0, True)
                body(i * 2 + 1, 1, True)

        @block.vector
        def _(v):
            def body(n, b, wait):
                if wait:
                    v.wait_ge(hot, n - 1)
                nc.vector.tensor_tensor(hots_[:, b], iota_b, per_token(i2T, n), ALU.is_equal).then_inc(col_hot, 1)
                if wait:
                    v.wait_ge(built, n - 1)
                nc.vector.tensor_tensor(rows_[:, b], iota_b, per_token(i1T, n), ALU.is_equal).then_inc(row_hot, 1)
            body(0, 0, False)
            body(1, 1, False)
            with v.Fori(1, NSTEP // 2) as i:
                body(i * 2, 0, True)
                body(i * 2 + 1, 1, True)

        @block.tensor
        def _(pe):
            def body(n, b, wait):
                pe.wait_ge(row_hot, n + 1)
                pe.wait_ge(hot, n + 1)
                if wait:
                    pe.wait_ge(copied, n - 1)
                for x in range(TB):
                    mm = nc.tensor.matmul(ps[:, b, x * P:(x + 1) * P], rows_[:, b, x], cols_[:, b, x], start=True, stop=True)
                mm.then_inc(built, 1)
            body(0, 0, False)
            body(1, 1, False)
            with pe.Fori(1, NSTEP // 2) as i:
                body(i * 2, 0, True)
                body(i * 2 + 1, 1, True)

        @block.scalar
        def _(act):
            for t in range(NT):
                if t >= 2:
                    act.wait_ge(stored[t % 2], 16)
                with act.Fori(0, PER // 2) as i:
                    for b in range(2):
                        act.wait_ge(built, i * 2 + (t * PER + b + 1))
                        nc.scalar.activation(stage[:, t % 2, :, bass.ds(i * (2 * TB) + b * TB, TB)].rearrange("p c t -> p t c"),
                                             ps[:, b].rearrange("p (t c) -> p t c", t=TB), ACT.Copy).then_inc(copied, 1)

        @block.sync
        def _(sp):
            for t in range(NT):
                sp.wait_ge(copied, (t + 1) * PER)
                sp.dma_start(gates.rearrange("c r t -> r c t")[:, :, t * P:(t + 1) * P], stage[:, t % 2]).then_inc(stored[t % 2], 16)
            for k in range(2):
                sp.wait_ge(stored[k], 16 * NT // 2)
    pr.close()
    if io["stop"] == "gates":
        return

    with ExitStack() as st:
        NG = EXP_N // GRP
        uraw = sb(st, "uraw", [P, GRP, KD, P])
        uhi = sb(st, "uhi", [P, 2, KD, P], F32R)
        ulo = sb(st, "ulo", [P, 2, KD, P], F32R)
        vraw = sb(st, "vraw", [P, GRP, D])
        vhi = sb(st, "vhi", [P, GRP, D], F32R)
        vlo = sb(st, "vlo", [P, GRP, D], F32R)
        gj = sb(st, "gj", [P, GRP, T])
        ge = sb(st, "ge", [P, 2, T])
        w_hi = sb(st, "w_hi", [P, 2 * GRP, T], F32R)
        w_lo = sb(st, "w_lo", [P, 2 * GRP, T], F32R)
        names = ("uhi ulo h gelu w0 w whi vhi vlo out added").split()
        S = dict(zip(names, sems(st, " ".join("ex_" + x for x in names))))
        u_loaded = sems(st, " ".join(f"ex_u_loaded{k}" for k in range(GRP)))
        v_loaded = sems(st, " ".join(f"ex_v_loaded{k}" for k in range(GRP)))
        g_loaded = sems(st, " ".join(f"ex_g_loaded{k}" for k in range(GRP)))
        block = st.enter_context(nc.Block())
        OB = 4

        @block.sync
        def _(sp):
            def load(j, k, wait):
                if wait:
                    sp.wait_ge(S["ulo"], j - (GRP - 1))
                sp.dma_start(uraw[:, k], io["u"][bass.ds(j, 1)].rearrange("o p k e -> (o p) k e")).then_inc(u_loaded[k], 16)
                if wait:
                    sp.wait_ge(S["w0"], j - (GRP - 1))
                sp.dma_start(gj[:, k], gates[bass.ds(j, 1)].rearrange("o r t -> (o r) t")).then_inc(g_loaded[k], 16)
                if wait:
                    sp.wait_ge(S["vlo"], j - (GRP - 1))
                sp.dma_start(vraw[:, k], io["v"][bass.ds(j, 1)].rearrange("o p d -> (o p) d")).then_inc(v_loaded[k], 16)
            for k in range(GRP):
                load(k, k, False)
            with sp.Fori(1, EXP_N // GRP) as b:
                for k in range(GRP):
                    load(b * GRP + k, k, True)

        @block.scalar
        def _(act):
            def split_u(j, k, wait):
                act.wait_ge(u_loaded[k % GRP], (j - k % GRP) * 4 + 16)
                if wait:
                    act.wait_ge(S["h"], j - 1)
                    act.wait_ge(S["ulo"], j - 1)
                nc.scalar.activation(uhi[:, k % 2], uraw[:, k % GRP], ACT.Copy).then_inc(S["uhi"], 1)

            def gelu(j, k, wait):
                act.wait_ge(S["h"], j + 1)
                if wait:
                    act.wait_ge(S["w"], j - 1)
                nc.scalar.activation(ge[:, k % 2], ps[:, k % 2], ACT.Gelu).then_inc(S["gelu"], 1)

            def split_v(j, k, n_out, wait):
                act.wait_ge(v_loaded[k % GRP], (j - k % GRP) * 4 + 16)
                if wait and k == 0:
                    act.wait_ge(S["out"], n_out)
                nc.scalar.activation(vhi[:, k], vraw[:, k % GRP], ACT.Copy).then_inc(S["vhi"], 1)

            split_u(0, 0, False)
            split_u(1, 1, False)
            gelu(0, 0, False)

            def group(g, first, last):
                j = g * GRP
                for k in range(GRP):
                    split_v(j + k, k, g * KD, not first)
                    if not (last and k >= 2):
                        split_u(j + (k + 2), k + 2, True)
                    if not (last and k == 3):
                        gelu(j + (k + 1), k + 1, not (first and k == 0))
            group(0, True, False)
            with act.Fori(1, NG - 1) as g:
                group(g, False, False)
            group(NG - 1, False, True)

        @block.gpsimd
        def _(pool):
            def split_v(j, k):
                pool.wait_ge(S["vhi"], j + 1)
                nc.gpsimd.tensor_tensor(vlo[:, k], vraw[:, k % GRP], vhi[:, k].bitcast(F32), ALU.subtract).then_inc(S["vlo"], 1)
            with pool.Fori(0, NG) as g:
                for k in range(GRP):
                    split_v(g * GRP + k, k)

        @block.vector
        def _(v):
            def split_u(j, k):
                v.wait_ge(S["uhi"], j + 1)
                nc.vector.tensor_tensor(ulo[:, k % 2], uraw[:, k % GRP], uhi[:, k % 2].bitcast(F32), ALU.subtract).then_inc(S["ulo"], 1)

            def weigh(j, k, par, n_out, wait):
                slot = par * GRP + k % GRP
                v.wait_ge(S["gelu"], j + 1)
                v.wait_ge(g_loaded[k % GRP], (j - k % GRP) * 4 + 16)
                nc.vector.tensor_tensor(ge[:, k % 2], ge[:, k % 2], gj[:, k % GRP], ALU.mult).then_inc(S["w0"], 1)
                v.wait_ge(S["w0"], j + 1)
                if wait:
                    v.wait_ge(S["out"], n_out)
                nc.vector.tensor_copy(w_hi[:, slot], ge[:, k % 2]).then_inc(S["whi"], 1)
                v.wait_ge(S["whi"], j + 1)
                nc.vector.tensor_tensor(w_lo[:, slot], ge[:, k % 2], w_hi[:, slot].bitcast(F32), ALU.subtract).then_inc(S["w"], 1)

            def add(g, m):
                v.wait_ge(S["out"], g * KD + m + 1)
                nc.vector.tensor_tensor(xT[:, m], ps[:, 2 + m % OB], xT[:, m], ALU.add).then_inc(S["added"], 1)

            split_u(0, 0)
            split_u(1, 1)
            weigh(0, 0, 0, 0, False)

            def group(g, par, first, last, wait):
                j = g * GRP
                for k in range(GRP):
                    if not (last and k >= 2):
                        split_u(j + (k + 2), k + 2)
                    if not (last and k == 3):
                        p2 = par if k < 3 else 1 - par
                        weigh(j + (k + 1), k + 1, p2, (g - 1) * KD if k < 3 else g * KD, wait if k < 3 else not first)
                for m in range(KD):
                    add(g, m)
            group(0, 0, True, False, False)
            group(1, 1, False, False, False)
            with v.Fori(1, NG // 2 - 1) as b:
                group(b * 2, 0, False, False, True)
                group(b * 2 + 1, 1, False, False, True)
            group(NG - 2, 0, False, False, True)
            group(NG - 1, 1, False, True, True)

        @block.tensor
        def _(pe):
            def hidden(j, k, wait):
                pe.wait_ge(S["uhi"], j + 1)
                pe.wait_ge(S["ulo"], j + 1)
                if wait:
                    pe.wait_ge(S["gelu"], j - 1)
                for x, (w, a) in enumerate(((uhi, act_hi), (uhi, act_lo), (ulo, act_hi))):
                    for d in range(KD):
                        mm = nc.tensor.matmul(ps[:, k % 2], w[:, k % 2, d], a[:, d], start=x == 0 and d == 0, stop=x == 2 and d == KD - 1)
                mm.then_inc(S["h"], 1)

            def outputs(g, par, first):
                pe.wait_ge(S["w"], g * GRP + GRP)
                pe.wait_ge(S["vlo"], g * GRP + GRP)
                for m in range(KD):
                    if not first or m >= OB:
                        pe.wait_ge(S["added"], g * KD + (m - OB + 1))
                    cols = slice(m * P, (m + 1) * P)
                    for k in range(GRP):
                        for x, (w, a) in enumerate(((vhi, w_hi), (vhi, w_lo), (vlo, w_hi))):
                            mm = nc.tensor.matmul(ps[:, 2 + m % OB], w[:, k, cols], a[:, par * GRP + k],
                                                  start=k == 0 and x == 0, stop=k == GRP - 1 and x == 2)
                    mm.then_inc(S["out"], 1)

            hidden(0, 0, False)

            def group(g, par, first, last):
                j = g * GRP
                for k in range(GRP):
                    if not (last and k == 3):
                        hidden(j + (k + 1), k + 1, not (first and k == 0))
                outputs(g, par, first)
            group(0, 0, True, False)
            with pe.Fori(0, (NG - 2) // 2) as b:
                group(b * 2 + 1, 1, False, False)
                group(b * 2 + 2, 0, False, False)
            group(NG - 1, 1, False, True)
    recycle()
    if io["stop"] == "peer":
        return

    norm_stage("nf", xT, KD, cst("mean1024"), lambda k: vec("norm_final_g", k), dst=xT)
    b2 = ExitStack()
    q2 = sb(b2, "q2", [P, 4, T])
    kc2, vc2, ks2, kw2, kr2 = (sb(b2, n, [P, T]) for n in ("kc2", "vc2", "ks2", "kw2", "kr2"))
    vs2, vw2, glt = (sb(b2, n, [P, NT, P]) for n in ("vs2", "vw2", "glt"))
    zz = sb(b2, "zz", [P, KD, T])
    cq = sb(b2, "cq", [P, 2, T])
    ckv = sb(b2, "ckv", [P, 1, T])
    tabs = sb(b2, "tabs", [P, 4, T])
    kcr = sb(b2, "kcr", [P, 32])
    vcr = sb(b2, "vcr", [P, 2, 64])
    pcT = sb(b2, "pcT", [P, 2, T])
    with ExitStack() as st:
        posi = sb(st, "posi", [P, T], I32)
        ang = sb(st, "ang", [P, 2, T])
        turn = sb(st, "turn", [P, 2, T])
        tmp = sb(st, "rope_tmp", [P, 2, T])
        flip = sb(st, "flip", [P, 3, T])
        w1 = sb(st, "w1", [P, 2, 16, P])
        w2 = sb(st, "w2", [P, 2, 64])
        cpos = sb(st, "cpos", [P, 16])
        kb = sb(st, "kb", [P, 2, 16, 2, NCMP])
        hid = sb(st, "hid", [P, 2, 2, 32])
        ktmp = sb(st, "ktmp", [P, 32])
        sc = sb(st, "sc", [P, NT, 8, 32])
        stat = sb(st, "stat", [P, NT, 4, 8])
        pos_loaded, cmp_loaded = sems(st, "pos_loaded cmp_loaded")

        def side_load(sp):
            sp.dma_start(posi[:], io["pos"].partition_broadcast(P)).then_inc(pos_loaded, 16)
            sp.dma_start(cpos[:], io["cpos"]).then_inc(cmp_loaded, 16)
            sp.dma_start(w2[:], io["w2"]).then_inc(cmp_loaded, 16)
            sp.dma_start(w1[:], io["w1"]).then_inc(cmp_loaded, 16)

        TWO_PI = 2 * np.pi
        C1 = 6.28125
        C2 = float(np.float32(np.round((TWO_PI - C1) * 2.0 ** 21) / 2.0 ** 21))
        C3 = float(np.float32(TWO_PI - C1 - C2))
        MAGIC = 1.5 * 2.0 ** 23
        LIM = 3.1415925

        def angles(inv):
            def f(_, chain):
                chain.eng.wait_ge(pos_loaded, 16)
                chain(nc.vector.tensor_copy(tmp[:, 0], posi[:]))
                for k in range(2):
                    ins = nc.vector.tensor_scalar(ang[:, k], tmp[:, 0], cst(inv), None, ALU.mult)
                chain(ins)
                for k in range(2):
                    ins = nc.vector.tensor_scalar(turn[:, k], ang[:, k], 1 / TWO_PI, 0.25 * k, ALU.mult, ALU.add)
                chain(ins)
                chain(nc.vector.tensor_scalar(turn[:], turn[:], MAGIC, MAGIC, ALU.add, ALU.subtract))
                for c in (C1, C2, C3):
                    chain(nc.vector.scalar_tensor_tensor(out=ang[:], in0=turn[:], scalar=-c, in1=ang[:], op0=ALU.mult, op1=ALU.add))
                chain(nc.vector.tensor_scalar(ang[:, 1], ang[:, 1], float(np.pi / 2), None, ALU.add))
                return nc.vector.tensor_scalar(ang[:], ang[:], LIM, -LIM, ALU.min, ALU.max)
            return f

        def sines(k):
            return lambda _, c: nc.scalar.activation(tabs[:, k:k + 2], ang[:], ACT.Sin)

        def rotated(x, rows=slice(0, P), k=0, slot=0):
            def f(bank, chain):
                nc.vector.tensor_tensor(tmp[rows, slot], bank[rows], tabs[rows, k], ALU.mult)
                chain(nc.vector.tensor_tensor(x, x, tabs[rows, k + 1], ALU.mult))
                return nc.vector.tensor_tensor(x, x, tmp[rows, slot], ALU.add)
            return f

        def rope_use(name, x, of, slot):
            return emit("rope " + name, "dve", lambda bank: nc.tensor.matmul(bank, cst("rot64"), x, start=True, stop=True),
                        rotated(x, slot=slot), [of], "sin64", of)

        def blocks(a, src):
            def f(bank, chain):
                chain.eng.wait_ge(cmp_loaded, 48)
                for parity in range(2):
                    rows = slice(64 * parity, 64 * parity + 64)
                    for g in range(2):
                        of = (src if g == parity else bank)[rows].rearrange("p (n s two) -> p two s n", s=8, two=2)[:, parity]
                        for half in range(2):
                            pairs = slice(8 * half, 8 * half + 8)
                            ins = nc.vector.tensor_tensor(kb[rows, a, pairs, g], of[:, :, half:half + NCMP],
                                                          cpos[rows, pairs].unsqueeze(2).broadcast_to([64, 8, NCMP]), ALU.add)
                return ins
            return f

        def exchanged(src):
            return lambda bank: nc.tensor.matmul(bank, cst("exchange"), src[:], start=True, stop=True)

        def first_layer(bank):
            for a in range(2):
                for l in range(16):
                    mm = nc.tensor.matmul(bank[:, a * 64:a * 64 + 2 * NCMP], w1[:, a, l], kb[:, a, l].rearrange("p g n -> p (g n)"),
                                          start=l == 0, stop=l == 15)
            return mm

        def hidden(bank, chain):
            for a in range(2):
                ins = nc.scalar.activation(hid[:, a, :, 0:NCMP], bank[:, a * 64:a * 64 + 2 * NCMP].rearrange("p (g n) -> p g n", g=2), ACT.Silu)
            return ins

        def cmp_keys(bank):
            for g in range(2):
                mm = nc.tensor.matmul(bank[64 * g:64 * g + 64, 0:32], w2[:, 0], hid[:, 0, g], start=True, stop=True)
            return mm

        def cmp_values(bank):
            for g in range(2):
                for r in range(4):
                    mm = nc.tensor.matmul(bank[32 * r:32 * r + 32, 64 * g:64 * g + 64], hid[:, 1, g], w2[:, 1], start=True, stop=True)
            return mm

        def rope_cmp(bank, chain):
            at_ends = lambda k: tabs[:, k, 31::16]
            nc.vector.tensor_tensor(ktmp[:, 0:NCMP], bank[:, 0:NCMP], at_ends(0), ALU.mult)
            chain(nc.vector.tensor_tensor(kcr[:, 0:NCMP], kcr[:, 0:NCMP], at_ends(1), ALU.mult))
            return nc.vector.tensor_tensor(kcr[:, 0:NCMP], kcr[:, 0:NCMP], ktmp[:, 0:NCMP], ALU.add)

        def cmp_scores(q, g):
            def f(bank):
                c0 = CSB["cmp_bias"][0] + q * 256
                r = slice(64 * g, 64 * g + 64)
                for h in range(4):
                    nc.tensor.matmul(bank[:, h * 32:h * 32 + 32], q2[r, h, q * P:(q + 1) * P], kcr[r],
                                     start=h == 0, stop=False, skip_group_check=True)
                return nc.tensor.matmul(bank[:, 0:128], identb, cb[:, c0:c0 + 128], start=False, stop=True, skip_group_check=True)
            return f

        def cmp_less_max(q, g):
            def f(bank, chain):
                s4 = bank[:, 0:128].rearrange("p (h k) -> p h k", h=4)
                top = stat[:, q, 0, 4 * g:4 * g + 4]
                chain(nc.vector.tensor_reduce(top, s4, AX.X, ALU.max))
                return nc.vector.tensor_tensor(sc[:, q, 4 * g:4 * g + 4], s4, top.unsqueeze(2).broadcast_to([P, 4, 32]), ALU.subtract)
            return f

        def cmp_normed(_, chain):
            flat_stat = lambda i: stat[:, :, i]
            chain(nc.vector.tensor_reduce(flat_stat(1), sc[:], AX.X, ALU.add))
            chain(nc.vector.reciprocal(flat_stat(2), flat_stat(1)))
            gates = glt[:, :, 0:24].rearrange("p q (h b) -> p q h b", b=3)[:, :, :, 0]
            nc.vector.tensor_tensor(flat_stat(3), flat_stat(2), gates, ALU.mult)
            mask = cst("cmp_mask").rearrange("p (q k) -> p q k", q=NT).unsqueeze(2).broadcast_to([P, NT, 8, 32])
            chain(nc.vector.tensor_tensor(sc[:], sc[:], mask, ALU.mult))
            return nc.vector.tensor_tensor(sc[:], sc[:], stat[:, :, 3].unsqueeze(3).broadcast_to([P, NT, 8, 32]), ALU.mult)

        def cmp_turn(g):
            def f(bank):
                for q in range(NT):
                    mm = nc.tensor.transpose(bank[:, q * P:(q + 1) * P], sc[:, q, 4 * g:4 * g + 4].rearrange("p h k -> p (h k)"), ident)
                return mm
            return f

        def latent_mean(sq, mean):
            def f(bank):
                for k, x in enumerate(sq):
                    mm = nc.tensor.matmul(bank, cst(mean), x, start=k == 0, stop=k == len(sq) - 1)
                return mm
            return f

        def latent_out(x, tiles, root, gain):
            def f(_, chain):
                chain(nc.vector.reciprocal(root, root))
                for k in range(tiles):
                    ins = nc.vector.scalar_tensor_tensor(out=x[:, k], in0=x[:, k], scalar=vec(gain, k), in1=root, op0=ALU.mult, op1=ALU.mult)
                return ins
            return f

        def root_of(dst):
            return lambda bank, c: nc.scalar.activation(dst, bank, ACT.Sqrt, bias=cst("eps"))

        rope_kr = slice(64, 96)
        specs = [own("clear", "dve", lambda _, c: nc.vector.memset(hid[:], 0.0)),
                 use("T", "dve", v_copy(kc2[:]), name="kc"), use("T", "dve", v_copy(vc2[:]), name="vc"),
                 own("angles 64", "dve", angles("inv64"))]
        specs += [use("T", "act", a_copy(q2[:, i]), name=f"q {i}") for i in range(2)]
        specs += [own("sin64", "act", sines(0), "angles 64"),
                  emit("kb", "dve", exchanged(kc2), blocks(0, kc2), ["kc"], "kc"), emit("vb", "dve", exchanged(vc2), blocks(1, vc2), ["vc"], "vc"),
                  own("angles 32", "dve", angles("inv32"), "sin64")]
        specs += [use("T", "act", a_copy(q2[:, i]), name=f"q {i}") for i in range(2, 4)]
        specs += [emit("hidden", "act", first_layer, hidden, ["kb", "vb"], "clear")]
        specs += [use("T", "dve", v_copy(ks2[:]), name="ks"), rope_use("q0", q2[:, 0], "q 0", 0), rope_use("q1", q2[:, 1], "q 1", 1)]
        specs += [own("sin32", "act", sines(2), "angles 32")]
        specs += [use("T", "dve", v_copy(kw2[:]), name="kw"), rope_use("q2", q2[:, 2], "q 2", 0), rope_use("q3", q2[:, 3], "q 3", 1)]
        specs += [emit("cmp keys", "dve", cmp_keys, lambda bank, c: nc.vector.tensor_copy(kcr[:], bank[:, 0:32]), ["hidden"]),
                  emit("cmp values", "dve", cmp_values, lambda bank, c: nc.vector.tensor_copy(vcr[:].rearrange("p g d -> p (g d)"), bank[:, 0:128]),
                       ["hidden"])]
        specs += [use("T", "dve", v_copy(kr2[:]), name="kr"), rope_use("ks", ks2[:], "ks", 0),
                  emit("rope cmp", "dve", lambda bank: nc.tensor.matmul(bank[:, 0:32], cst("rot64"), kcr[:], start=True, stop=True),
                       rope_cmp, ["cmp keys"], "cmp keys", "sin64")]
        (gate_logits,), gate_turn = with_turns([("gate logits", glt[:])], flip[:, 2:3], ACT.Sigmoid)
        (turn_vs, turn_vw, ready_vs), ready_vw = with_turns([("vs", vs2[:]), ("vw", vw2[:])], flip)
        specs += [gate_logits, rope_use("kw", kw2[:], "kw", 1)]
        def scores_of(q):
            return [emit(f"cmp scores {q}{g}", "dve", cmp_scores(q, g), cmp_less_max(q, g), ["rope cmp", "rope q3"]) for g in range(2)]
        specs += [use("T", "dve", v_copy(cq[:, 0]), name="cq 0"), gate_turn] + scores_of(0)
        specs += [use("T", "dve", v_copy(cq[:, 1]), name="cq 1")] + scores_of(1)
        specs += [use("T", "dve", v_copy(ckv[:, 0]), name="ckv")] + scores_of(2)
        specs += [emit("rope kr", "dve", lambda bank: nc.tensor.matmul(bank[rope_kr], cst("rot32")[rope_kr], kr2[rope_kr], start=True, stop=True),
                       rotated(kr2[rope_kr], rope_kr, 2, 0), ["kr"], "sin32", "kr")]
        specs += [turn_vs] + scores_of(3)
        specs += [turn_vw, ready_vs,
                  own("cmp exp", "act", lambda _, c: nc.scalar.activation(sc[:], sc[:], ACT.Exp, scale=0.125), "cmp scores 31"),
                  own("cmp normed", "dve", cmp_normed, "cmp exp", "turn gate logits"),
                  own("squares", "act", lambda _, c: nc.scalar.activation(ang[:], cq[:], ACT.Square), "cq 1"),
                  own("square", "act", lambda _, c: nc.scalar.activation(turn[:, 0], ckv[:, 0], ACT.Square), "ckv")]
        specs += [use("T", "act", a_func(zz[:, 0], ACT.Silu)), ready_vw]
        specs += [use("T", "act", a_func(zz[:, 1], ACT.Silu)),
                  emit("cq root", "act", latent_mean([ang[:, 0], ang[:, 1]], "mean256"), root_of(turn[:, 1]), ["squares"]),
                  emit("ckv root", "act", latent_mean([turn[:, 0]], "mean128"), root_of(tmp[:, 1]), ["square"], "rope kw"),
                  own("cq normed", "dve", latent_out(cq, 2, turn[:, 1], "q_norm_g"), "cq root"),
                  own("ckv normed", "dve", latent_out(ckv, 1, tmp[:, 1], "kv_norm_g"), "ckv root")]
        specs += [emit(f"cmp turned {g}", "act", cmp_turn(g), lambda bank, c, g=g: nc.scalar.activation(pcT[:, g], bank, ACT.Copy), ["cmp normed"])
                  for g in range(2)]
        specs += [use("T", "act", a_func(zz[:, i], ACT.Silu)) for i in range(2, 8)]
        weights = Weights(st, "in2", PAN["kc"])
        norm_stage("n3", xT, KD, cst("mean1024"), lambda k: gain2[:, k:k + 1], shift=lambda k: mod[:, k:k + 1],
                   dst_hi=act_hi, dst_lo=act_lo, ahead=weights)
        panel_stage("in2", PAN["kc"], specs, side_load=side_load, weights=weights)

    recycle()
    if io["stop"] == "cmp":
        return
    qm = sb(b2, "qm", [P, HEADS, T])
    km = sb(b2, "km", [P, HEADS, T])
    vm = sb(b2, "vm", [P, NT, 512])
    with ExitStack() as st:
        qup = sb(st, "qup", [P, 2, 768])
        kvup = sb(st, "kvup", [P, 2, 512])
        tmp = sb(st, "mla_tmp", [P, 2, T])
        ld, dve, qp, qe, kp, ke, rt, ap, vp, ve, kc_ = sems(st, "m_ld m_dve m_qp m_qe m_kp m_ke m_rt m_ap m_vp m_ve m_kc")
        with nc.Block() as block:
            @block.sync
            def _(sp):
                sp.dma_start(qup[:], io["qup"]).then_inc(ld, 16)
                sp.dma_start(kvup[:], io["kvup"]).then_inc(ld, 16)

            @block.gpsimd
            def _(pool):
                for h in range(HEADS):
                    nc.gpsimd.tensor_copy(km[64:96, h], kr2[64:96]).then_inc(kc_, 1)

            @block.tensor
            def _(pe):
                pe.wait_ge(ld, 32)

                def rotate(h):
                    pe.wait_ge(qe, h + 1)
                    if h >= 2:
                        pe.wait_ge(ap, h - 1)
                    nc.tensor.matmul(ps[64:96, 6 + h % 2], cst("rot32")[64:96], qm[64:96, h], start=True, stop=True).then_inc(rt, 1)

                for h in range(HEADS):
                    if h >= 2:
                        pe.wait_ge(qe, h - 1)
                    for k in range(2):
                        mm = nc.tensor.matmul(ps[0:96, h % 2], qup[:, k, h * 96:h * 96 + 96], cq[:, k], start=k == 0, stop=k == 1)
                    mm.then_inc(qp, 1)
                    if h >= 2:
                        pe.wait_ge(ke, h - 1)
                    nc.tensor.matmul(ps[0:64, 2 + h % 2], kvup[:, 0, h * 64:h * 64 + 64], ckv[:, 0], start=True, stop=True).then_inc(kp, 1)
                    if h:
                        rotate(h - 1)
                rotate(HEADS - 1)
                for t in range(NT):
                    if t >= 2:
                        pe.wait_ge(ve, t - 1)
                    nc.tensor.matmul(ps[:, 4 + t % 2], ckv[:, 0, t * P:(t + 1) * P], kvup[:, 1], start=True, stop=True).then_inc(vp, 1)

            @block.scalar
            def _(act):
                for h in range(HEADS):
                    act.wait_ge(qp, h + 1)
                    nc.scalar.activation(qm[0:96, h], ps[0:96, h % 2], ACT.Copy).then_inc(qe, 1)
                    act.wait_ge(kp, h + 1)
                    nc.scalar.activation(km[0:64, h], ps[0:64, 2 + h % 2], ACT.Copy).then_inc(ke, 1)
                for t in range(NT):
                    act.wait_ge(vp, t + 1)
                    nc.scalar.activation(vm[:, t], ps[:, 4 + t % 2], ACT.Copy).then_inc(ve, 1)

            @block.vector
            def _(v):
                step = Chain(v, dve)
                r = slice(64, 96)
                for h in range(HEADS):
                    v.wait_ge(rt, h + 1)
                    nc.vector.tensor_tensor(tmp[r, h % 2], ps[r, 6 + h % 2], tabs[r, 2], ALU.mult)
                    step(nc.vector.tensor_tensor(qm[r, h], qm[r, h], tabs[r, 3], ALU.mult))
                    nc.vector.tensor_tensor(qm[r, h], qm[r, h], tmp[r, h % 2], ALU.add).then_inc(ap, 1)

    jobs, units = [], []
    branches = (("slc", ks2, vs2, 1), ("win", kw2, vw2, 2))
    g = 0

    def causal_job(lhs, rhs, q, scale, gate, group):
        nk = (q + 1) * P
        return dict(scores=[(lhs[..., q * P:(q + 1) * P], rhs[..., 0:nk], 0, nk)], n=nk, scale=scale,
                    bias=[(causal, q * P, nk)], gate=gate, sink=None, group=group, query=q, chunk0=0)

    def causal_pv(values, rows, bank, pt, first, last):
        return [(values[:, kt], pt[:, kt, kt * P:T], bank[rows, kt * P:T], first and kt == 0, last and kt == NT - 1)
                for kt in range(NT)]

    def out_tile(u):
        def f(bank, chain):
            chain(nc.vector.tensor_tensor(zz[:, u], bank, zz[:, u], ALU.mult))
            chain(nc.vector.tensor_copy(act_hi[:, u], zz[:, u]))
            return nc.vector.tensor_tensor(act_lo[:, u], zz[:, u], act_hi[:, u].bitcast(F32), ALU.subtract)
        return f

    def nsa_pv(i):
        def f(g, bank, pt):
            half, br = (g % 4) // 2, g % 2
            rows = slice(64 * half, 64 * half + 64)
            vals = branches[br][2]
            out = []
            if br == 0:
                r = slice(32 * i, 32 * i + 32)
                out.append((vcr[r, half], pcT[r, half], bank[rows], True, False))
            return out + causal_pv(vals[:, :, 64 * half:64 * half + 64], rows, bank, pt, False, br == 1)
        return f

    for i in range(4):
        for half in range(2):
            h = i + 4 * half
            rows = slice(64 * half, 64 * half + 64)
            for _, keys2, _, b in branches:
                for q in range(NT):
                    jobs.append(causal_job(q2[rows, i], keys2[rows], q, 0.125, glt[:, q, 3 * h + b:3 * h + b + 1], g))
                g += 1
        units.append(dict(groups=list(range(4 * i, 4 * i + 4)), pv=nsa_pv(i), evac=out_tile(i)))

    def mla_pv(g, bank, pt):
        h = g - 16
        return causal_pv(vm[:, :, 64 * h:64 * h + 64], slice(64 * (h % 2), 64 * (h % 2) + 64), bank, pt, True, True)

    for h in range(HEADS):
        for q in range(NT):
            jobs.append(causal_job(qm[0:96, h], km[0:96, h], q, 96 ** -0.5, None, g))
        g += 1
    for i in range(4):
        units.append(dict(groups=[16 + 2 * i, 17 + 2 * i], pv=mla_pv, evac=out_tile(4 + i)))
    attention_stage("ca", jobs, units)

    panel_stage("o2", PAN["out2"], [
        dict(kind="T", src=act_src, on="dve",
             evac=lambda bank, chain, m=m: nc.vector.scalar_tensor_tensor(
                 out=xT[:, m], in0=bank, scalar=mod[:, 16 + m:17 + m], in1=xT[:, m], op0=ALU.mult, op1=ALU.add))
        for m in range(KD)])
    b2.close()
    norm_stage("n4", xT, KD, cst("mean1024"), lambda k: vec("final_norm_g", k), dst=xT, store=io["out"])


def host_constants():
    cf = np.zeros((P, NCST), np.float32)
    cbt = np.zeros((P, NCSB), np.float32)

    def put(name, a):
        c, w = CST[name]
        cf[:, c:c + w] = a
    r = np.arange(P)
    put("ident", np.eye(P))
    put("mean1024", 1 / 1024)
    put("mean128", 1 / 128)
    put("mean256", 1 / 256)
    same = r[:, None] // CHUNK == r[None, :] // CHUNK
    put("hgrn_mask", (same & (r[:, None] <= r[None, :])).astype(np.float32))
    rot = np.zeros((P, P), np.float32)
    for m in range(P):
        if m % 64 < 32:
            rot[m + 32, m] = -1
        else:
            rot[m - 32, m] = 1
    put("rot64", rot)
    put("exchange", np.roll(np.eye(P), 64, axis=0))
    rot = np.zeros((P, 32), np.float32)
    for m in range(32):
        if m < 16:
            rot[64 + m + 16, m] = -1
        else:
            rot[64 + m - 16, m] = 1
    put("rot32", rot)
    put("inv64", (np.float32(10000.0) ** (-(r % 32).astype(np.float32) / np.float32(32)))[:, None])
    put("inv32", (np.float32(10000.0) ** (-(r % 16).astype(np.float32) / np.float32(16)))[:, None])
    put("eps", 1e-6)
    put("iota", r[None, :])
    put("iota16", np.arange(16)[None, :])
    ends = 16 * np.arange(32) + 31
    mask = np.zeros((P, 4, 32), np.float32)
    for q in range(4):
        mask[:, q, :NCMP] = ends[None, :NCMP] <= (q * P + r)[:, None]
    put("cmp_mask", mask.reshape(P, -1))
    cbt[:, 0:128] = np.eye(P)
    cbt[:, 128:256] = np.where(r[None, :] <= r[:, None], 0, NEG)
    dist = (r[:, None] + P) - np.arange(2 * P)[None, :]
    valid = (dist >= 0) & (dist < P)
    for h in range(HEADS):
        slope = 2.0 ** -(h + 1)
        cbt[:, 256 + h * 256:256 + (h + 1) * 256] = np.where(valid, -slope * dist * 8.0, NEG)
    bias = np.where(mask > 0, 0, NEG)
    c0 = CSB["cmp_bias"][0]
    cbt[:, c0:c0 + 1024] = np.broadcast_to(bias[:, :, None, :], (P, 4, 8, 32)).reshape(P, -1)
    return cf, (cbt.view(np.uint32) >> 16).astype(np.uint16)


def panels_of(w):
    return w.reshape(KD, P, -1, P).transpose(2, 1, 0, 3)


def columns(v):
    return np.asarray(v, np.float32).reshape(-1, P).T


def lay_out(a):
    f = lambda x: np.asarray(x)
    heads = [h for i in range(4) for h in (i, i + 4)]
    perm = np.concatenate([np.arange(64) + 64 * h for h in heads])
    w = f(a["w_in"])[0]
    o = np.cumsum([0, 512, 128, 128, 512, 512, 512, 512, 1024, 1024])
    part = [w[:, o[i]:o[i + 1]] for i in range(9)]
    pan = [panels_of(part[4]), panels_of(part[3]), panels_of(part[0][:, perm])] + [panels_of(part[i]) for i in (1, 2, 5, 6)]
    ga, gh = panels_of(part[7]), panels_of(part[8])
    proj = panels_of(np.concatenate([f(a["w_attn_proj"])[0][perm], f(a["w_hgrn_proj"])[0]], axis=0))
    pan.append(np.stack([ga, gh, proj], axis=1).reshape(24, P, KD, P))
    pan.append(panels_of(f(a["w_out"])[0]))
    pan.append(panels_of(f(a["w_peer_q"])[0]))
    pan.append(panels_of(f(a["ada_w_2"])[0]))
    w = f(a["w_in_2"])[0]
    o = np.cumsum([0, 512, 128, 128, 128, 128, 128, 128, 24, 512, 256, 128, 32, 512])
    part = [w[:, o[i]:o[i + 1]] for i in range(13)]
    gl = np.zeros((D, P), np.float32)
    gl[:, 0:24] = part[7]
    kr = np.zeros((D, P), np.float32)
    kr[:, 64:96] = part[11]
    pan += [panels_of(x) for x in (part[1], part[2], part[0][:, perm], part[3], part[5], kr, gl, part[9], part[10],
                                   part[4], part[6], part[8][:, perm], part[12])]
    wo = f(a["w_out_2"])[0]
    pan.append(panels_of(np.concatenate([wo[:512][perm], wo[512:]], axis=0)))
    vecs = np.zeros((P, NVEC), np.float32)
    lb = f(a["hgrn_lb_logits"])
    for name, v in (("norm_mix_g", a["norm_mix_g"]), ("hgrn_norm_g", a["hgrn_norm_g"]), ("norm_ffn_g", a["norm_ffn_g"]),
                    ("norm_final_g", a["norm_final_g"]), ("lb0", lb[0]), ("lb1", lb[1]), ("ada_b", a["ada_b_2"]),
                    ("norm_g_2", a["norm_g_2"]), ("q_norm_g", a["q_norm_g_2"]), ("kv_norm_g", a["kv_norm_g_2"]),
                    ("final_norm_g", a["final_norm_g_2"]), ("c", a["c_2"])):
        c, n = VEC[name]
        vecs[:, c:c + n] = columns(v)
    cf, cbt = host_constants()
    w1 = np.stack([f(a["cmp_k_w1_2"])[0], f(a["cmp_v_w1_2"])[0]])
    w1 = w1.reshape(2, 16, P, P).transpose(2, 0, 1, 3)
    cpos = f(a["cmp_pos_2"])[0].reshape(16, P).T
    w2 = np.stack([f(a["cmp_k_w2_2"])[0], f(a["cmp_v_w2_2"])[0]], axis=1)
    kvup = f(a["w_kv_up_2"])[0].reshape(P, 8, 2, 64).transpose(0, 2, 1, 3)
    return {
        "x": f(a["x"])[0].T.reshape(KD, P, T).transpose(1, 0, 2),
        "vecs": vecs, "cf": cf, "cb": cbt,
        "sinks": f(a["attn_sinks"])[0],
        "panels": np.concatenate(pan, axis=0),
        "keys": f(a["peer_keys"])[0].transpose(3, 1, 0, 2).reshape(P, 16, EXP_N),
        "u": f(a["peer_u"])[0].reshape(P, P, KD, P).transpose(1, 3, 2, 0),
        "v": f(a["peer_v"])[0].reshape(P, P, D).transpose(1, 0, 2),
        "pos": f(a["positions_2"])[0],
        "w1": w1, "cpos": cpos, "w2": w2,
        "qup": f(a["w_q_up_2"])[0].reshape(2, P, 768).transpose(1, 0, 2),
        "kvup": kvup.reshape(P, 2, 512),
    }


def build(nc, shapes, stop=""):
    io = {"stop": stop}
    for name, (shape, dt) in shapes.items():
        io[name] = nc.dram_tensor("in_" + name, shape, dt, kind="ExternalInput").ap()
    io["out"] = nc.dram_tensor("out_0", [P, KD, T], F32, kind="ExternalOutput").ap()
    io["gates"] = nc.dram_tensor("gates", [EXP_N, P, T], F32, kind="Internal").ap()
    program(nc, io)


def kernel(**inputs):
    import concourse.bacc as _bacc
    from concourse.bass_utils import run_bass_kernel_spmd as _run
    nc = _bacc.Bacc("TRN2", target_bir_lowering=False, num_devices=1)
    arrays = {k: np.ascontiguousarray(v) for k, v in lay_out(inputs).items()}
    build(nc, {k: (list(v.shape), mybir.dt.from_np(v.dtype)) for k, v in arrays.items()})
    r = _run(nc, [{"in_" + k: v for k, v in arrays.items()}], core_ids=[0])
    return np.ascontiguousarray(r.results[0]["out_0"].transpose(2, 1, 0)).reshape(1, T, D)
```
